# Optimizing a Trainium2 kernel written in Bass

```python
import jax, jax.numpy as jnp
from jax import lax
import numpy as np

D_MODEL = 1024
BATCH = 1
SEQ = 512
DEPTH = 2

GRID_W = 64
CTX_LEN = 256
HEAD_DIM = 64
NA_HEADS = 4
NA_WIN_R = 8
NA_WIN_C = 16
NA_QCB = 16
NA_BAND = 32
FNET_GROUPS = 4
FNET_GROUP_DIM = 64
SWA_HEADS = 4
SWA_KV_HEADS = 2
SWA_WINDOW = 128
SWA_BLOCK = 128
HGRN_HEADS = 4
HGRN_DK = 64
HGRN_DV = 64
HGRN_CHUNK = 64
ROPE_THETA = 10000.0
EPS = 1e-6
W_A = NA_HEADS * HEAD_DIM
W_B = FNET_GROUPS * FNET_GROUP_DIM
W_C = SWA_HEADS * HEAD_DIM
W_C_KV = SWA_KV_HEADS * HEAD_DIM
W_DK = HGRN_HEADS * HGRN_DK
W_DV = HGRN_HEADS * HGRN_DV
D_MIX = W_A + W_B + W_C + W_DV
IN_SPLITS = (W_A, W_A, W_A, W_B, W_C, W_C_KV, W_C_KV, W_DK, W_DK, W_DK, W_DV, W_DV)
D_IN = sum(IN_SPLITS)
D_FF = -(-8 * D_MODEL // (3 * 256)) * 256

kernel_name = "hybrid_natten_fnet_swa_hgrn2_dit"

F32 = jnp.float32

def rms_norm(x, g):
    xf = x.astype(F32)
    y = xf * lax.rsqrt(jnp.mean(xf * xf, axis=-1, keepdims=True) + EPS)
    return (y * g.astype(F32)).astype(x.dtype)

def modulate(h, shift, scale):
    return h * (1 + scale) + shift

def split_in(y):
    out, start = [], 0
    for w in IN_SPLITS:
        out.append(y[..., start:start + w])
        start += w
    return out

def heads(t, n):
    b, l, _ = t.shape
    return t.reshape(b, l, n, -1).transpose(0, 2, 1, 3)

def merge(t):
    b, h, l, d = t.shape
    return t.transpose(0, 2, 1, 3).reshape(b, l, h * d)

def rope_1d(x, pos):
    half = x.shape[-1] // 2
    freqs = ROPE_THETA ** (-jnp.arange(half, dtype=F32) / half)
    ang = jnp.asarray(pos, F32)[:, None] * freqs
    cos, sin = jnp.cos(ang).astype(x.dtype), jnp.sin(ang).astype(x.dtype)
    x1, x2 = x[..., :half], x[..., half:]
    return jnp.concatenate([x1 * cos - x2 * sin, x1 * sin + x2 * cos], axis=-1)

def axial_rope(x, rows, cols):
    half = x.shape[-1] // 2
    return jnp.concatenate([rope_1d(x[..., :half], rows), rope_1d(x[..., half:], cols)], axis=-1)

def dense_attention(q, k, v, sink=None):
    b, hq, l, d = q.shape
    g = k.shape[1]
    qg = q.reshape(b, g, hq // g, l, d)
    s = jnp.einsum('bgrqd,bgkd->bgrqk', qg, k).astype(F32) * HEAD_DIM ** -0.5
    if sink is not None:
        s_sink = jnp.broadcast_to(sink.astype(F32).reshape(1, g, hq // g, 1, 1), s.shape[:-1] + (1,))
        s = jnp.concatenate([s, s_sink], axis=-1)
    p = jax.nn.softmax(s, axis=-1)[..., :l].astype(v.dtype)
    return jnp.einsum('bgrqk,bgkd->bgrqd', p, v).reshape(b, hq, l, d)

def neighbourhood_attention(q, k, v, kc, vc, rpb):
    b, h, n, d = q.shape
    rows = n // GRID_W
    kr = min(NA_WIN_R, rows)
    ncb = GRID_W // NA_QCB
    r = np.arange(rows)
    row_idx = np.clip(r - kr // 2, 0, rows - kr)[:, None] + np.arange(kr)
    qcol = np.arange(GRID_W).reshape(ncb, NA_QCB)
    cs = np.clip(qcol - NA_WIN_C // 2, 0, GRID_W - NA_WIN_C)
    band = np.clip(np.arange(ncb) * NA_QCB - NA_WIN_C // 2, 0, GRID_W - NA_BAND)[:, None] + np.arange(NA_BAND)
    col_ok = (band[:, None, :] >= cs[:, :, None]) & (band[:, None, :] < cs[:, :, None] + NA_WIN_C)
    dr = row_idx - r[:, None] + NA_WIN_R - 1
    dc = np.clip(band[:, None, :] - qcol[:, :, None], -(NA_WIN_C - 1), NA_WIN_C - 1) + NA_WIN_C - 1
    bias = rpb[:, dr[:, None, None, :, None], dc[None, :, :, None, :]].astype(F32)
    bias = jnp.where(col_ok[None, None, :, :, None, :], bias, -jnp.inf)
    qg = q.reshape(b, h, rows, ncb, NA_QCB, d)
    gi_r, gi_c = row_idx[:, :, None, None], band[None, None, :, :]
    kg = k.reshape(b, h, rows, GRID_W, d)[:, :, gi_r, gi_c]
    vg = v.reshape(b, h, rows, GRID_W, d)[:, :, gi_r, gi_c]
    scale = HEAD_DIM ** -0.5
    s_nb = jnp.einsum('bhrcqd,bhrwckd->bhrcqwk', qg, kg).astype(F32) * scale + bias
    s_nb = s_nb.reshape(b, h, rows, ncb, NA_QCB, kr * NA_BAND)
    s_ctx = jnp.einsum('bhrcqd,bhjd->bhrcqj', qg, kc).astype(F32) * scale
    p = jax.nn.softmax(jnp.concatenate([s_nb, s_ctx], axis=-1), axis=-1)
    p_nb = p[..., :kr * NA_BAND].reshape(b, h, rows, ncb, NA_QCB, kr, NA_BAND).astype(v.dtype)
    p_ctx = p[..., kr * NA_BAND:].astype(v.dtype)
    o = jnp.einsum('bhrcqwk,bhrwckd->bhrcqd', p_nb, vg) + jnp.einsum('bhrcqj,bhjd->bhrcqd', p_ctx, vc)
    return o.reshape(b, h, n, d)

def fourier_mix(u):
    b, l, _ = u.shape
    z = jnp.fft.fft2(u.astype(F32).reshape(b, l, FNET_GROUPS, FNET_GROUP_DIM), axes=(1, 3), norm='ortho')
    return jnp.real(z).reshape(b, l, W_B).astype(u.dtype)

def sliding_window_gqa(q, k, v, kc, vc, sink):
    b, hq, n, d = q.shape
    g = k.shape[1]
    rep = hq // g
    blk = SWA_BLOCK
    nb = n // blk
    lc = kc.shape[2]
    qb = q.reshape(b, g, rep, nb, blk, d)

    def banded(t):
        tp = jnp.pad(t, ((0, 0), (0, 0), (blk, blk), (0, 0))).reshape(b, g, nb + 2, blk, d)
        return jnp.concatenate([tp[:, :, :-2], tp[:, :, 1:-1], tp[:, :, 2:]], axis=3)

    kb, vb = banded(k), banded(v)
    i = np.arange(blk)
    m = np.arange(3 * blk)
    rel = m[None, :] - blk - i[:, None]
    s_pos = np.arange(nb)[:, None, None] * blk - blk + m[None, None, :]
    ok = (np.abs(rel)[None] <= SWA_WINDOW) & (s_pos >= 0) & (s_pos < n)
    scale = HEAD_DIM ** -0.5
    s_loc = jnp.einsum('bgrnqd,bgnkd->bgrnqk', qb, kb).astype(F32) * scale
    s_loc = jnp.where(ok, s_loc, -jnp.inf)
    s_ctx = jnp.einsum('bgrnqd,bgjd->bgrnqj', qb, kc).astype(F32) * scale
    s_sink = jnp.broadcast_to(sink.astype(F32).reshape(1, g, rep, 1, 1, 1), s_loc.shape[:-1] + (1,))
    p = jax.nn.softmax(jnp.concatenate([s_loc, s_ctx, s_sink], axis=-1), axis=-1)
    p_loc = p[..., :3 * blk].astype(v.dtype)
    p_ctx = p[..., 3 * blk:3 * blk + lc].astype(v.dtype)
    o = jnp.einsum('bgrnqk,bgnkd->bgrnqd', p_loc, vb) + jnp.einsum('bgrnqj,bgjd->bgrnqd', p_ctx, vc)
    return o.reshape(b, hq, n, d)

def hgrn2_gates(fz, lb):
    lb = lb.reshape(HGRN_HEADS, 1, HGRN_DK)
    logf = jnp.logaddexp(jnp.log(lb), jnp.log1p(-lb) + jax.nn.log_sigmoid(fz.astype(F32)))
    return logf, -jnp.expm1(logf)

def chunk_gated_scan(q, k, v, logf, s0):
    b, h, l, dk = q.shape
    dv = v.shape[-1]
    nc = l // HGRN_CHUNK
    causal = np.tril(np.ones((HGRN_CHUNK, HGRN_CHUNK), dtype=bool))

    def to_chunks(t):
        return jnp.moveaxis(t.reshape(b, h, nc, HGRN_CHUNK, t.shape[-1]), 2, 0)

    def step(state, inp):
        qc, kc, vc, gc = inp
        cum = jnp.cumsum(gc, axis=2)
        decay = jnp.exp(jnp.where(causal[:, :, None], cum[:, :, :, None, :] - cum[:, :, None, :, :], -jnp.inf))
        att = jnp.einsum('bhtk,bhsk,bhtsk->bhts', qc, kc, decay)
        o = jnp.einsum('bhts,bhsv->bhtv', att, vc) + jnp.einsum('bhtk,bhkv->bhtv', qc * jnp.exp(cum), state)
        last = cum[:, :, -1]
        state = jnp.exp(last)[..., None] * state + jnp.einsum('bhsk,bhsv->bhkv', kc * jnp.exp(last[:, :, None, :] - cum), vc)
        return state, o

    s_fin, o = lax.scan(step, s0, (to_chunks(q), to_chunks(k), to_chunks(v), to_chunks(logf)))
    return jnp.moveaxis(o, 0, 2).reshape(b, h, l, dv), s_fin

def hgrn2_bidir(q, fz_f, fz_b, v, lb_f, lb_b, s0_f, s0_b):
    dt = v.dtype
    q32, v32 = q.astype(F32), v.astype(F32)
    logf_f, k_f = hgrn2_gates(fz_f, lb_f)
    logf_b, k_b = hgrn2_gates(fz_b, lb_b)
    o_f, s_f = chunk_gated_scan(q32, k_f, v32, logf_f, s0_f)
    rev = lambda t: jnp.flip(t, axis=2)
    o_b, s_b = chunk_gated_scan(rev(q32), rev(k_b), rev(v32), rev(logf_b), s0_b)
    return (o_f + rev(o_b)).astype(dt), s_f, s_b

def hgrn_out(o, g, gain):
    om = merge(o)
    b, l, _ = om.shape
    on = rms_norm(om.reshape(b, l, HGRN_HEADS, HGRN_DV), gain.reshape(HGRN_HEADS, HGRN_DV)).reshape(b, l, W_DV)
    return on * jax.nn.silu(g)

def swiglu(h, w_in, w_out):
    a, gt = jnp.split(h @ w_in, 2, axis=-1)
    return (jax.nn.silu(a) * gt) @ w_out

def setup_inputs(seed: int = 0) -> dict:
    key = jax.random.key(seed)
    ks = jax.random.split(key, 20)
    nrm = lambda k, shape, s: jax.random.normal(k, shape, F32) * s
    return {
        'x': nrm(ks[0], (BATCH, SEQ, D_MODEL), 1.0),
        'c': nrm(ks[1], (BATCH, D_MODEL), 1.0),
        'ctx': nrm(ks[2], (BATCH, CTX_LEN, D_MODEL), 1.0),
        'c_ctx': nrm(ks[3], (D_MODEL,), 1.0),
        'w_ada': nrm(ks[4], (DEPTH, D_MODEL, 6 * D_MODEL), 0.5 * D_MODEL ** -0.5),
        'b_ada': nrm(ks[5], (DEPTH, 6 * D_MODEL), 0.02),
        'g_pre_mix': 1.0 + nrm(ks[6], (DEPTH, D_MODEL), 0.1),
        'g_post_mix': 1.0 + nrm(ks[7], (DEPTH, D_MODEL), 0.1),
        'g_pre_ffn': 1.0 + nrm(ks[8], (DEPTH, D_MODEL), 0.1),
        'g_post_ffn': 1.0 + nrm(ks[9], (DEPTH, D_MODEL), 0.1),
        'w_in': nrm(ks[10], (DEPTH, D_MODEL, D_IN), D_MODEL ** -0.5),
        'w_out': nrm(ks[11], (DEPTH, D_MIX, D_MODEL), D_MIX ** -0.5),
        'na_rpb': nrm(ks[12], (DEPTH, NA_HEADS, 2 * NA_WIN_R - 1, 2 * NA_WIN_C - 1), 0.2),
        'w_fnet': nrm(ks[13], (DEPTH, W_B, W_B), W_B ** -0.5),
        'swa_sink': nrm(ks[14], (DEPTH, SWA_HEADS), 1.0),
        'hgrn_lb_logits': nrm(ks[15], (2, DEPTH, W_DK), 1.0),
        'hgrn_norm_g': 1.0 + nrm(ks[16], (DEPTH, W_DV), 0.1),
        'w_ffn_in': nrm(ks[17], (DEPTH, D_MODEL, 2 * D_FF), D_MODEL ** -0.5),
        'w_ffn_out': nrm(ks[18], (DEPTH, D_FF, D_MODEL), D_FF ** -0.5),
    }

def reference(x, c, ctx, c_ctx, w_ada, b_ada, g_pre_mix, g_post_mix, g_pre_ffn, g_post_ffn, w_in, w_out,
              na_rpb, w_fnet, swa_sink, hgrn_lb_logits, hgrn_norm_g, w_ffn_in, w_ffn_out):
    b, n, _ = x.shape
    pos = np.arange(n)
    rows_pos, cols_pos = pos // GRID_W, pos % GRID_W
    lb_all = jnp.cumsum(jax.nn.softmax(hgrn_lb_logits.astype(F32), axis=1), axis=1)
    lb_all = lb_all - lb_all[:, :1]
    s_zero = jnp.zeros((b, HGRN_HEADS, HGRN_DK, HGRN_DV), F32)
    h_ctx = ctx
    for l in range(DEPTH):
        sh1, sc1, gt1, sh2, sc2, gt2 = jnp.split((jax.nn.silu(c) @ w_ada[l] + b_ada[l])[:, None, :], 6, axis=-1)
        csh1, csc1, cgt1, csh2, csc2, cgt2 = jnp.split((jax.nn.silu(c_ctx) @ w_ada[l] + b_ada[l])[None, None, :], 6, axis=-1)
        u = modulate(rms_norm(x, g_pre_mix[l]), sh1, sc1) @ w_in[l]
        uc = modulate(rms_norm(h_ctx, g_pre_mix[l]), csh1, csc1) @ w_in[l]
        qa, ka, va, ub, qs, ks, vs, qd, fdf, fdb, iv, gd = split_in(u)
        qa_c, ka_c, va_c, ub_c, qs_c, ks_c, vs_c, qd_c, fdf_c, fdb_c, iv_c, gd_c = split_in(uc)
        ka_c, va_c = heads(ka_c, NA_HEADS), heads(va_c, NA_HEADS)
        ks_c, vs_c = heads(ks_c, SWA_KV_HEADS), heads(vs_c, SWA_KV_HEADS)
        od_c, s_f, s_b = hgrn2_bidir(jax.nn.silu(heads(qd_c, HGRN_HEADS)), heads(fdf_c, HGRN_HEADS),
                                     heads(fdb_c, HGRN_HEADS), heads(iv_c, HGRN_HEADS),
                                     lb_all[0, l], lb_all[1, l], s_zero, s_zero)
        o_a = neighbourhood_attention(heads(qa, NA_HEADS), heads(ka, NA_HEADS), heads(va, NA_HEADS), ka_c, va_c, na_rpb[l])
        o_b = fourier_mix(ub) @ w_fnet[l]
        o_c = sliding_window_gqa(axial_rope(heads(qs, SWA_HEADS), rows_pos, cols_pos),
                                 axial_rope(heads(ks, SWA_KV_HEADS), rows_pos, cols_pos),
                                 heads(vs, SWA_KV_HEADS), ks_c, vs_c, swa_sink[l])
        od, _, _ = hgrn2_bidir(jax.nn.silu(heads(qd, HGRN_HEADS)), heads(fdf, HGRN_HEADS), heads(fdb, HGRN_HEADS),
                               heads(iv, HGRN_HEADS), lb_all[0, l], lb_all[1, l], s_f, s_b)
        o_d = hgrn_out(od, gd, hgrn_norm_g[l])
        mix = jnp.concatenate([merge(o_a), o_b, merge(o_c), o_d], axis=-1) @ w_out[l]
        x = x + gt1 * rms_norm(mix, g_post_mix[l])
        ffn = swiglu(modulate(rms_norm(x, g_pre_ffn[l]), sh2, sc2), w_ffn_in[l], w_ffn_out[l])
        x = x + gt2 * rms_norm(ffn, g_post_ffn[l])
        if l < DEPTH - 1:
            o_a_c = dense_attention(heads(qa_c, NA_HEADS), ka_c, va_c)
            o_b_c = fourier_mix(ub_c) @ w_fnet[l]
            o_c_c = dense_attention(heads(qs_c, SWA_HEADS), ks_c, vs_c, swa_sink[l])
            o_d_c = hgrn_out(od_c, gd_c, hgrn_norm_g[l])
            mix_c = jnp.concatenate([merge(o_a_c), o_b_c, merge(o_c_c), o_d_c], axis=-1) @ w_out[l]
            h_ctx = h_ctx + cgt1 * rms_norm(mix_c, g_post_mix[l])
            ffn_c = swiglu(modulate(rms_norm(h_ctx, g_pre_ffn[l]), csh2, csc2), w_ffn_in[l], w_ffn_out[l])
            h_ctx = h_ctx + cgt2 * rms_norm(ffn_c, g_post_ffn[l])
    return x


_drawn_inputs = setup_inputs


def setup_inputs(seed=0):
    import zlib

    import numpy as np

    out = dict(_drawn_inputs(seed))
    spreads = {}
    factors = {'na_rpb': 8.0, 'swa_sink': 8.0, 'hgrn_lb_logits': 3.341}
    for name, (base, spread) in spreads.items():
        noise = np.random.default_rng([zlib.crc32(name.encode()), seed]).standard_normal(out[name].shape)
        drawn = base * np.exp(spread * noise) if base else spread * noise
        out[name] = __import__('jax').numpy.asarray(drawn.astype(out[name].dtype))
    for name, factor in factors.items():
        out[name] = (out[name] * factor).astype(out[name].dtype)
    return out
```

```python
from contextlib import ExitStack

import numpy as np

import concourse.bass as bass
from concourse import mybir
from concourse.alu_op_type import AluOpType as ALU

ACT = mybir.ActivationFunctionType
AX_X = mybir.AxisListType.X
F32 = mybir.dt.float32
F32R = mybir.dt.float32r
U8 = mybir.dt.uint8

P = 128
D = 1024
NC = D // P
LAT, CTX = 512, 256
TOK = LAT + CTX
DEPTH = 2
DFF = 2816
GRID_W, ROWS = 64, LAT // 64
HD = 64
EPS = 1e-6
NEG = -1e30
SCALE = HD ** -0.5

KA, VA, KS, VS, FF, FB, IV, QA, UB, QS, QD, GD = 0, 2, 4, 5, 6, 8, 10, 12, 14, 16, 18, 20
N_PROJ, N_PROJ_CTX = 22, 12
FFN_CHUNKS = (8, 8, 6)
N_OUT = NC

SH1, SC1, GT1, SH2, SC2, GT2 = (NC * i for i in range(6))
N_ADA = 6 * NC
G_PRE_MIX, G_POST_MIX, G_PRE_FFN, G_POST_FFN = range(4)

RPB_W = 64
RPB_PAD = 16
BAND = 32
BAND0 = (0, 8, 24, 32)

LEVELS = 7

STREAMS = ((0, LAT, 0), (LAT, TOK, 1))


def tile_counts(layer):
    g = layer * 49
    at = {"proj": g}
    g += N_PROJ // 2
    at["wout"] = g
    g += N_OUT // 2
    for p, kc in enumerate(FFN_CHUNKS):
        at["in", p] = g
        g += kc
        at["out", p] = g
        g += N_OUT // 2
    at["end"] = g
    return at


N_PAIRS = tile_counts(DEPTH - 1)["end"]


def backwards(ap):
    dims = [list(d) for d in ap.ap]
    step, n = dims[-1]
    return bass.AP(ap.tensor, ap.offset + step * (n - 1), dims[:-1] + [[-step, n]])


def attention_plan(kind, layer):
    return [(True, t) for t in range(4)] + ([(False, t) for t in range(2)] if layer < DEPTH - 1 else [])


def misc_uses(kind, tiles):
    order = {}
    if kind == "na":
        order["vctx"] = len(order)
    steps = 4 * len(tiles) + 2
    for s in range(steps):
        if kind == "na" and s % 4 == 0 and s // 4 < 4:
            order["v", s // 4] = len(order)
        if s >= 7 and s % 4 == 3:
            order["o", s // 4 - 1] = len(order)
    order["o", len(tiles) - 1] = len(order)
    return order


def hybrid_kernel(nc, xT, cvec, wstream, adaT, badaT, gT, rpb, wf, sink, lbT, hgT, dftL, dftC, dftD, rotm,
                  rope, swamask, namask, lvmask, sqc, out):
    with ExitStack() as ctx:
        def sem(name):
            return ctx.enter_context(nc.semaphore(name))

        top = [(nc.sbuf_base + 63) // 64 * 64]
        ctx.enter_context(nc.sbuf_tensor("arena", [P, 212_600], U8))

        def region(nbytes):
            top[0] += nbytes
            return top[0] - nbytes

        def at(name, shape, dt, base, off=0):
            return nc.alloc_sbuf_tensor_at(name, shape, dt, offset=base + off)

        CH = TOK * 4
        r_x, r_h, r_big, r_f = region(NC * CH), region(2 * NC * CH), region(N_PROJ * CH), region(NC * CH)
        r_w, r_ada, r_cb = region(3 * 2 * D * 4), region(2 * D * 4), region(2 * D * 4)
        r_sm = region(5700)
        assert top[0] <= nc.sbuf_usable_end

        x = at("x", [P, NC, TOK], F32, r_x)
        h_hi = at("h_hi", [P, NC, TOK], F32R, r_h)
        h_lo = at("h_lo", [P, NC, TOK], F32R, r_h, NC * CH)
        u_t = at("u_t", [P, N_PROJ, TOK], F32, r_big)
        hid_hi = at("hid_hi", [P, 8, TOK], F32R, r_big)
        hid_lo = at("hid_lo", [P, 8, TOK], F32R, r_big, 8 * CH)
        sq = at("sq", [P, 2, TOK], F32, r_big, 16 * CH)
        tmp = at("tmp", [P, 2, TOK], F32, r_big, 18 * CH)
        lnms = at("lnms", [P, TOK], F32, r_big, 20 * CH)
        rstd = at("rstd", [P, TOK], F32, r_big, 21 * CH)
        f_t = at("f_t", [P, NC, TOK], F32, r_f)
        raw = at("raw", [P, 2, D], F32, r_w)
        w_hi = at("w_hi", [P, 2, NC, P], F32R, r_w, 2 * D * 4)
        w_lo = at("w_lo", [P, 2, NC, P], F32R, r_w, 4 * D * 4)
        ada_w = at("ada_w", [P, 2, D], F32, r_ada)
        c_b = at("c_b", [P, 2, D], F32, r_cb)
        small_top = [0]

        def small(name, shape, dt=F32):
            n = int(np.prod(shape[1:])) * (4 if dt == F32 else 1)
            small_top[0] += (n + 31) // 32 * 32
            assert small_top[0] <= 5700
            return at(name, shape, dt, r_sm, small_top[0] - (n + 31) // 32 * 32)

        consts = small("consts", [P, 3, P])
        ones, ident, blockones = consts[:, 0], consts[:, 1], consts[:, 2]
        ada_c = [small(f"ada_c{l}", [P, N_ADA, 2]) for l in range(DEPTH)]
        ada_t = small("ada_t", [P, 2, 2])
        bada = small("bada", [P, DEPTH, N_ADA])
        gcol = small("gcol", [P, DEPTH, 4, NC])
        col_sh = small("col_sh", [P, NC, 2])
        col_sc = small("col_sc", [P, NC, 2])
        col_gs = small("col_gs", [P, NC, 2])
        col_gg = small("col_gg", [P, NC, 2])
        eps_c = small("eps_c", [P, 1])
        sinks = small("sinks", [P, DEPTH, 4])
        sink8 = small("sink8", [P, DEPTH, 4])
        lbc = small("lbc", [P, 2, DEPTH, 2])
        lb = small("lb", [P, 2, 2])
        lb1 = small("lb1", [P, 2, 2])
        lbt = small("lbt", [P, 2, 2, 2])
        hgain = small("hgain", [P, DEPTH, 2])
        mx = small("mx", [P, 2])
        nb = small("nb", [P, 4])
        sums = small("sums", [P, 2, 4])
        sinke = small("sinke", [P, 2, 4])
        rinv = small("rinv", [P, 4])

        fn_l = at("fn_l", [P, 4, 2, LAT], F32, r_h)
        fn_c = at("fn_c", [P, 2, 2, CTX], F32, r_h, 16384)
        fn_d = at("fn_d", [P, 2 * P], F32, r_h, 20480)
        fn_w = at("fn_w", [P, 2, 2 * P], F32, r_h, 21504)
        fn_ab = at("fn_ab", [P, 6, 4 * P], F32, r_h, 23552)
        fn_f = at("fn_f", [P, 2, TOK], F32, r_h, 35840)

        s_sb = at("s_sb", [P, 2, 640], F32, r_h)
        p_sb = at("p_sb", [P, 2, 640], F32, r_h, 5120)
        pt_sb = at("pt_sb", [P, 2, 640], F32, r_h, 10240)
        o_sb = at("o_sb", [P, 2, 256], F32, r_h, 15360)
        na_b = at("na_b", [P, 2, 4, 512], F32, r_h, 17408)
        na_v = at("na_v", [P, 2, 2, 256], F32, r_h, 33792)
        na_vc = at("na_vc", [P, 2, 256], F32, r_h, 37888)
        na_m = at("na_m", [P, 4, BAND], F32, r_h, 39936)
        na_r = at("na_r", [P, 2, 1024], F32, r_h, 40448)
        na_q = at("na_q", [P, 2, 2, P], F32, r_f, 6 * CH)
        na_vs = at("na_vs", [P, 2, 2, 256], F32, r_f, 6 * CH + 2048)
        sw_m = at("sw_m", [P, 3, 640], F32, r_h, 17408)
        sw_v = at("sw_v", [P, 6, P], F32, r_h, 25088)
        sw_cs = at("sw_cs", [P, 2, LAT], F32, r_h, 28160)
        sw_r = at("sw_r", [P, P], F32, r_h, 32256)
        sw_t = at("sw_t", [P, 2, LAT], F32, r_h, 32768)

        hq = at("hq", [P, 2, TOK], F32, r_h)
        hk = at("hk", [P, 2, TOK], F32, r_h, 6144)
        ha = at("ha", [P, 2, TOK], F32, r_h, 12288)
        hatt = at("hatt", [P, 2, TOK], F32, r_h, 18432)
        hv = at("hv", [P, 6, P], F32, r_h, 24576)
        hkt = at("hkt", [P, 2, TOK], F32, r_h, 27648)
        hst = at("hst", [P, 2, 6, P], F32, r_h, 33792)
        ho = at("ho", [P, TOK], F32, r_h, 39936)
        hmask = at("hmask", [P, 2 * LEVELS, P], U8, r_h, 43008)
        hmask_f = at("hmask_f", [P, 2 * LEVELS, P], F32, r_h, 12288)
        hms = at("hms", [P, TOK], F32, r_h, 44800)

        ps = [ctx.enter_context(nc.psum_tensor(f"ps{i}", [P, 1024], F32)) for i in range(4)]
        ps_o, ps_m = ps[3][:, 0:512], ps[3][:, 512:1024]

        raw_ld = [sem(f"raw_loaded{u}") for u in range(2)]
        w_hi_done, w_lo_done = sem("w_hi_done"), sem("w_lo_done")
        blk_done = sem("block_product_done")
        bank_free = [sem(f"block_bank_free{u}") for u in range(2)]
        hid_hi_done, hid_lo_done = sem("hid_hi_done"), sem("hid_lo_done")
        ada_ld = [sem(f"ada_loaded{u}") for u in range(2)]
        ada_done, ada_copied = sem("ada_products_done"), sem("ada_copied")
        s_in, s_cin, s_cb = sem("inputs_loaded"), sem("c_loaded"), sem("c_activated")
        s_out = sem("output_stored")
        consts_done = sem("small_consts_done")
        dve_chain, act_chain = sem("dve_chain"), sem("act_chain")
        sq_ready, sq_used = sem("squares_ready"), sem("squares_used")
        rstd_ready = sem("rstd_ready")
        scaled = sem("scaled_ready")
        hhi_ready, hlo_ready = sem("h_hi_ready"), sem("h_lo_ready")
        x_upd, pn_m = sem("x_updated"), sem("post_norm_scaled")
        mix_done = sem("mixer_done")
        fn_ld, fn_a, fn_abe = sem("fnet_loaded"), sem("fnet_channels"), sem("fnet_channels_copied")
        fn_t, fn_te, fn_o = sem("fnet_tokens"), sem("fnet_tokens_copied"), sem("fnet_out")
        at_ld = sem("attention_consts_loaded")
        na_ld = [sem(f"na_bias_loaded{u}") for u in range(2)]
        na_bias, na_st = sem("na_bias_ready"), sem("na_block_staged")
        at_pre, at_pre_c = sem("attention_v_transposed"), sem("attention_v_copied")
        rope_p, rope_d = sem("rope_rotated"), sem("rope_done")
        at_s, at_n, at_p = sem("scores"), sem("score_max"), sem("probs")
        at_t, at_tc, at_pv = sem("probs_transposed"), sem("probs_t_copied"), sem("pv_done")
        at_sk = sem("sink_exp")
        at_o, ms_w, ms_r = sem("attention_out_scaled"), sem("misc_written"), sem("misc_read")
        hg_ld, hg_gate, hg_init = sem("hgrn_masks_loaded"), sem("hgrn_gates"), sem("hgrn_init")
        hg_v, hg_vc = sem("hgrn_v_transposed"), sem("hgrn_v_copied")
        hg_a, hg_m, hg_u = sem("hgrn_att"), sem("hgrn_att_masked"), sem("hgrn_level_up")
        hg_kt, hg_ktc = sem("hgrn_k_transposed"), sem("hgrn_k_copied")
        hg_ds, hg_st, hg_o = sem("hgrn_ds"), sem("hgrn_states"), sem("hgrn_out")
        hg_sq, hg_ms, hg_rs, hg_end = sem("hgrn_sq"), sem("hgrn_ms"), sem("hgrn_rstd"), sem("hgrn_pair_done")

        block = ctx.enter_context(nc.Block())
        TP = [tile_counts(l) for l in range(DEPTH)]
        full = [l < DEPTH - 1 for l in range(DEPTH)]
        width = [TOK if f else LAT for f in full]
        MIXERS = 4
        phases = [(kind, l) for l in range(DEPTH) for kind in ("na", "swa")]
        unit0, tile0, misc0 = {}, {}, {}
        t0_swa = [l * len(attention_plan("swa", 0)) for l in range(DEPTH)]
        nu = nt = nm = 0
        for ph in phases:
            unit0[ph], tile0[ph], misc0[ph] = nu, nt, nm
            tiles = attention_plan(*ph)
            nu, nt, nm = nu + 4 * len(tiles), nt + len(tiles), nm + len(misc_uses(ph[0], tiles))

        @block.sync
        def _(sp):
            for u in range(2):
                sp.dma_start(raw[:, u], wstream[u]).then_inc(raw_ld[u], 16)
            with sp.Fori(1, N_PAIRS) as g:
                for u in range(2):
                    sp.wait_ge(w_lo_done, 2 * g + (u - 1))
                    sp.dma_start(raw[:, u], wstream[2 * g + u]).then_inc(raw_ld[u], 16)
            sp.wait_ge(x_upd, 2 * DEPTH * NC)
            sp.dma_start(out.rearrange("(c p) t -> p c t", p=P), x[:, :, 0:LAT]).then_inc(s_out, 16)
            sp.wait_ge(s_out, 16)

        @block.gpsimd
        def _(pool):
            def ada_loads(p0, n):
                with pool.Fori(p0, p0 + n) as q:
                    for u in range(2):
                        pool.wait_ge(ada_done, 4 * q + (2 * u - 1))
                        pool.dma_start(ada_w[:, u], adaT[2 * q + u]).then_inc(ada_ld[u], 16)

            for v in range(2):
                pool.dma_start(c_b[:, v], bass.AP(cvec.tensor, v * D, [[0, P], [1, D]])).then_inc(s_cin, 16)
            for u in range(2):
                pool.dma_start(ada_w[:, u], adaT[u]).then_inc(ada_ld[u], 16)
            pool.dma_start(x[:], xT.rearrange("(c p) t -> p c t", p=P)).then_inc(s_in, 16)
            pool.dma_start(consts[:], sqc.rearrange("k p n -> p k n")).then_inc(s_in, 16)
            pool.dma_start(bada[:], badaT).then_inc(s_in, 16)
            pool.dma_start(gcol[:], gT).then_inc(s_in, 16)
            pool.dma_start(sinks[:], bass.AP(sink.tensor, 0, [[0, P], [4, DEPTH], [1, 4]])).then_inc(s_in, 16)
            pool.dma_start(lbc[:], lbT).then_inc(s_in, 16)
            pool.dma_start(hgain[:], hgT).then_inc(s_in, 16)
            ada_loads(1, 8)
            for l in range(DEPTH):
                if l == 0:
                    ada_loads(9, 11)
                pool.wait_ge(blk_done, 2 * TP[l]["wout"])
                pool.dma_start(fn_d[:], dftD).then_inc(fn_ld, 16)
                pool.dma_start(fn_l[:], dftL).then_inc(fn_ld, 16)
                pool.dma_start(fn_c[:], dftC).then_inc(fn_ld, 16)
                pool.dma_start(fn_w[:], wf[l]).then_inc(fn_ld, 16)
                pool.wait_ge(mix_done, MIXERS * l + 1)
                pool.dma_start(na_m[:], namask).then_inc(at_ld, 16)
                for cb in range(4):
                    if cb >= 2:
                        pool.wait_ge(na_bias, 4 * l + cb - 1)
                    for rq in range(ROWS):
                        off = (l * 15 + 7 - rq) * 4 * RPB_W + BAND0[cb] - 16 * cb + RPB_PAD
                        src = bass.AP(rpb.tensor, off, [[1, 16], [RPB_W, 4 * ROWS], [1, BAND]])
                        dst = na_r[16 * rq:16 * rq + 16, cb % 2].rearrange("p (n c) -> p n c", c=BAND)
                        pool.dma_start(dst, src).then_inc(na_ld[cb % 2], 16)
                    if cb >= 2:
                        pool.wait_ge(at_s, unit0["na", l] + 4 * (cb - 1))
                    for p in range(2):
                        q = u_t[:, QA + p, 0:LAT].rearrange("p (r c) -> p r c", c=GRID_W)
                        v = u_t[:, VA + p, 0:LAT].rearrange("p (r c) -> p r c", c=GRID_W)
                        pool.tensor_copy(na_q[:, cb % 2, p].rearrange("p (r c) -> p r c", c=16),
                                         backwards(q[:, :, 16 * cb:16 * cb + 16]))
                        ins = pool.tensor_copy(na_vs[:, cb % 2, p].rearrange("p (r c) -> p r c", c=BAND),
                                               v[:, :, BAND0[cb]:BAND0[cb] + BAND])
                    ins.then_inc(na_st, 1)
                pool.wait_ge(mix_done, MIXERS * l + 2)
                pool.dma_start(sw_r[:], rotm).then_inc(at_ld, 16)
                pool.dma_start(sw_cs[:], rope).then_inc(at_ld, 16)
                pool.dma_start(sw_m[:], swamask).then_inc(at_ld, 16)
                pool.wait_ge(mix_done, MIXERS * l + 3)
                pool.dma_start(hmask_f[:], lvmask).then_inc(hg_ld, 16)
                if l == 0:
                    ada_loads(20, 4)
                    ada_loads(24, 24)

        @block.scalar
        def _(act):
            chain = [0]

            def link(ins):
                chain[0] += 1
                ins.then_inc(act_chain, 1)
                act.wait_ge(act_chain, chain[0])

            def split_hi(g, u):
                act.wait_ge(raw_ld[u], 16 * g + 32)
                act.wait_ge(blk_done, 2 * g + (u + 1))
                act.activation(w_hi[:, u].rearrange("p c n -> p (c n)"), raw[:, u], ACT.Copy).then_inc(w_hi_done, 1)

            def copy_phase(g0, n, dst, b0, T):
                with act.Fori(0, n) as i:
                    for u in range(2):
                        act.wait_ge(blk_done, 2 * i + (2 * g0 + u + 1))
                        act.activation(dst[:, 2 * i + (b0 + u), 0:T], ps[u][:, 0:T], ACT.Copy)\
                           .then_inc(bank_free[u], 1)
                        split_hi(i + g0, u)

            def splits_only(g0, n, last):
                if n - last > 0:
                    with act.Fori(0, n - last) as i:
                        for u in range(2):
                            split_hi(i + g0, u)

            def ffn_in(g0, q0, n, T):
                with act.Fori(0, n) as i:
                    act.wait_ge(blk_done, 2 * i + (2 * g0 + 1))
                    act.wait_ge(bank_free[1], i + (g0 + 1))
                    act.activation(tmp[:, 0, 0:T], ps[0][:, 0:T], ACT.Silu).then_inc(bank_free[0], 1)
                    split_hi(i + g0, 0)
                    split_hi(i + g0, 1)
                    act.wait_ge(bank_free[1], i + (g0 + 2))
                    act.activation(hid_hi[:, i, 0:T], tmp[:, 1, 0:T], ACT.Copy).then_inc(hid_hi_done, 1)

            nsq, nn = [0], [0]

            def mean_square(src, T, ready):
                for c in range(NC):
                    ready(c)
                    if nsq[0] >= 2:
                        act.wait_ge(sq_used, nsq[0] - 1)
                    act.activation(sq[:, c % 2, 0:T], src[:, c, 0:T], ACT.Square).then_inc(sq_ready, 1)
                    nsq[0] += 1
                act.wait_ge(sq_used, nsq[0])
                link(act.activation(lnms[:, 0:T], ps[2][:, 0:T], ACT.Ln, bias=eps_c[:, 0:1], scale=1.0 / D))
                act.activation(rstd[:, 0:T], lnms[:, 0:T], ACT.Exp, scale=-0.5).then_inc(rstd_ready, 1)

            def pre_norm(T, ready):
                mean_square(x, T, ready)
                for c in range(NC):
                    for lo, hi, v in STREAMS[:2 if T == TOK else 1]:
                        act.wait_ge(scaled, nn[0] + 1)
                        nn[0] += 1
                        act.activation(h_hi[:, c, lo:hi], tmp[:, c % 2, lo:hi], ACT.Identity,
                                       bias=col_sh[:, c, v:v + 1]).then_inc(hhi_ready, 1)

            def attention(kind, l):
                tiles = attention_plan(kind, l)
                u0, t0 = unit0[kind, l], tile0[kind, l]
                U = 4 * len(tiles)
                if kind == "swa":
                    act.wait_ge(mix_done, MIXERS * l + 2)
                else:
                    act.wait_ge(mix_done, MIXERS * l + 1)
                for s in range(U + 1):
                    if s < U:
                        n = (384 if kind == "swa" else 256) * tiles[s // 4][0] + 256
                        act.wait_ge(at_n, u0 + s + 1)
                        if u0 + s >= 2:
                            act.wait_ge(at_t, u0 + s - 1)
                        if s % 4 == 0 and s >= 8:
                            act.wait_ge(at_o, t0 + s // 4 - 1)
                        act.activation(p_sb[:, s % 2, 0:n], s_sb[:, s % 2, 0:n], ACT.Exp,
                                       bias=nb[:, s % 4:s % 4 + 1], scale=SCALE,
                                       accum_out=sums[:, s // 4 % 2, s % 4:s % 4 + 1]).then_inc(at_p, 1)
                        if kind == "swa" and s % 4 == 3:
                            act.activation(sinke[:, s // 4 % 2], sinke[:, s // 4 % 2], ACT.Exp).then_inc(at_sk, 1)
                    if s >= 1:
                        v = s - 1
                        n = (384 if kind == "swa" else 256) * tiles[v // 4][0] + 256
                        act.wait_ge(at_t, u0 + v + 1)
                        if u0 + v >= 2:
                            act.wait_ge(at_pv, u0 + v - 1)
                        act.activation(pt_sb[:, v % 2, 0:n], ps[2][:, 0:n], ACT.Copy).then_inc(at_tc, 1)

            for u in range(2):
                act.sem_inc(bank_free[u], 1)
            act.wait_ge(s_cin, 32)
            act.activation(c_b[:].rearrange("p v d -> p (v d)"), c_b[:].rearrange("p v d -> p (v d)"),
                           ACT.Silu).then_inc(s_cb, 1)
            for u in range(2):
                act.wait_ge(raw_ld[u], 16)
                act.activation(w_hi[:, u].rearrange("p c n -> p (c n)"), raw[:, u], ACT.Copy).then_inc(w_hi_done, 1)
            act.wait_ge(consts_done, 1)
            act.activation(lbt[:], lbt[:], ACT.Exp).then_inc(consts_done, 1)

            for l in range(DEPTH):
                tp, T = TP[l], width[l]
                if l == 0:
                    act.wait_ge(s_in, 16 * 7)
                    act.wait_ge(consts_done, 2)
                    pre_norm(TOK, lambda c: None)
                    copy_phase(tp["proj"], N_PROJ // 2, u_t, 0, TOK)
                else:
                    pre_norm(TOK, lambda c: act.wait_ge(x_upd, 2 * l * NC - NC + c + 1))
                    copy_phase(tp["proj"], N_PROJ_CTX // 2, u_t, 0, TOK)
                    copy_phase(tp["proj"] + N_PROJ_CTX // 2, (N_PROJ - N_PROJ_CTX) // 2, u_t, N_PROJ_CTX, LAT)
                for j in range(T // P):
                    act.wait_ge(fn_a, sum(width[:l]) // P + j + 1)
                    act.activation(fn_ab[:, j], ps[j % 2][:, 0:512], ACT.Copy).then_inc(fn_abe, 1)
                attention("na", l)
                attention("swa", l)
                act.wait_ge(mix_done, MIXERS * l + 3)
                for p in range(2):
                    n = 2 * l + p
                    if p:
                        act.wait_ge(hg_end, n)
                    for d in range(2):
                        fz = u_t[:, (FF, FB)[d] + p, :]
                        link(act.activation(hk[:, d], fz, ACT.Sigmoid, scale=-1.0))
                        act.activation(fz, fz, ACT.Sigmoid)
                    act.activation(u_t[:, QD + p, 0:T], u_t[:, QD + p, 0:T], ACT.Silu)
                    act.activation(u_t[:, GD + p, 0:T], u_t[:, GD + p, 0:T], ACT.Silu).then_inc(hg_gate, 1)
                    for d in range(2):
                        act.wait_ge(hg_kt, 2 * n + d + 1)
                        act.activation(hkt[:, d], ps[d][:, 0:TOK], ACT.Copy).then_inc(hg_ktc, 1)
                    act.wait_ge(hg_o, n + 1)
                    act.activation(hkt[:, 0, 0:T], ps[3][:, 0:T], ACT.Square).then_inc(hg_sq, 1)
                    act.wait_ge(hg_ms, n + 1)
                    link(act.activation(hms[:, 0:T], ps[2][:, 0:T], ACT.Ln, bias=eps_c[:, 0:1], scale=1.0 / HD))
                    act.activation(hkt[:, 1, 0:T], hms[:, 0:T], ACT.Exp, scale=-0.5).then_inc(hg_rs, 1)
                act.wait_ge(mix_done, MIXERS * l + 4)
                for c in range(NC):
                    act.activation(h_hi[:, c, 0:T], f_t[:, c, 0:T], ACT.Copy).then_inc(hhi_ready, 1)
                copy_phase(tp["wout"], N_OUT // 2, f_t, 0, T)
                act.wait_ge(bank_free[0], tp["wout"] + N_OUT // 2 + 1)
                act.wait_ge(bank_free[1], tp["wout"] + N_OUT // 2 + 1)
                mean_square(f_t, T, lambda c: None)
                pre_norm(T, lambda c: act.wait_ge(x_upd, 2 * l * NC + c + 1))
                for p, kc in enumerate(FFN_CHUNKS):
                    ffn_in(tp["in", p], 0, kc, T)
                    if p == 0:
                        copy_phase(tp["out", p], N_OUT // 2, f_t, 0, T)
                    else:
                        last = l == DEPTH - 1 and p == len(FFN_CHUNKS) - 1
                        splits_only(tp["out", p], N_OUT // 2, last)
                act.wait_ge(bank_free[0], tp["end"] + 1)
                act.wait_ge(bank_free[1], tp["end"] + 1)
                mean_square(f_t, T, lambda c: None)

        @block.tensor
        def _(pe):
            def product_phase(g0, n, rhs_hi, rhs_lo, kc, T):
                with pe.Fori(0, n) as i:
                    for u in range(2):
                        pe.wait_ge(w_lo_done, 2 * i + (2 * g0 + u + 1))
                        pe.wait_ge(bank_free[u], i + (g0 + 1))
                        for k in range(kc):
                            for w, r, first, last in ((w_hi, rhs_hi, k == 0, False), (w_hi, rhs_lo, False, False),
                                                      (w_lo, rhs_hi, False, k == kc - 1)):
                                for lo, hi, _ in STREAMS[:2 if T == TOK else 1]:
                                    mm = pe.matmul(ps[u][:, lo:hi], w[:, u, k], r[:, k, lo:hi],
                                                   start=first, stop=last)
                        mm.then_inc(blk_done, 1)

            nsq = [0]

            def mean_square(T):
                for c in range(NC):
                    pe.wait_ge(sq_ready, nsq[0] + 1)
                    for lo, hi, _ in STREAMS[:2 if T == TOK else 1]:
                        mm = pe.matmul(ps[2][:, lo:hi], ones, sq[:, c % 2, lo:hi], start=c == 0, stop=c == NC - 1)
                    mm.then_inc(sq_used, 1)
                    nsq[0] += 1

            def fourier(l):
                T = width[l]
                pe.wait_ge(fn_ld, 64 * (l + 1))
                done = sum(width[:l]) // P
                for j in range(T // P):
                    if j >= 2:
                        pe.wait_ge(fn_abe, done + j - 1)
                    for b in range(2):
                        mm = pe.matmul(ps[j % 2][:, 256 * b:256 * b + 256], u_t[:, UB + b, P * j:P * j + P],
                                       fn_d[:], start=True, stop=True)
                    mm.then_inc(fn_a, 1)
                pe.wait_ge(fn_abe, done + T // P)
                for b in range(2):
                    for lo, hi, m, tab in ((0, LAT, 4, fn_l), (LAT, TOK, 2, fn_c))[:2 if T == TOK else 1]:
                        for j in range(m):
                            for part in range(2):
                                mm = pe.matmul(ps[b][:, lo:hi],
                                               fn_ab[:, lo // P + j, 256 * b + P * part:256 * b + P * part + P],
                                               tab[:, j, part], start=j + part == 0, stop=j == m - 1 and part == 1)
                    mm.then_inc(fn_t, 1)
                pe.wait_ge(fn_te, 2 * (l + 1))
                for n in range(2):
                    for lo, hi, _ in STREAMS[:2 if T == TOK else 1]:
                        for b in range(2):
                            mm = pe.matmul(ps[2 + n][:, lo:hi], fn_w[:, b, P * n:P * n + P], fn_f[:, b, lo:hi],
                                           start=b == 0, stop=b == 1)
                    mm.then_inc(fn_o, 1)

            def attention(kind, l):
                tiles = attention_plan(kind, l)
                u0, t0, m0 = unit0[kind, l], tile0[kind, l], misc0[kind, l]
                uses = misc_uses(kind, tiles)
                U = 4 * len(tiles)
                L = 384 if kind == "swa" else 256

                def misc_free(key):
                    if m0 + uses[key] > 0:
                        pe.wait_ge(ms_r, m0 + uses[key])

                def lat_rows(blk, lo, hi, row0, nrow, col0, ncol):
                    v = u_t[lo:hi, blk, 0:LAT].rearrange("p (r c) -> p r c", c=GRID_W)
                    return v[:, row0:row0 + nrow, col0:col0 + ncol]

                def queries(t, h):
                    lat, i = tiles[t]
                    if kind == "na":
                        a = 64 * (h % 2)
                        return (na_q[a:a + 64, i % 2, h // 2] if lat else
                                u_t[a:a + 64, QA + h // 2, LAT + P * i:LAT + P * i + P])
                    a = 64 * (h // 2)
                    o = P * i if lat else LAT + P * i
                    return u_t[a:a + 64, QS + h % 2, o:o + P]

                def scores(s):
                    t, h = s // 4, s % 4
                    lat, i = tiles[t]
                    bank = ps[s % 2]
                    if u0 + s >= 2:
                        pe.wait_ge(at_n, u0 + s - 1)
                    a, kb = (64 * (h % 2), KA + h // 2) if kind == "na" else (64 * (h // 2), KS)
                    if lat:
                        if kind == "na":
                            keys = lat_rows(kb, a, a + 64, 0, ROWS, BAND0[i], BAND)
                            dst = bank[:, 256:512].rearrange("p (r c) -> p r c", c=BAND)
                        else:
                            first = P * min(max(i - 1, 0), 1)
                            keys = u_t[a:a + 64, kb, first:first + L]
                            dst = bank[:, 512 - L:512]
                        pe.matmul(dst, queries(t, h), keys, start=True, stop=True)
                    pe.matmul(bank[:, 512:768], queries(t, h), u_t[a:a + 64, kb, LAT:TOK],
                              start=True, stop=True).then_inc(at_s, 1)

                def transposes(v):
                    n = L * tiles[v // 4][0] + 256
                    pe.wait_ge(at_p, u0 + v + 1)
                    if u0 + v >= 1:
                        pe.wait_ge(at_tc, u0 + v)
                    for j in range(n // P):
                        mm = pe.transpose(ps[2][:, P * j:P * j + P], p_sb[:, v % 2, P * j:P * j + P], ident)
                    mm.then_inc(at_t, 1)

                def pv(v):
                    t, h = v // 4, v % 4
                    lat, i = tiles[t]
                    n = L * lat + 256
                    pe.wait_ge(at_tc, u0 + v + 1)
                    if h == 0 and t0 + t > 0:
                        pe.wait_ge(at_o, t0 + t)
                    if kind == "na" and h == 0:
                        pe.wait_ge(ms_r, m0 + 1 + (uses["v", i] if lat else 0))
                    for j in range(n // P):
                        local = j < L // P and lat
                        if kind == "na":
                            val = (na_v[:, i % 2, j] if local else na_vc[:, j - L // P * lat])[:, HD * h:HD * h + HD]
                        else:
                            row = min(max(i - 1, 0), 1) + j if local else 4 + j - L // P * lat
                            val = sw_v[:, row, HD * (h // 2):HD * (h // 2) + HD]
                        mm = pe.matmul(ps_o[:, HD * h:HD * h + HD], pt_sb[:, v % 2, P * j:P * j + P], val,
                                       start=j == 0, stop=j == n // P - 1)
                    mm.then_inc(at_pv, 1)

                def out_t(t):
                    pe.wait_ge(at_o, t0 + t + 1)
                    misc_free(("o", t))
                    for p in range(2):
                        mm = pe.transpose(ps_m[:, P * p:P * p + P], o_sb[:, t % 2, P * p:P * p + P], ident)
                    mm.then_inc(ms_w, 1)

                def band_v(i):
                    pe.wait_ge(na_st, 4 * l + i + 1)
                    misc_free(("v", i))
                    for j in range(2):
                        for p in range(2):
                            mm = pe.transpose(ps_m[:, 256 * j + P * p:256 * j + P * p + P],
                                              na_vs[:, i % 2, p, P * j:P * j + P], ident)
                    mm.then_inc(ms_w, 1)

                pe.wait_ge(mix_done, MIXERS * l + (1 if kind == "na" else 2))
                if kind == "na":
                    misc_free("vctx")
                    for j in range(2):
                        for p in range(2):
                            mm = pe.transpose(ps_m[:, 256 * j + P * p:256 * j + P * p + P],
                                              u_t[:, VA + p, LAT + P * j:LAT + P * j + P], ident)
                    mm.then_inc(ms_w, 1)
                else:
                    for j in range(6):
                        mm = pe.transpose(ps[2][:, P * j:P * j + P], u_t[:, VS, P * j:P * j + P], ident)
                    mm.then_inc(at_pre, 1)
                    pe.wait_ge(at_ld, 64 * l + 64)
                    for n, blk in enumerate((KS, QS, QS + 1)):
                        if n >= 2:
                            pe.wait_ge(rope_d, 3 * l + n - 1)
                        pe.matmul(ps[n % 2][:, 0:LAT], sw_r[:], u_t[:, blk, 0:LAT], start=True, stop=True)\
                          .then_inc(rope_p, 1)
                    pe.wait_ge(rope_d, 3 * l + 3)
                    pe.wait_ge(at_pre_c, l + 1)
                for s in range(U + 2):
                    if kind == "na" and s % 4 == 0 and s // 4 < 4:
                        band_v(s // 4)
                    if s < U:
                        scores(s)
                    if 1 <= s <= U:
                        transposes(s - 1)
                    if s >= 2:
                        pv(s - 2)
                    if s >= 7 and s % 4 == 3:
                        out_t(s // 4 - 1)
                out_t(len(tiles) - 1)

            na = [0]

            def hgrn_att(d, h, q, T, n_acc=1):
                for c in range(T // P):
                    mm = pe.matmul(ps[h][:, P * c:P * c + P], hk[64 * h:64 * h + 64, d, P * c:P * c + P],
                                   q[64 * h:64 * h + 64, P * c:P * c + P], start=True, stop=True)
                return mm

            def hgrn(l):
                T = width[l]
                pe.wait_ge(mix_done, MIXERS * l + 3)
                for p in range(2):
                    n = 2 * l + p
                    m0 = 30 * n
                    if p:
                        pe.wait_ge(hg_end, n)
                    for c in range(6):
                        mm = pe.transpose(ps[2][:, P * c:P * c + P], u_t[:, IV + p, P * c:P * c + P], ident)
                    mm.then_inc(hg_v, 1)
                    pe.wait_ge(hg_init, 2 * n + 2)
                    for h in range(2):
                        for c in range(T // P):
                            for d in range(2):
                                mm = pe.matmul(ps[h][:, P * c:P * c + P], hk[64 * h:64 * h + 64, d, P * c:P * c + P],
                                               u_t[64 * h:64 * h + 64, QD + p, P * c:P * c + P],
                                               start=d == 0, stop=d == 1)
                        mm.then_inc(hg_a, 1)
                    for i in range(LEVELS):
                        for d in range(2):
                            if i:
                                pe.wait_ge(hg_u, 14 * n + 2 * (i - 1) + d + 1)
                            for h in range(2):
                                pe.wait_ge(hg_m, m0 + 2 * (2 * i + d) + h + 1)
                                hgrn_att(d, h, hq[:, d], T).then_inc(hg_a, 1)
                    for d in range(2):
                        pe.wait_ge(hg_u, 14 * n + 12 + d + 1)
                        pe.wait_ge(hg_m, m0 + 30)
                        for c in range(6):
                            mm = pe.transpose(ps[d][:, P * c:P * c + P], hk[:, d, P * c:P * c + P], ident)
                        mm.then_inc(hg_kt, 1)
                    pe.wait_ge(hg_vc, n + 1)
                    for d in range(2):
                        pe.wait_ge(hg_ktc, 2 * n + d + 1)
                        if d:
                            pe.wait_ge(hg_st, 2 * n + 1)
                        for j, c in enumerate(ORDER[d][:5]):
                            mm = pe.matmul(ps[2][:, P * j:P * j + P], hkt[:, d, P * c:P * c + P], hv[:, c],
                                           start=True, stop=True)
                        mm.then_inc(hg_ds, 1)
                    pe.wait_ge(hg_st, 2 * n + 2)
                    for c in range(T // P):
                        o = ps[3][:, P * c:P * c + P]
                        terms = [d for d in range(2) if ORDER[d].index(c) > 0]
                        for h in range(2):
                            pe.matmul(o[64 * h:64 * h + 64], hv[:, c, 64 * h:64 * h + 64],
                                      hatt[:, h, P * c:P * c + P], start=True, stop=False, skip_group_check=True)
                        for d in terms:
                            mm = pe.matmul(o, hst[:, d, ORDER[d].index(c)], hq[:, d, P * c:P * c + P], start=False,
                                           stop=d == terms[-1], skip_group_check=True)
                    mm.then_inc(hg_o, 1)
                    pe.wait_ge(hg_sq, n + 1)
                    for lo, hi, _ in STREAMS[:2 if T == TOK else 1]:
                        mm = pe.matmul(ps[2][:, lo:hi], blockones, hkt[:, 0, lo:hi], start=True, stop=True)
                    mm.then_inc(hg_ms, 1)

            hh = [0]
            for l in range(DEPTH):
                tp, T = TP[l], width[l]
                if l == 0:
                    pe.wait_ge(s_in, 16 * 7)
                mean_square(TOK)
                hh[0] += 2 * NC
                pe.wait_ge(hlo_ready, hh[0])
                if full[l]:
                    product_phase(tp["proj"], N_PROJ // 2, h_hi, h_lo, NC, TOK)
                else:
                    product_phase(tp["proj"], N_PROJ_CTX // 2, h_hi, h_lo, NC, TOK)
                    product_phase(tp["proj"] + N_PROJ_CTX // 2, (N_PROJ - N_PROJ_CTX) // 2, h_hi, h_lo, NC, LAT)
                for u in range(2):
                    pe.wait_ge(bank_free[u], tp["wout"] + 1)
                fourier(l)
                attention("na", l)
                attention("swa", l)
                hgrn(l)
                hh[0] += NC
                pe.wait_ge(hlo_ready, hh[0])
                product_phase(tp["wout"], N_OUT // 2, h_hi, h_lo, NC, T)
                mean_square(T)
                mean_square(T)
                hh[0] += NC * (2 if full[l] else 1)
                pe.wait_ge(hlo_ready, hh[0])
                for p, kc in enumerate(FFN_CHUNKS):
                    product_phase(tp["in", p], kc, h_hi, h_lo, NC, T)
                    pe.wait_ge(hid_lo_done, l * 22 + sum(FFN_CHUNKS[:p + 1]) + 1)
                    product_phase(tp["out", p], N_OUT // 2, hid_hi, hid_lo, kc, T)
                mean_square(T)

        @block.vector
        def _(dve):
            chain = [0]

            def link(ins):
                chain[0] += 1
                ins.then_inc(dve_chain, 1)
                dve.wait_ge(dve_chain, chain[0])

            def split_lo(g, u):
                dve.wait_ge(w_hi_done, 2 * g + (u + 3))
                dve.tensor_tensor(w_lo[:, u].rearrange("p c n -> p (c n)"), raw[:, u],
                                  w_hi[:, u].rearrange("p c n -> p (c n)").bitcast(F32), ALU.subtract)\
                   .then_inc(w_lo_done, 1)

            def ada_pair(q, l, ql):
                dve.wait_ge(ada_copied, q + 1)
                for u in range(2):
                    dve.wait_ge(ada_ld[u], 16 * q + 16)
                    for v in range(2):
                        dve.wait_ge(ada_done, 4 * q + (2 * u + v + 1))
                        dve.tensor_tensor_reduce(ps[3][:], ada_w[:, u], c_b[:, v], 1.0, 0.0, ALU.mult, ALU.add,
                                                 ada_t[:, u, v:v + 1]).then_inc(ada_done, 1)
                dve.wait_ge(ada_done, 4 * q + 5)
                dst = ada_c[l][:].rearrange("p n v -> p (n v)")[:, bass.ds(4 * ql, 4)]
                dve.tensor_copy(dst, ada_t[:].rearrange("p u v -> p (u v)")).then_inc(ada_copied, 1)

            def lo_phase(g0, n, ada=None, add=False, T=TOK, last=False):
                def body(i, split):
                    for u in range(2):
                        if add:
                            dve.wait_ge(blk_done, 2 * i + (2 * g0 + u + 1))
                            dst = f_t[:, 2 * i + u, 0:T]
                            dve.tensor_tensor(dst, dst, ps[u][:, 0:T], ALU.add).then_inc(bank_free[u], 1)
                        if split:
                            split_lo(i + g0, u)
                    if ada:
                        ada_pair(i + ada[0], ada[1], i + ada[2])
                with dve.Fori(0, n - last) as i:
                    body(i, True)
                if last:
                    body(n - 1, False)

            def ffn_in(g0, q0, n, T, ada=None):
                with dve.Fori(0, n) as i:
                    dve.wait_ge(blk_done, 2 * i + (2 * g0 + 2))
                    dve.wait_ge(bank_free[0], i + (g0 + 2))
                    dve.wait_ge(hid_lo_done, i + (q0 + 1))
                    dve.wait_ge(hid_hi_done, i + (q0 + 1))
                    dve.tensor_tensor(tmp[:, 1, 0:T], tmp[:, 0, 0:T], ps[1][:, 0:T], ALU.mult)\
                       .then_inc(bank_free[1], 1)
                    split_lo(i + g0, 0)
                    split_lo(i + g0, 1)
                    dve.wait_ge(hid_hi_done, i + (q0 + 2))
                    dve.tensor_tensor(hid_lo[:, i, 0:T], tmp[:, 1, 0:T], hid_hi[:, i, 0:T].bitcast(F32),
                                      ALU.subtract).then_inc(hid_lo_done, 1)
                    if ada:
                        ada_pair(i + ada[0], ada[1], i + ada[2])

            def cols(l, chunk0, dst):
                b = bada[:, l, chunk0:chunk0 + NC].unsqueeze(2).to_broadcast([P, NC, 2])
                link(dve.tensor_tensor(dst[:], ada_c[l][:, chunk0:chunk0 + NC], b, ALU.add))

            def gain(l, which):
                return gcol[:, l, which].unsqueeze(2).to_broadcast([P, NC, 2])

            nrs, nhi, nlo, nm, nx = [0], [0], [0], [0], [0]

            def pre_norm(l, sh, sc, g, T):
                cols(l, sh, col_sh)
                cols(l, sc, col_sc)
                link(dve.scalar_tensor_tensor(col_gs[:], col_sc[:], 1.0, gain(l, g), ALU.add, ALU.mult))
                nrs[0] += 1
                dve.wait_ge(rstd_ready, nrs[0])
                st = STREAMS[:2 if T == TOK else 1]
                for c in range(NC + 1):
                    if c >= 2:
                        dve.wait_ge(hlo_ready, nlo[0])
                    if c < NC:
                        for lo, hi, v in st:
                            dve.scalar_tensor_tensor(tmp[:, c % 2, lo:hi], x[:, c, lo:hi], col_gs[:, c, v:v + 1],
                                                     rstd[:, lo:hi], ALU.mult, ALU.mult).then_inc(scaled, 1)
                    if c:
                        for lo, hi, v in st:
                            nhi[0] += 1
                            nlo[0] += 1
                            dve.wait_ge(hhi_ready, nhi[0])
                            dve.scalar_tensor_tensor(h_lo[:, c - 1, lo:hi], tmp[:, (c - 1) % 2, lo:hi],
                                                     col_sh[:, c - 1, v:v + 1], h_hi[:, c - 1, lo:hi].bitcast(F32),
                                                     ALU.add, ALU.subtract).then_inc(hlo_ready, 1)
                dve.wait_ge(hlo_ready, nlo[0])

            def post_norm(l, gt, g, T):
                cols(l, gt, col_gg)
                link(dve.tensor_tensor(col_gg[:], col_gg[:], gain(l, g), ALU.mult))
                nrs[0] += 1
                dve.wait_ge(rstd_ready, nrs[0])
                st = STREAMS[:2 if T == TOK else 1]
                for c in range(NC + 1):
                    if c < NC:
                        for lo, hi, v in st:
                            dve.scalar_tensor_tensor(f_t[:, c, lo:hi], f_t[:, c, lo:hi], col_gg[:, c, v:v + 1],
                                                     rstd[:, lo:hi], ALU.mult, ALU.mult).then_inc(pn_m, 1)
                    if c:
                        dve.wait_ge(pn_m, nm[0] + c * len(st))
                        dve.tensor_tensor(x[:, c - 1, 0:T], x[:, c - 1, 0:T], f_t[:, c - 1, 0:T], ALU.add)\
                           .then_inc(x_upd, 1)
                nm[0] += NC * len(st)
                nx[0] += NC
                dve.wait_ge(x_upd, nx[0])

            def attention(kind, l):
                tiles = attention_plan(kind, l)
                u0, t0, m0 = unit0[kind, l], tile0[kind, l], misc0[kind, l]
                uses = misc_uses(kind, tiles)
                U = 4 * len(tiles)
                L = 384 if kind == "swa" else 256
                f0 = 0 if kind == "na" else 4

                def band_bias(cb):
                    if cb >= 2:
                        dve.wait_ge(at_n, u0 + 4 * (cb - 1))
                    dve.wait_ge(na_ld[cb % 2], 16 * ROWS * (2 * l + cb // 2 + 1))
                    for h in range(4):
                        v = na_b[:, cb % 2, h, 0:256].rearrange("p (r c) -> p r c", c=BAND)
                        m = na_m[:, cb].unsqueeze(1).to_broadcast([P, ROWS, BAND])
                        r = na_r[:, cb % 2].rearrange("p (r h c) -> p r h c", r=ROWS, h=4)[:, :, h]
                        ins = dve.scalar_tensor_tensor(v, r, 1.0 / SCALE, m, ALU.mult, ALU.add)
                    ins.then_inc(na_bias, 1)
                    dve.wait_ge(na_bias, 4 * l + cb + 1)

                def score_max(s):
                    t, h = s // 4, s % 4
                    lat, i = tiles[t]
                    n = L * lat + 256
                    dve.wait_ge(at_s, u0 + s + 1)
                    if u0 + s >= 2:
                        dve.wait_ge(at_p, u0 + s - 1)
                    if u0 + s >= 2:
                        dve.wait_ge(at_n, u0 + s - 1)
                    if kind == "na":
                        bias = na_b[:, i % 2, h, :] if lat else na_b[:, 0, h, 256:512]
                    else:
                        bias = sw_m[:, (0, 1, 1, 2)[i], :] if lat else sw_m[:, 0, 384:640]
                    link(dve.tensor_tensor_reduce(s_sb[:, s % 2, 0:n], ps[s % 2][:, 768 - n:768], bias, 1.0, -3e38,
                                                  ALU.add, ALU.max, mx[:, s % 2:s % 2 + 1]))
                    if kind == "na":
                        dve.tensor_scalar(nb[:, h:h + 1], mx[:, s % 2:s % 2 + 1], -SCALE, None, ALU.mult)\
                           .then_inc(at_n, 1)
                    else:
                        link(dve.tensor_scalar(nb[:, h:h + 1], mx[:, s % 2:s % 2 + 1], sink8[:, l, h:h + 1],
                                               -SCALE, ALU.max, ALU.mult))
                        dve.tensor_tensor(sinke[:, t % 2, h:h + 1], nb[:, h:h + 1], sinks[:, l, h:h + 1], ALU.add)\
                           .then_inc(at_n, 1)

                def tile_end(t):
                    dve.wait_ge(at_pv, u0 + 4 * t + 4)
                    if t0 + t > 0:
                        dve.wait_ge(at_o, t0 + t)
                    if kind == "swa":
                        dve.wait_ge(at_sk, t0_swa[l] + t + 1)
                        link(dve.tensor_tensor(sums[:, t % 2], sums[:, t % 2], sinke[:, t % 2], ALU.add))
                    link(dve.reciprocal(rinv[:], sums[:, t % 2]))
                    dve.tensor_tensor(o_sb[:, t % 2].rearrange("p (h d) -> p h d", d=HD),
                                      ps_o[:, 0:256].rearrange("p (h d) -> p h d", d=HD),
                                      rinv[:].unsqueeze(2).to_broadcast([P, 4, HD]), ALU.mult).then_inc(at_o, 1)

                def out_copy(t):
                    lat, i = tiles[t]
                    dve.wait_ge(ms_w, m0 + uses["o", t] + 1)
                    for p in range(2):
                        src, dst = ps_m[:, P * p:P * p + P], f_t[:, f0 + p, :]
                        if kind == "na" and lat:
                            dst = dst[:, 0:LAT].rearrange("p (r c) -> p r c", c=GRID_W)[:, :, 16 * i:16 * i + 16]
                            dst = backwards(dst)
                            src = src.rearrange("p (r c) -> p r c", c=16)
                        else:
                            o = P * i if lat else LAT + P * i
                            dst = dst[:, o:o + P]
                        ins = dve.tensor_copy(dst, src)
                    ins.then_inc(ms_r, 1)
                    return ins

                if kind == "na":
                    dve.wait_ge(mix_done, MIXERS * l + 1)
                    for h in range(4):
                        for b in range(2):
                            dve.memset(na_b[:, b, h, 256:512], 0.0)
                    dve.wait_ge(ms_w, m0 + 1)
                    dve.tensor_copy(na_vc[:].rearrange("p j d -> p (j d)"), ps_m).then_inc(ms_r, 1)
                    dve.wait_ge(at_ld, 64 * l + 16)
                else:
                    dve.wait_ge(at_pre, l + 1)
                    dve.tensor_copy(sw_v[:].rearrange("p j d -> p (j d)"), ps[2][:, 0:TOK]).then_inc(at_pre_c, 1)
                    dve.wait_ge(at_ld, 64 * l + 64)
                    for n, blk in enumerate((KS, QS, QS + 1)):
                        dve.wait_ge(rope_p, 3 * l + n + 1)
                        if 3 * l + n:
                            dve.wait_ge(rope_d, 3 * l + n)
                        dve.tensor_tensor(sw_t[:, 0], ps[n % 2][:, 0:LAT], sw_cs[:, 1], ALU.mult)
                        link(dve.tensor_tensor(sw_t[:, 1], u_t[:, blk, 0:LAT], sw_cs[:, 0], ALU.mult))
                        dve.tensor_tensor(u_t[:, blk, 0:LAT], sw_t[:, 0], sw_t[:, 1], ALU.add).then_inc(rope_d, 1)
                for s in range(U + 2):
                    if kind == "na" and s % 4 == 0 and s // 4 < 4:
                        dve.wait_ge(ms_w, m0 + uses["v", s // 4] + 1)
                        dve.tensor_copy(na_v[:, s // 4 % 2].rearrange("p j d -> p (j d)"), ps_m).then_inc(ms_r, 1)
                        band_bias(s // 4)
                    if s < U:
                        score_max(s)
                    if s >= 2 and (s - 2) % 4 == 3:
                        tile_end((s - 2) // 4)
                    if s >= 7 and s % 4 == 3:
                        out_copy(s // 4 - 1)
                out_copy(len(tiles) - 1)
                dve.wait_ge(ms_r, m0 + len(uses))
                dve.sem_inc(mix_done, 1)

            def hgrn(l):
                T = width[l]
                nch = T // P
                dve.wait_ge(mix_done, MIXERS * l + 3)
                dve.wait_ge(hg_ld, 16 * (l + 1))
                link(dve.tensor_copy(hmask[:], hmask_f[:]))
                for p in range(2):
                    n = 2 * l + p
                    dve.wait_ge(hg_gate, n + 1)
                    for d in range(2):
                        f = u_t[:, (FF, FB)[d] + p, :]
                        if l:
                            dve.tensor_scalar(hk[:, d], hk[:, d], lb1[:, d, p:p + 1], None, ALU.mult)
                            link(dve.tensor_scalar(f, f, lb1[:, d, p:p + 1], lb[:, d, p:p + 1], ALU.mult, ALU.add))
                        dve.tensor_tensor(hq[:, d, 0:T], u_t[:, QD + p, 0:T], f[:, 0:T], ALU.mult)\
                           .then_inc(hg_init, 1)
                    dve.wait_ge(hg_v, n + 1)
                    dve.tensor_copy(hv[:].rearrange("p c d -> p (c d)"), ps[2][:, 0:TOK]).then_inc(hg_vc, 1)
                    na = 30 * n
                    for h in range(2):
                        dve.wait_ge(hg_a, na + h + 1)
                        dve.tensor_tensor(hatt[:, h, 0:T].rearrange("p (c t) -> p c t", t=P),
                                          ps[h][:, 0:T].rearrange("p (c t) -> p c t", t=P),
                                          ident.unsqueeze(1).to_broadcast([P, nch, P]), ALU.mult).then_inc(hg_m, 1)
                    tot = [u_t[:, FF + p, :], u_t[:, FB + p, :]]
                    off = 0
                    for i in range(LEVELS):
                        m = 1 << i
                        nbk = TOK // (2 * m)
                        for d in range(2):
                            for h in range(2):
                                k = na + 2 + 2 * (2 * i + d) + h
                                dve.wait_ge(hg_a, k + 1)
                                dve.wait_ge(hg_m, k)
                                dve.copy_predicated(hatt[:, h, 0:T].rearrange("p (c t) -> p c t", t=P),
                                                    hmask[:, LEVELS * d + i].unsqueeze(1).to_broadcast([P, nch, P]),
                                                    ps[h][:, 0:T].rearrange("p (c t) -> p c t", t=P))\
                                   .then_inc(hg_m, 1)
                            a = tot[d].rearrange("p (n two) -> p n two", two=2)
                            kv = hk[:, d].rearrange("p (n two m) -> p n two m", two=2, m=m)
                            qv = hq[:, d].rearrange("p (n two m) -> p n two m", two=2, m=m)
                            nq = T // (2 * m)
                            qs, ks = (1, 0) if d == 0 else (0, 1)
                            dve.tensor_tensor(qv[:, 0:nq, qs], qv[:, 0:nq, qs],
                                              a[:, 0:nq, 1 - qs].unsqueeze(2).to_broadcast([P, nq, m]), ALU.mult)
                            dve.tensor_tensor(kv[:, :, ks], kv[:, :, ks],
                                              a[:, :, 1 - ks].unsqueeze(2).to_broadcast([P, nbk, m]), ALU.mult)
                            nxt = ha[:, d, off:off + nbk]
                            dve.tensor_tensor(nxt, a[:, :, 0], a[:, :, 1], ALU.mult).then_inc(hg_u, 1)
                            dve.wait_ge(hg_u, 14 * n + 2 * i + d + 1)
                            tot[d] = nxt
                        off += nbk
                    for d in range(2):
                        dve.wait_ge(hg_ds, 2 * n + d + 1)
                        for j, c in enumerate(ORDER[d][:5]):
                            ds = ps[2][:, P * j:P * j + P]
                            if j == 0:
                                link(dve.tensor_copy(hst[:, d, 1], ds))
                            else:
                                link(dve.scalar_tensor_tensor(hst[:, d, j + 1], hst[:, d, j], tot[d][:, c:c + 1], ds,
                                                              ALU.mult, ALU.add))
                        dve.tensor_tensor(hst[:, d, 1:6], hst[:, d, 1:6],
                                          blockones.unsqueeze(1).to_broadcast([P, 5, P]), ALU.mult)\
                           .then_inc(hg_st, 1)
                    dve.wait_ge(hg_rs, n + 1)
                    link(dve.scalar_tensor_tensor(ho[:, 0:T], ps[3][:, 0:T], hgain[:, l, p:p + 1], hkt[:, 1, 0:T],
                                                  ALU.mult, ALU.mult))
                    link(dve.tensor_tensor(f_t[:, 6 + p, 0:T], ho[:, 0:T], u_t[:, GD + p, 0:T], ALU.mult))
                    dve.sem_inc(hg_end, 1)
                dve.sem_inc(mix_done, 1)

            dve.memset(eps_c[:], EPS)
            for count in (hid_hi_done, hid_lo_done, ada_done, ada_copied):
                dve.sem_inc(count, 1)
            dve.wait_ge(s_in, 16 * 7)
            dve.tensor_scalar(sink8[:], sinks[:], 1.0 / SCALE, None, ALU.mult)
            link(dve.tensor_tensor(lb[:], lbc[:, :, 0], lbc[:, :, 1], ALU.max))
            for j in range(2):
                ins = dve.tensor_tensor(lbt[:, j], lbc[:, :, j], lb[:], ALU.subtract)
            ins.then_inc(consts_done, 1)
            dve.wait_ge(consts_done, 2)
            link(dve.tensor_tensor(lb1[:], lbt[:, 0], lbt[:, 1], ALU.add))
            link(dve.reciprocal(lb1[:], lb1[:]))
            link(dve.tensor_tensor(lb[:], lbt[:, 1], lb1[:], ALU.mult))
            link(dve.tensor_tensor(lb1[:], lbt[:, 0], lb1[:], ALU.mult))
            for u in range(2):
                dve.wait_ge(w_hi_done, u + 1)
                dve.tensor_tensor(w_lo[:, u].rearrange("p c n -> p (c n)"), raw[:, u],
                                  w_hi[:, u].rearrange("p c n -> p (c n)").bitcast(F32), ALU.subtract)\
                   .then_inc(w_lo_done, 1)
            dve.wait_ge(s_cb, 1)
            with dve.Fori(0, 9) as q:
                ada_pair(q, 0, q)

            for l in range(DEPTH):
                tp, T = TP[l], width[l]
                dve.wait_ge(ada_copied, 10 if l == 0 else 49)
                pre_norm(l, SH1, SC1, G_PRE_MIX, TOK)
                lo_phase(tp["proj"], N_PROJ // 2, ada=(9, 0, 9) if l == 0 else None)
                for u in range(2):
                    dve.wait_ge(bank_free[u], tp["wout"] + 1)
                for b in range(2):
                    dve.wait_ge(fn_t, 2 * l + b + 1)
                    dve.tensor_copy(fn_f[:, b, 0:T], ps[b][:, 0:T]).then_inc(fn_te, 1)
                for n in range(2):
                    dve.wait_ge(fn_o, 2 * l + n + 1)
                    ins = dve.tensor_copy(f_t[:, 2 + n, 0:T], ps[2 + n][:, 0:T])
                ins.then_inc(mix_done, 1)
                attention("na", l)
                attention("swa", l)
                hgrn(l)
                for c in range(NC):
                    nhi[0] += 1
                    nlo[0] += 1
                    dve.wait_ge(hhi_ready, nhi[0])
                    dve.tensor_tensor(h_lo[:, c, 0:T], f_t[:, c, 0:T], h_hi[:, c, 0:T].bitcast(F32),
                                      ALU.subtract).then_inc(hlo_ready, 1)
                lo_phase(tp["wout"], N_OUT // 2, ada=(20, 0, 20) if l == 0 else None)
                if l == 0:
                    dve.wait_ge(ada_copied, 25)
                post_norm(l, GT1, G_POST_MIX, T)
                pre_norm(l, SH2, SC2, G_PRE_FFN, T)
                for p, kc in enumerate(FFN_CHUNKS):
                    a = (24 + 12 * p, 1, 12 * p) if l == 0 and p < 2 else None
                    ffn_in(tp["in", p], l * 22 + sum(FFN_CHUNKS[:p]), kc, T, a)
                    a = (32 + 12 * p, 1, 12 * p + 8) if l == 0 and p < 2 else None
                    lo_phase(tp["out", p], N_OUT // 2, ada=a, add=p > 0, T=T,
                             last=l == DEPTH - 1 and p == len(FFN_CHUNKS) - 1)
                post_norm(l, GT2, G_POST_FFN, T)


ORDER = ((4, 5, 0, 1, 2, 3), (5, 4, 3, 2, 1, 0))


def _tile(w):
    t = np.zeros((P, NC, P), w.dtype)
    t[:, :w.shape[0] // P] = w.reshape(-1, P, P).transpose(1, 0, 2)
    return t.reshape(P, NC * P)


def _weight_stream(w_in, w_out, w_ffn_in, w_ffn_out):
    tiles = []
    swa = np.r_[0:64, 128:192, 64:128, 192:256] + 8 * P
    cols = [range(P * b, P * b + P) for b in (2, 3, 4, 5, 10, 11, 14, 15, 16, 17, 18, 19, 0, 1, 6, 7)]
    cols += [swa[:P], swa[P:]] + [range(P * b, P * b + P) for b in (12, 13, 20, 21)]
    for l in range(DEPTH):
        tiles += [_tile(w_in[l][:, np.asarray(c)]) for c in cols]
        tiles += [_tile(w_out[l][:, P * o:P * o + P]) for o in range(NC)]
        j = 0
        for kc in FFN_CHUNKS:
            for c in range(j, j + kc):
                tiles += [_tile(w_ffn_in[l][:, h * DFF + P * c:h * DFF + P * c + P]) for h in range(2)]
            tiles += [_tile(w_ffn_out[l][P * j:P * (j + kc), P * o:P * o + P]) for o in range(NC)]
            j += kc
    return np.stack(tiles)


def _tables():
    f = np.float32
    tok, ch = np.arange(LAT), np.arange(HD)

    def dft(n):
        a = 2 * np.pi * (np.outer(np.arange(n), np.arange(n)) % n) / n
        t = np.stack([np.cos(a), -np.sin(a)], 1) / np.sqrt(n * HD)
        return t.reshape(n // P, P, 2, n).transpose(1, 0, 2, 3).astype(f)

    a = 2 * np.pi * (np.outer(ch, ch) % HD) / HD
    dftd = np.concatenate([np.kron(np.eye(2), np.cos(a)), np.kron(np.eye(2), np.sin(a))], 1).astype(f)
    d = np.arange(P)
    rot = np.zeros((P, P), f)
    first = d % 32 < 16
    rot[d[first] + 16, d[first]] = -1
    rot[d[~first] - 16, d[~first]] = 1
    freq = 10000.0 ** (-(d % 16) / 16)
    pos = np.where((d % HD < 32)[:, None], tok // GRID_W, tok % GRID_W)
    rope = np.stack([np.cos(pos * freq[:, None]), np.sin(pos * freq[:, None])], 1).astype(f)
    swa = np.zeros((P, 3, 640), f)
    for kind in range(3):
        rel = np.arange(384) - P * kind - d[:, None]
        swa[:, kind, :384] = np.where(np.abs(rel) <= 128, 0, NEG)
    na = np.zeros((P, 4, BAND), f)
    for cb in range(4):
        q = 16 * cb + 15 - d % 16
        first_col = np.clip(q - 8, 0, GRID_W - 16)[:, None]
        key = BAND0[cb] + np.arange(BAND)
        na[:, cb] = np.where((key >= first_col) & (key < first_col + 16), 0, NEG)
    lv = np.zeros((P, 2 * LEVELS, P), f)
    for i in range(LEVELS):
        m = 1 << i
        same = d[:, None] // (2 * m) == d // (2 * m)
        right = d // m % 2 == 1
        lv[:, i] = same & ~right[:, None] & right
        lv[:, LEVELS + i] = same & right[:, None] & ~right
    squares = np.stack([np.ones((P, P)), np.eye(P), np.kron(np.eye(2), np.ones((HD, HD)))]).astype(f)
    return {"dftL": dft(LAT), "dftC": dft(CTX), "dftD": dftd, "rotm": rot, "rope": rope, "swamask": swa,
            "namask": na, "lvmask": lv, "sqc": squares}


def kernel(x, c, ctx, c_ctx, w_ada, b_ada, g_pre_mix, g_post_mix, g_pre_ffn, g_post_ffn, w_in, w_out, na_rpb, w_fnet,
           swa_sink, hgrn_lb_logits, hgrn_norm_g, w_ffn_in, w_ffn_out):
    import concourse.bacc as bacc
    from concourse.bass_utils import run_bass_kernel_spmd

    a = {
        "xT": np.concatenate([np.asarray(x)[0].T, np.asarray(ctx)[0].T], 1),
        "cvec": np.stack([np.asarray(c)[0], np.asarray(c_ctx)]),
        "wstream": _weight_stream(*map(np.asarray, (w_in, w_out, w_ffn_in, w_ffn_out))),
        "adaT": np.asarray(w_ada).transpose(0, 2, 1).reshape(DEPTH * N_ADA, P, D),
        "badaT": np.asarray(b_ada).reshape(DEPTH, N_ADA, P).transpose(2, 0, 1),
        "gT": np.stack([np.asarray(g) for g in (g_pre_mix, g_post_mix, g_pre_ffn, g_post_ffn)], 1)
        .reshape(DEPTH, 4, NC, P).transpose(3, 0, 1, 2),
        "rpb": np.pad(np.asarray(na_rpb).transpose(0, 2, 1, 3), ((0, 0), (0, 0), (0, 0), (RPB_PAD, RPB_W - RPB_PAD - 31))),
        "wf": np.asarray(w_fnet).reshape(DEPTH, 2, P, 2 * P).transpose(0, 2, 1, 3),
        "sink": np.asarray(swa_sink),
        "lbT": np.asarray(hgrn_lb_logits).reshape(2, DEPTH, 2, P).transpose(3, 0, 1, 2),
        "hgT": np.asarray(hgrn_norm_g).reshape(DEPTH, 2, P).transpose(2, 0, 1),
        **_tables(),
    }
    arrays = {f"in_{k}": np.ascontiguousarray(v) for k, v in a.items()}
    nc = bacc.Bacc("TRN2", target_bir_lowering=False, num_devices=1)
    args = {k: nc.dram_tensor(f"in_{k}", arrays[f"in_{k}"].shape, mybir.dt.from_np(arrays[f"in_{k}"].dtype),
                              kind="ExternalInput").ap() for k in a}
    out = nc.dram_tensor("out_xT", (D, LAT), F32, kind="ExternalOutput").ap()
    hybrid_kernel(nc, **args, out=out)
    r = run_bass_kernel_spmd(nc, [arrays], core_ids=[0])
    return np.ascontiguousarray(r.results[0]["out_xT"].T)[None]
```

```python
from contextlib import ExitStack

import numpy as np

import concourse.bass as bass
from concourse import mybir
from concourse.alu_op_type import AluOpType as ALU

ACT = mybir.ActivationFunctionType
AX_X = mybir.AxisListType.X
F32 = mybir.dt.float32
F32R = mybir.dt.float32r
U8 = mybir.dt.uint8

P = 128
D = 1024
NC = D // P
LAT, CTX = 512, 256
TOK = LAT + CTX
DEPTH = 2
DFF = 2816
GRID_W, ROWS = 64, LAT // 64
HD = 64
EPS = 1e-6
NEG = -1e30
SCALE = HD ** -0.5

KA, VA, KS, VS, FF, FB, IV, QA, UB, QS, QD, GD = 0, 2, 4, 5, 6, 8, 10, 12, 14, 16, 18, 20
N_PROJ, N_PROJ_CTX = 22, 12
FFN_CHUNKS = (8, 8, 6)
N_OUT = NC

SH1, SC1, GT1, SH2, SC2, GT2 = (NC * i for i in range(6))
N_ADA = 6 * NC
G_PRE_MIX, G_POST_MIX, G_PRE_FFN, G_POST_FFN = range(4)

RPB_W = 64
RPB_PAD = 16
BAND = 32
BAND0 = (0, 8, 24, 32)

LEVELS = 7

KEYS = 640

STREAMS = ((0, LAT, 0), (LAT, TOK, 1))


def tile_counts(layer):
    g = layer * 49
    at = {"proj": g}
    g += N_PROJ // 2
    at["wout"] = g
    g += N_OUT // 2
    for p, kc in enumerate(FFN_CHUNKS):
        at["in", p] = g
        g += kc
        at["out", p] = g
        g += N_OUT // 2
    at["end"] = g
    return at


N_PAIRS = tile_counts(DEPTH - 1)["end"]


def backwards(ap):
    dims = [list(d) for d in ap.ap]
    step, n = dims[-1]
    return bass.AP(ap.tensor, ap.offset + step * (n - 1), dims[:-1] + [[-step, n]])


def attention_plan(kind, layer):
    return [(True, t) for t in range(4)] + ([(False, t) for t in range(2)] if layer < DEPTH - 1 else [])


def hybrid_kernel(nc, xT, cvec, wstream, adaT, badaT, gT, rpb, wf, sink, lbT, hgT, dftL, dftC, dftD, rotm,
                  rope, swamask, namask, lvmask, sqc, out):
    with ExitStack() as ctx:
        def sem(name):
            return ctx.enter_context(nc.semaphore(name))

        top = [(nc.sbuf_base + 63) // 64 * 64]
        ctx.enter_context(nc.sbuf_tensor("arena", [P, 212_600], U8))

        def region(nbytes):
            top[0] += nbytes
            return top[0] - nbytes

        def at(name, shape, dt, base, off=0):
            return nc.alloc_sbuf_tensor_at(name, shape, dt, offset=base + off)

        CH = TOK * 4
        r_x, r_h, r_big, r_f = region(NC * CH), region(2 * NC * CH), region(N_PROJ * CH), region(NC * CH)
        r_w, r_ada, r_cb = region(3 * 2 * D * 4), region(2 * D * 4), region(2 * D * 4)
        r_sm = region(5700)
        assert top[0] <= nc.sbuf_usable_end

        x = at("x", [P, NC, TOK], F32, r_x)
        h_hi = at("h_hi", [P, NC, TOK], F32R, r_h)
        h_lo = at("h_lo", [P, NC, TOK], F32R, r_h, NC * CH)
        u_t = at("u_t", [P, N_PROJ, TOK], F32, r_big)
        hid_hi = at("hid_hi", [P, 8, TOK], F32R, r_big)
        hid_lo = at("hid_lo", [P, 8, TOK], F32R, r_big, 8 * CH)
        sq = at("sq", [P, 2, TOK], F32, r_big, 16 * CH)
        tmp = at("tmp", [P, 2, TOK], F32, r_big, 18 * CH)
        lnms = at("lnms", [P, TOK], F32, r_big, 20 * CH)
        rstd = at("rstd", [P, TOK], F32, r_big, 21 * CH)
        f_t = at("f_t", [P, NC, TOK], F32, r_f)
        raw = at("raw", [P, 2, D], F32, r_w)
        w_hi = at("w_hi", [P, 2, NC, P], F32R, r_w, 2 * D * 4)
        w_lo = at("w_lo", [P, 2, NC, P], F32R, r_w, 4 * D * 4)
        ada_w = at("ada_w", [P, 2, D], F32, r_ada)
        c_b = at("c_b", [P, 2, D], F32, r_cb)
        small_top = [0]

        def small(name, shape, dt=F32):
            n = int(np.prod(shape[1:])) * (4 if dt == F32 else 1)
            small_top[0] += (n + 31) // 32 * 32
            assert small_top[0] <= 5700
            return at(name, shape, dt, r_sm, small_top[0] - (n + 31) // 32 * 32)

        consts = small("consts", [P, 3, P])
        ones, ident, blockones = consts[:, 0], consts[:, 1], consts[:, 2]
        ada_c = [small(f"ada_c{l}", [P, N_ADA, 2]) for l in range(DEPTH)]
        ada_t = small("ada_t", [P, 2, 2])
        bada = small("bada", [P, DEPTH, N_ADA])
        gcol = small("gcol", [P, DEPTH, 4, NC])
        col_sh = small("col_sh", [P, NC, 2])
        col_sc = small("col_sc", [P, NC, 2])
        col_gs = small("col_gs", [P, NC, 2])
        col_gg = small("col_gg", [P, NC, 2])
        eps_c = small("eps_c", [P, 1])
        sinks = small("sinks", [P, DEPTH, 4])
        sink8 = small("sink8", [P, DEPTH, 4])
        lbc = small("lbc", [P, 2, DEPTH, 2])
        lb = small("lb", [P, 2, 2])
        lb1 = small("lb1", [P, 2, 2])
        lbt = small("lbt", [P, 2, 2, 2])
        hgain = small("hgain", [P, DEPTH, 2])
        mx = small("mx", [P, 2])
        nb = small("nb", [P, 4])
        sums = small("sums", [P, 4])
        rinv = small("rinv", [P, 1])

        fn_l = at("fn_l", [P, 4, 2, LAT], F32, r_f)
        fn_c = at("fn_c", [P, 2, 2, CTX], F32, r_f, 16384)
        fn_d = at("fn_d", [P, 2 * P], F32, r_f, 20480)
        fn_w = at("fn_w", [P, 2, 2 * P], F32, r_f, 21504)
        fn_ab = at("fn_ab", [P, 6, 4 * P], F32, r_h)
        fn_f = at("fn_f", [P, 2, TOK], F32, r_h, 12288)

        s_sb = at("s_sb", [P, 4, 656], F32, r_h)
        p_sb = at("p_sb", [P, 3, 656], F32, r_h, 10496)
        pt_sb = at("pt_sb", [P, 2, 640], F32, r_h, 18368)
        na_b = at("na_b", [P, 9, 256], F32, r_h, 23488)
        na_v = at("na_v", [P, 2, 2, 256], F32, r_h, 32704)
        na_vc = at("na_vc", [P, 2, 256], F32, r_h, 36800)
        na_m = at("na_m", [P, 4, BAND], F32, r_h, 38848)
        na_r = at("na_r", [P, 2, 1024], F32, r_h, 39360)
        na_q = at("na_q", [P, 2, 2, P], F32, r_f, 6 * CH)
        na_vs = at("na_vs", [P, 2, 2, 256], F32, r_f, 6 * CH + 2048)
        sw_m = at("sw_m", [P, 3, 640], F32, r_h, 23488)
        sw_v = at("sw_v", [P, 6, P], F32, r_h, 31168)
        sw_cs = at("sw_cs", [P, 2, LAT], F32, r_h, 34240)
        sw_r = at("sw_r", [P, P], F32, r_h, 38336)
        sw_t = at("sw_t", [P, 2, LAT], F32, r_h, 38848)

        hq = at("hq", [P, 2, TOK], F32, r_h)
        hk = at("hk", [P, 2, TOK], F32, r_h, 6144)
        ha = at("ha", [P, 2, TOK], F32, r_h, 12288)
        hatt = at("hatt", [P, 2, TOK], F32, r_h, 18432)
        hv = at("hv", [P, 6, P], F32, r_h, 24576)
        hkt = at("hkt", [P, 2, TOK], F32, r_h, 27648)
        hst = at("hst", [P, 2, 6, P], F32, r_h, 33792)
        ho = at("ho", [P, TOK], F32, r_h, 39936)
        hmask = at("hmask", [P, 2 * LEVELS, P], U8, r_h, 43008)
        hmask_f = at("hmask_f", [P, 2 * LEVELS, P], F32, r_h, 12288)
        hms = at("hms", [P, TOK], F32, r_h, 44800)

        ps = [ctx.enter_context(nc.psum_tensor(f"ps{i}", [P, 1024], F32)) for i in range(4)]
        ps_out = [ps[3][:, 0:512], ps[3][:, 512:1024]]
        ps_v = ps[2][:, 512:1024]

        raw_ld = [sem(f"raw_loaded{u}") for u in range(2)]
        w_hi_done, w_lo_done = sem("w_hi_done"), sem("w_lo_done")
        blk_done = sem("block_product_done")
        bank_free = [sem(f"block_bank_free{u}") for u in range(2)]
        hid_hi_done, hid_lo_done = sem("hid_hi_done"), sem("hid_lo_done")
        ada_ld = [sem(f"ada_loaded{u}") for u in range(2)]
        ada_done, ada_copied = sem("ada_products_done"), sem("ada_copied")
        s_in, s_cin, s_cb = sem("inputs_loaded"), sem("c_loaded"), sem("c_activated")
        s_out = sem("output_stored")
        consts_done = sem("small_consts_done")
        dve_chain, act_chain = sem("dve_chain"), sem("act_chain")
        sq_ready, sq_used = sem("squares_ready"), sem("squares_used")
        rstd_ready = sem("rstd_ready")
        scaled = sem("scaled_ready")
        hhi_ready, hlo_ready = sem("h_hi_ready"), sem("h_lo_ready")
        x_upd, pn_m = sem("x_updated"), sem("post_norm_scaled")
        mix_done = sem("mixer_done")
        fn_ld, fn_a, fn_abe = sem("fnet_loaded"), sem("fnet_channels"), sem("fnet_channels_copied")
        fn_t, fn_te, fn_o = sem("fnet_tokens"), sem("fnet_tokens_copied"), sem("fnet_out")
        at_ld = sem("attention_consts_loaded")
        na_ld = [sem(f"na_bias_loaded{u}") for u in range(2)]
        na_bias, na_st = sem("na_bias_ready"), sem("na_block_staged")
        at_pre, at_pre_c = sem("attention_v_transposed"), sem("attention_v_copied")
        rope_p, rope_d = sem("rope_rotated"), sem("rope_done")
        at_s, at_n, at_p = sem("scores"), sem("score_max"), sem("probs")
        at_t, at_tc, at_pv = sem("probs_transposed"), sem("probs_t_copied"), sem("pv_done")
        at_q, at_o = sem("probs_scaled"), sem("attention_out_copied")
        nv_t, nv_c = sem("na_v_transposed"), sem("na_v_copied")
        hg_ld, hg_gate, hg_init = sem("hgrn_masks_loaded"), sem("hgrn_gates"), sem("hgrn_init")
        hg_v, hg_vc = sem("hgrn_v_transposed"), sem("hgrn_v_copied")
        hg_a, hg_m, hg_u = sem("hgrn_att"), sem("hgrn_att_masked"), sem("hgrn_level_up")
        hg_kt, hg_ktc = sem("hgrn_k_transposed"), sem("hgrn_k_copied")
        hg_ds, hg_st, hg_o = sem("hgrn_ds"), sem("hgrn_states"), sem("hgrn_out")
        hg_sq, hg_ms, hg_rs, hg_end = sem("hgrn_sq"), sem("hgrn_ms"), sem("hgrn_rstd"), sem("hgrn_pair_done")

        block = ctx.enter_context(nc.Block())
        TP = [tile_counts(l) for l in range(DEPTH)]
        full = [l < DEPTH - 1 for l in range(DEPTH)]
        width = [TOK if f else LAT for f in full]
        MIXERS = 4
        phases = [(kind, l) for l in range(DEPTH) for kind in ("na", "swa")]
        unit0, tile0 = {}, {}
        nu = nt = 0
        for ph in phases:
            unit0[ph], tile0[ph] = nu, nt
            tiles = attention_plan(*ph)
            nu, nt = nu + 4 * len(tiles), nt + len(tiles)

        @block.sync
        def _(sp):
            for u in range(2):
                sp.dma_start(raw[:, u], wstream[u]).then_inc(raw_ld[u], 16)
            with sp.Fori(1, N_PAIRS) as g:
                for u in range(2):
                    sp.wait_ge(w_lo_done, 2 * g + (u - 1))
                    sp.dma_start(raw[:, u], wstream[2 * g + u]).then_inc(raw_ld[u], 16)
            sp.wait_ge(x_upd, 2 * DEPTH * NC)
            sp.dma_start(out.rearrange("(c p) t -> p c t", p=P), x[:, :, 0:LAT]).then_inc(s_out, 16)
            sp.wait_ge(s_out, 16)

        @block.gpsimd
        def _(pool):
            def ada_loads(p0, n):
                with pool.Fori(p0, p0 + n) as q:
                    for u in range(2):
                        pool.wait_ge(ada_done, 4 * q + (2 * u - 1))
                        pool.dma_start(ada_w[:, u], adaT[2 * q + u]).then_inc(ada_ld[u], 16)

            for v in range(2):
                pool.dma_start(c_b[:, v], bass.AP(cvec.tensor, v * D, [[0, P], [1, D]])).then_inc(s_cin, 16)
            for u in range(2):
                pool.dma_start(ada_w[:, u], adaT[u]).then_inc(ada_ld[u], 16)
            pool.dma_start(x[:], xT.rearrange("(c p) t -> p c t", p=P)).then_inc(s_in, 16)
            pool.dma_start(consts[:], sqc.rearrange("k p n -> p k n")).then_inc(s_in, 16)
            pool.dma_start(bada[:], badaT).then_inc(s_in, 16)
            pool.dma_start(gcol[:], gT).then_inc(s_in, 16)
            pool.dma_start(sinks[:], bass.AP(sink.tensor, 0, [[0, P], [4, DEPTH], [1, 4]])).then_inc(s_in, 16)
            pool.dma_start(lbc[:], lbT).then_inc(s_in, 16)
            pool.dma_start(hgain[:], hgT).then_inc(s_in, 16)
            ada_loads(1, 8)
            for l in range(DEPTH):
                if l:
                    pool.wait_ge(x_upd, 2 * l * NC)
                pool.dma_start(fn_d[:], dftD).then_inc(fn_ld, 16)
                pool.dma_start(fn_l[:], dftL).then_inc(fn_ld, 16)
                pool.dma_start(fn_c[:], dftC).then_inc(fn_ld, 16)
                pool.dma_start(fn_w[:], wf[l]).then_inc(fn_ld, 16)
                if l == 0:
                    ada_loads(9, 11)
                pool.wait_ge(mix_done, MIXERS * l + 1)
                pool.dma_start(na_m[:], namask).then_inc(at_ld, 16)
                for cb in range(4):
                    if cb >= 2:
                        pool.wait_ge(na_bias, 4 * l + cb - 1)
                    for rq in range(ROWS):
                        off = (l * 15 + 7 - rq) * 4 * RPB_W + BAND0[cb] - 16 * cb + RPB_PAD
                        src = bass.AP(rpb.tensor, off, [[1, 16], [RPB_W, 4 * ROWS], [1, BAND]])
                        dst = na_r[16 * rq:16 * rq + 16, cb % 2].rearrange("p (n c) -> p n c", c=BAND)
                        pool.dma_start(dst, src).then_inc(na_ld[cb % 2], 16)
                    if cb >= 2:
                        pool.wait_ge(at_s, unit0["na", l] + 4 * (cb - 1))
                    for p in range(2):
                        q = u_t[:, QA + p, 0:LAT].rearrange("p (r c) -> p r c", c=GRID_W)
                        v = u_t[:, VA + p, 0:LAT].rearrange("p (r c) -> p r c", c=GRID_W)
                        pool.tensor_copy(na_q[:, cb % 2, p].rearrange("p (r c) -> p r c", c=16),
                                         backwards(q[:, :, 16 * cb:16 * cb + 16]))
                        ins = pool.tensor_copy(na_vs[:, cb % 2, p].rearrange("p (r c) -> p r c", c=BAND),
                                               v[:, :, BAND0[cb]:BAND0[cb] + BAND])
                    ins.then_inc(na_st, 1)
                pool.wait_ge(mix_done, MIXERS * l + 2)
                pool.dma_start(sw_r[:], rotm).then_inc(at_ld, 16)
                pool.dma_start(sw_cs[:], rope).then_inc(at_ld, 16)
                pool.dma_start(sw_m[:], swamask).then_inc(at_ld, 16)
                pool.wait_ge(mix_done, MIXERS * l + 3)
                pool.dma_start(hmask_f[:], lvmask).then_inc(hg_ld, 16)
                if l == 0:
                    ada_loads(20, 4)
                    ada_loads(24, 24)

        @block.scalar
        def _(act):
            chain = [0]

            def link(ins):
                chain[0] += 1
                ins.then_inc(act_chain, 1)
                act.wait_ge(act_chain, chain[0])

            def split_hi(g, u):
                act.wait_ge(raw_ld[u], 16 * g + 32)
                act.wait_ge(blk_done, 2 * g + (u + 1))
                act.activation(w_hi[:, u].rearrange("p c n -> p (c n)"), raw[:, u], ACT.Copy).then_inc(w_hi_done, 1)

            def copy_phase(g0, n, dst, b0, T):
                with act.Fori(0, n) as i:
                    for u in range(2):
                        act.wait_ge(blk_done, 2 * i + (2 * g0 + u + 1))
                        act.activation(dst[:, 2 * i + (b0 + u), 0:T], ps[u][:, 0:T], ACT.Copy)\
                           .then_inc(bank_free[u], 1)
                        split_hi(i + g0, u)

            def splits_only(g0, n, last):
                if n - last > 0:
                    with act.Fori(0, n - last) as i:
                        for u in range(2):
                            split_hi(i + g0, u)

            def ffn_in(g0, q0, n, T):
                with act.Fori(0, n) as i:
                    act.wait_ge(blk_done, 2 * i + (2 * g0 + 1))
                    act.wait_ge(bank_free[1], i + (g0 + 1))
                    act.activation(tmp[:, 0, 0:T], ps[0][:, 0:T], ACT.Silu).then_inc(bank_free[0], 1)
                    split_hi(i + g0, 0)
                    split_hi(i + g0, 1)
                    act.wait_ge(bank_free[1], i + (g0 + 2))
                    act.activation(hid_hi[:, i, 0:T], tmp[:, 1, 0:T], ACT.Copy).then_inc(hid_hi_done, 1)

            nsq, nn = [0], [0]

            def mean_square(src, T, ready):
                for c in range(NC):
                    ready(c)
                    if nsq[0] >= 2:
                        act.wait_ge(sq_used, nsq[0] - 1)
                    act.activation(sq[:, c % 2, 0:T], src[:, c, 0:T], ACT.Square).then_inc(sq_ready, 1)
                    nsq[0] += 1
                act.wait_ge(sq_used, nsq[0])
                link(act.activation(lnms[:, 0:T], ps[2][:, 0:T], ACT.Ln, bias=eps_c[:, 0:1], scale=1.0 / D))
                act.activation(rstd[:, 0:T], lnms[:, 0:T], ACT.Exp, scale=-0.5).then_inc(rstd_ready, 1)

            def pre_norm(T, ready):
                mean_square(x, T, ready)
                for c in range(NC):
                    for lo, hi, v in STREAMS[:2 if T == TOK else 1]:
                        act.wait_ge(scaled, nn[0] + 1)
                        nn[0] += 1
                        act.activation(h_hi[:, c, lo:hi], tmp[:, c % 2, lo:hi], ACT.Identity,
                                       bias=col_sh[:, c, v:v + 1]).then_inc(hhi_ready, 1)

            def attention(kind, l):
                tiles = attention_plan(kind, l)
                u0, t0 = unit0[kind, l], tile0[kind, l]
                U = 4 * len(tiles)
                if kind == "swa":
                    act.wait_ge(mix_done, MIXERS * l + 2)
                else:
                    act.wait_ge(mix_done, MIXERS * l + 1)
                for s in range(U + 2):
                    if s < U:
                        n = (384 if kind == "swa" else 256) * tiles[s // 4][0] + 256
                        last = KEYS + (kind == "swa")
                        act.wait_ge(at_n, u0 + s + 1)
                        if u0 + s >= 3:
                            act.wait_ge(at_t, u0 + s - 2)
                        if u0 + s >= 4:
                            act.wait_ge(at_q, u0 + s - 3)
                        act.activation(p_sb[:, s % 3, KEYS - n:last], s_sb[:, s % 4, KEYS - n:last], ACT.Exp,
                                       bias=nb[:, s % 4:s % 4 + 1], scale=SCALE,
                                       accum_out=sums[:, s % 4:s % 4 + 1]).then_inc(at_p, 1)
                    if s >= 2:
                        v = s - 2
                        n = (384 if kind == "swa" else 256) * tiles[v // 4][0] + 256
                        act.wait_ge(at_t, u0 + v + 1)
                        if u0 + v >= 2:
                            act.wait_ge(at_pv, u0 + v - 1)
                        act.activation(pt_sb[:, v % 2, 0:n], ps[2][:, 0:n], ACT.Copy).then_inc(at_tc, 1)

            for u in range(2):
                act.sem_inc(bank_free[u], 1)
            act.wait_ge(s_cin, 32)
            act.activation(c_b[:].rearrange("p v d -> p (v d)"), c_b[:].rearrange("p v d -> p (v d)"),
                           ACT.Silu).then_inc(s_cb, 1)
            for u in range(2):
                act.wait_ge(raw_ld[u], 16)
                act.activation(w_hi[:, u].rearrange("p c n -> p (c n)"), raw[:, u], ACT.Copy).then_inc(w_hi_done, 1)
            act.wait_ge(consts_done, 1)
            act.activation(lbt[:], lbt[:], ACT.Exp).then_inc(consts_done, 1)

            for l in range(DEPTH):
                tp, T = TP[l], width[l]
                if l == 0:
                    act.wait_ge(s_in, 16 * 7)
                    act.wait_ge(consts_done, 2)
                    pre_norm(TOK, lambda c: None)
                    copy_phase(tp["proj"], N_PROJ // 2, u_t, 0, TOK)
                else:
                    pre_norm(TOK, lambda c: act.wait_ge(x_upd, 2 * l * NC - NC + c + 1))
                    copy_phase(tp["proj"], N_PROJ_CTX // 2, u_t, 0, TOK)
                    copy_phase(tp["proj"] + N_PROJ_CTX // 2, (N_PROJ - N_PROJ_CTX) // 2, u_t, N_PROJ_CTX, LAT)
                for j in range(T // P):
                    act.wait_ge(fn_a, sum(width[:l]) // P + j + 1)
                    act.activation(fn_ab[:, j], ps[j % 2][:, 0:512], ACT.Copy).then_inc(fn_abe, 1)
                attention("na", l)
                attention("swa", l)
                act.wait_ge(mix_done, MIXERS * l + 3)
                for p in range(2):
                    n = 2 * l + p
                    if p:
                        act.wait_ge(hg_end, n)
                    for d in range(2):
                        fz = u_t[:, (FF, FB)[d] + p, :]
                        link(act.activation(hk[:, d], fz, ACT.Sigmoid, scale=-1.0))
                        act.activation(fz, fz, ACT.Sigmoid)
                    act.activation(u_t[:, QD + p, 0:T], u_t[:, QD + p, 0:T], ACT.Silu)
                    act.activation(u_t[:, GD + p, 0:T], u_t[:, GD + p, 0:T], ACT.Silu).then_inc(hg_gate, 1)
                    for d in range(2):
                        act.wait_ge(hg_kt, 2 * n + d + 1)
                        act.activation(hkt[:, d], ps[d][:, 0:TOK], ACT.Copy).then_inc(hg_ktc, 1)
                    act.wait_ge(hg_o, n + 1)
                    act.activation(hkt[:, 0, 0:T], ps[3][:, 0:T], ACT.Square).then_inc(hg_sq, 1)
                    act.wait_ge(hg_ms, n + 1)
                    link(act.activation(hms[:, 0:T], ps[2][:, 0:T], ACT.Ln, bias=eps_c[:, 0:1], scale=1.0 / HD))
                    act.activation(hkt[:, 1, 0:T], hms[:, 0:T], ACT.Exp, scale=-0.5).then_inc(hg_rs, 1)
                act.wait_ge(mix_done, MIXERS * l + 4)
                for c in range(NC):
                    act.activation(h_hi[:, c, 0:T], f_t[:, c, 0:T], ACT.Copy).then_inc(hhi_ready, 1)
                copy_phase(tp["wout"], N_OUT // 2, f_t, 0, T)
                act.wait_ge(bank_free[0], tp["wout"] + N_OUT // 2 + 1)
                act.wait_ge(bank_free[1], tp["wout"] + N_OUT // 2 + 1)
                mean_square(f_t, T, lambda c: None)
                pre_norm(T, lambda c: act.wait_ge(x_upd, 2 * l * NC + c + 1))
                for p, kc in enumerate(FFN_CHUNKS):
                    ffn_in(tp["in", p], 0, kc, T)
                    if p == 0:
                        copy_phase(tp["out", p], N_OUT // 2, f_t, 0, T)
                    else:
                        last = l == DEPTH - 1 and p == len(FFN_CHUNKS) - 1
                        splits_only(tp["out", p], N_OUT // 2, last)
                act.wait_ge(bank_free[0], tp["end"] + 1)
                act.wait_ge(bank_free[1], tp["end"] + 1)
                mean_square(f_t, T, lambda c: None)

        @block.tensor
        def _(pe):
            def product_phase(g0, n, rhs_hi, rhs_lo, kc, T):
                with pe.Fori(0, n) as i:
                    for u in range(2):
                        pe.wait_ge(w_lo_done, 2 * i + (2 * g0 + u + 1))
                        pe.wait_ge(bank_free[u], i + (g0 + 1))
                        for k in range(kc):
                            for w, r, first, last in ((w_hi, rhs_hi, k == 0, False), (w_hi, rhs_lo, False, False),
                                                      (w_lo, rhs_hi, False, k == kc - 1)):
                                for lo, hi, _ in STREAMS[:2 if T == TOK else 1]:
                                    mm = pe.matmul(ps[u][:, lo:hi], w[:, u, k], r[:, k, lo:hi],
                                                   start=first, stop=last)
                        mm.then_inc(blk_done, 1)

            nsq = [0]

            def mean_square(T):
                for c in range(NC):
                    pe.wait_ge(sq_ready, nsq[0] + 1)
                    for lo, hi, _ in STREAMS[:2 if T == TOK else 1]:
                        mm = pe.matmul(ps[2][:, lo:hi], ones, sq[:, c % 2, lo:hi], start=c == 0, stop=c == NC - 1)
                    mm.then_inc(sq_used, 1)
                    nsq[0] += 1

            def fourier(l):
                T = width[l]
                pe.wait_ge(fn_ld, 64 * (l + 1))
                done = sum(width[:l]) // P
                for j in range(T // P):
                    if j >= 2:
                        pe.wait_ge(fn_abe, done + j - 1)
                    for b in range(2):
                        mm = pe.matmul(ps[j % 2][:, 256 * b:256 * b + 256], u_t[:, UB + b, P * j:P * j + P],
                                       fn_d[:], start=True, stop=True)
                    mm.then_inc(fn_a, 1)
                pe.wait_ge(fn_abe, done + T // P)
                for b in range(2):
                    for lo, hi, m, tab in ((0, LAT, 4, fn_l), (LAT, TOK, 2, fn_c))[:2 if T == TOK else 1]:
                        for j in range(m):
                            for part in range(2):
                                mm = pe.matmul(ps[b][:, lo:hi],
                                               fn_ab[:, lo // P + j, 256 * b + P * part:256 * b + P * part + P],
                                               tab[:, j, part], start=j + part == 0, stop=j == m - 1 and part == 1)
                    mm.then_inc(fn_t, 1)
                pe.wait_ge(fn_te, 2 * (l + 1))
                for n in range(2):
                    for lo, hi, _ in STREAMS[:2 if T == TOK else 1]:
                        for b in range(2):
                            mm = pe.matmul(ps[2 + n][:, lo:hi], fn_w[:, b, P * n:P * n + P], fn_f[:, b, lo:hi],
                                           start=b == 0, stop=b == 1)
                    mm.then_inc(fn_o, 1)

            def attention(kind, l):
                tiles = attention_plan(kind, l)
                u0, t0 = unit0[kind, l], tile0[kind, l]
                U = 4 * len(tiles)
                L = 384 if kind == "swa" else 256

                def lat_rows(blk, lo, hi, row0, nrow, col0, ncol):
                    v = u_t[lo:hi, blk, 0:LAT].rearrange("p (r c) -> p r c", c=GRID_W)
                    return v[:, row0:row0 + nrow, col0:col0 + ncol]

                def queries(t, h):
                    lat, i = tiles[t]
                    if kind == "na":
                        a = 64 * (h % 2)
                        return (na_q[a:a + 64, i % 2, h // 2] if lat else
                                u_t[a:a + 64, QA + h // 2, LAT + P * i:LAT + P * i + P])
                    a = 64 * (h // 2)
                    o = P * i if lat else LAT + P * i
                    return u_t[a:a + 64, QS + h % 2, o:o + P]

                def scores(s):
                    t, h = s // 4, s % 4
                    lat, i = tiles[t]
                    bank = ps[s % 2]
                    if u0 + s >= 2:
                        pe.wait_ge(at_n, u0 + s - 1)
                    a, kb = (64 * (h % 2), KA + h // 2) if kind == "na" else (64 * (h // 2), KS)
                    if lat:
                        if kind == "na":
                            keys = lat_rows(kb, a, a + 64, 0, ROWS, BAND0[i], BAND)
                            dst = bank[:, 256:512].rearrange("p (r c) -> p r c", c=BAND)
                        else:
                            first = P * min(max(i - 1, 0), 1)
                            keys = u_t[a:a + 64, kb, first:first + L]
                            dst = bank[:, 512 - L:512]
                        pe.matmul(dst, queries(t, h), keys, start=True, stop=True)
                    pe.matmul(bank[:, 512:768], queries(t, h), u_t[a:a + 64, kb, LAT:TOK],
                              start=True, stop=True).then_inc(at_s, 1)

                def transposes(v):
                    n = L * tiles[v // 4][0] + 256
                    pe.wait_ge(at_q, u0 + v + 1)
                    if u0 + v >= 1:
                        pe.wait_ge(at_tc, u0 + v)
                    for j in range(n // P):
                        o = KEYS - n + P * j
                        mm = pe.transpose(ps[2][:, P * j:P * j + P], p_sb[:, v % 3, o:o + P], ident)
                    mm.then_inc(at_t, 1)

                def pv(v):
                    t, h = v // 4, v % 4
                    lat, i = tiles[t]
                    n = L * lat + 256
                    pe.wait_ge(at_tc, u0 + v + 1)
                    if h == 0 and t0 + t >= 2:
                        pe.wait_ge(at_o, t0 + t - 1)
                    if kind == "na" and h == 0:
                        pe.wait_ge(nv_c, 5 * l + (i + 2 if lat else 1))
                    a = 64 * (h % 2)
                    dst = ps_out[(t0 + t) % 2][a:a + 64, P * (h // 2):P * (h // 2) + P]
                    for j in range(n // P):
                        local = j < L // P and lat
                        if kind == "na":
                            val = (na_v[:, i % 2, j] if local else na_vc[:, j - L // P * lat])[:, HD * h:HD * h + HD]
                        else:
                            row = min(max(i - 1, 0), 1) + j if local else 4 + j - L // P * lat
                            val = sw_v[:, row, HD * (h // 2):HD * (h // 2) + HD]
                        mm = pe.matmul(dst, val, pt_sb[:, v % 2, P * j:P * j + P], start=j == 0,
                                       stop=j == n // P - 1, skip_group_check=True)
                    mm.then_inc(at_pv, 1)

                def band_v(i):
                    pe.wait_ge(na_st, 4 * l + i + 1)
                    pe.wait_ge(nv_c, 5 * l + i + 1)
                    for j in range(2):
                        for p in range(2):
                            mm = pe.transpose(ps_v[:, 256 * j + P * p:256 * j + P * p + P],
                                              na_vs[:, i % 2, p, P * j:P * j + P], ident)
                    mm.then_inc(nv_t, 1)

                pe.wait_ge(mix_done, MIXERS * l + (1 if kind == "na" else 2))
                if kind == "na":
                    for j in range(2):
                        for p in range(2):
                            mm = pe.transpose(ps_v[:, 256 * j + P * p:256 * j + P * p + P],
                                              u_t[:, VA + p, LAT + P * j:LAT + P * j + P], ident)
                    mm.then_inc(nv_t, 1)
                else:
                    for j in range(6):
                        mm = pe.transpose(ps[2][:, P * j:P * j + P], u_t[:, VS, P * j:P * j + P], ident)
                    mm.then_inc(at_pre, 1)
                    pe.wait_ge(at_ld, 64 * l + 64)
                    for n, blk in enumerate((KS, QS, QS + 1)):
                        if n >= 2:
                            pe.wait_ge(rope_d, 3 * l + n - 1)
                        pe.matmul(ps[n % 2][:, 0:LAT], sw_r[:], u_t[:, blk, 0:LAT], start=True, stop=True)\
                          .then_inc(rope_p, 1)
                    pe.wait_ge(rope_d, 3 * l + 3)
                    pe.wait_ge(at_pre_c, l + 1)
                for s in range(U + 3):
                    if kind == "na" and s % 4 == 0 and s // 4 < 4:
                        band_v(s // 4)
                    if s < U:
                        scores(s)
                    if 2 <= s < U + 2:
                        transposes(s - 2)
                    if s >= 3:
                        pv(s - 3)

            na = [0]

            def hgrn_att(d, h, q, T, n_acc=1):
                for c in range(T // P):
                    mm = pe.matmul(ps[h][:, P * c:P * c + P], hk[64 * h:64 * h + 64, d, P * c:P * c + P],
                                   q[64 * h:64 * h + 64, P * c:P * c + P], start=True, stop=True)
                return mm

            def hgrn(l):
                T = width[l]
                pe.wait_ge(mix_done, MIXERS * l + 3)
                for p in range(2):
                    n = 2 * l + p
                    m0 = 30 * n
                    if p:
                        pe.wait_ge(hg_end, n)
                    for c in range(6):
                        mm = pe.transpose(ps[2][:, P * c:P * c + P], u_t[:, IV + p, P * c:P * c + P], ident)
                    mm.then_inc(hg_v, 1)
                    pe.wait_ge(hg_init, 3 * n + 3)
                    for h in range(2):
                        for c in range(T // P):
                            mm = pe.matmul(ps[h][:, P * c:P * c + P], ho[64 * h:64 * h + 64, P * c:P * c + P],
                                           u_t[64 * h:64 * h + 64, QD + p, P * c:P * c + P], start=True, stop=True)
                        mm.then_inc(hg_a, 1)
                    for i in range(LEVELS):
                        for d in range(2):
                            if i:
                                pe.wait_ge(hg_u, 14 * n + 2 * (i - 1) + d + 1)
                            for h in range(2):
                                pe.wait_ge(hg_m, m0 + 2 * (2 * i + d) + h + 1)
                                hgrn_att(d, h, hq[:, d], T).then_inc(hg_a, 1)
                    for d in range(2):
                        pe.wait_ge(hg_u, 14 * n + 12 + d + 1)
                        pe.wait_ge(hg_m, m0 + 30)
                        for c in range(6):
                            mm = pe.transpose(ps[d][:, P * c:P * c + P], hk[:, d, P * c:P * c + P], ident)
                        mm.then_inc(hg_kt, 1)
                    pe.wait_ge(hg_vc, n + 1)
                    for d in range(2):
                        pe.wait_ge(hg_ktc, 2 * n + d + 1)
                        if d:
                            pe.wait_ge(hg_st, 2 * n + 1)
                        for j, c in enumerate(ORDER[d][:5]):
                            mm = pe.matmul(ps[2][:, P * j:P * j + P], hkt[:, d, P * c:P * c + P], hv[:, c],
                                           start=True, stop=True)
                        mm.then_inc(hg_ds, 1)
                    pe.wait_ge(hg_st, 2 * n + 2)
                    for c in range(T // P):
                        o = ps[3][:, P * c:P * c + P]
                        terms = [d for d in range(2) if ORDER[d].index(c) > 0]
                        for h in range(2):
                            pe.matmul(o[64 * h:64 * h + 64], hv[:, c, 64 * h:64 * h + 64],
                                      hatt[:, h, P * c:P * c + P], start=True, stop=False, skip_group_check=True)
                        for d in terms:
                            mm = pe.matmul(o, hst[:, d, ORDER[d].index(c)], hq[:, d, P * c:P * c + P], start=False,
                                           stop=d == terms[-1], skip_group_check=True)
                    mm.then_inc(hg_o, 1)
                    pe.wait_ge(hg_sq, n + 1)
                    for lo, hi, _ in STREAMS[:2 if T == TOK else 1]:
                        mm = pe.matmul(ps[2][:, lo:hi], blockones, hkt[:, 0, lo:hi], start=True, stop=True)
                    mm.then_inc(hg_ms, 1)

            hh = [0]
            for l in range(DEPTH):
                tp, T = TP[l], width[l]
                if l == 0:
                    pe.wait_ge(s_in, 16 * 7)
                mean_square(TOK)
                hh[0] += 2 * NC
                pe.wait_ge(hlo_ready, hh[0])
                if full[l]:
                    product_phase(tp["proj"], N_PROJ // 2, h_hi, h_lo, NC, TOK)
                else:
                    product_phase(tp["proj"], N_PROJ_CTX // 2, h_hi, h_lo, NC, TOK)
                    product_phase(tp["proj"] + N_PROJ_CTX // 2, (N_PROJ - N_PROJ_CTX) // 2, h_hi, h_lo, NC, LAT)
                for u in range(2):
                    pe.wait_ge(bank_free[u], tp["wout"] + 1)
                fourier(l)
                attention("na", l)
                attention("swa", l)
                hgrn(l)
                hh[0] += NC
                pe.wait_ge(hlo_ready, hh[0])
                product_phase(tp["wout"], N_OUT // 2, h_hi, h_lo, NC, T)
                mean_square(T)
                mean_square(T)
                hh[0] += NC * (2 if full[l] else 1)
                pe.wait_ge(hlo_ready, hh[0])
                for p, kc in enumerate(FFN_CHUNKS):
                    product_phase(tp["in", p], kc, h_hi, h_lo, NC, T)
                    pe.wait_ge(hid_lo_done, l * 22 + sum(FFN_CHUNKS[:p + 1]) + 1)
                    product_phase(tp["out", p], N_OUT // 2, hid_hi, hid_lo, kc, T)
                mean_square(T)

        @block.vector
        def _(dve):
            chain = [0]

            def link(ins):
                chain[0] += 1
                ins.then_inc(dve_chain, 1)
                dve.wait_ge(dve_chain, chain[0])

            def split_lo(g, u):
                dve.wait_ge(w_hi_done, 2 * g + (u + 3))
                dve.tensor_tensor(w_lo[:, u].rearrange("p c n -> p (c n)"), raw[:, u],
                                  w_hi[:, u].rearrange("p c n -> p (c n)").bitcast(F32), ALU.subtract)\
                   .then_inc(w_lo_done, 1)

            def ada_pair(q, l, ql):
                dve.wait_ge(ada_copied, q + 1)
                for u in range(2):
                    dve.wait_ge(ada_ld[u], 16 * q + 16)
                    for v in range(2):
                        dve.wait_ge(ada_done, 4 * q + (2 * u + v + 1))
                        dve.tensor_tensor_reduce(ps[3][:], ada_w[:, u], c_b[:, v], 1.0, 0.0, ALU.mult, ALU.add,
                                                 ada_t[:, u, v:v + 1]).then_inc(ada_done, 1)
                dve.wait_ge(ada_done, 4 * q + 5)
                dst = ada_c[l][:].rearrange("p n v -> p (n v)")[:, bass.ds(4 * ql, 4)]
                dve.tensor_copy(dst, ada_t[:].rearrange("p u v -> p (u v)")).then_inc(ada_copied, 1)

            def lo_phase(g0, n, ada=None, add=False, T=TOK, last=False):
                def body(i, split):
                    for u in range(2):
                        if add:
                            dve.wait_ge(blk_done, 2 * i + (2 * g0 + u + 1))
                            dst = f_t[:, 2 * i + u, 0:T]
                            dve.tensor_tensor(dst, dst, ps[u][:, 0:T], ALU.add).then_inc(bank_free[u], 1)
                        if split:
                            split_lo(i + g0, u)
                    if ada:
                        ada_pair(i + ada[0], ada[1], i + ada[2])
                with dve.Fori(0, n - last) as i:
                    body(i, True)
                if last:
                    body(n - 1, False)

            def ffn_in(g0, q0, n, T, ada=None):
                with dve.Fori(0, n) as i:
                    split_lo(i + g0, 0)
                    dve.wait_ge(blk_done, 2 * i + (2 * g0 + 2))
                    dve.wait_ge(bank_free[0], i + (g0 + 2))
                    dve.wait_ge(hid_lo_done, i + (q0 + 1))
                    dve.wait_ge(hid_hi_done, i + (q0 + 1))
                    dve.tensor_tensor(tmp[:, 1, 0:T], tmp[:, 0, 0:T], ps[1][:, 0:T], ALU.mult)\
                       .then_inc(bank_free[1], 1)
                    split_lo(i + g0, 1)
                    dve.wait_ge(hid_hi_done, i + (q0 + 2))
                    dve.tensor_tensor(hid_lo[:, i, 0:T], tmp[:, 1, 0:T], hid_hi[:, i, 0:T].bitcast(F32),
                                      ALU.subtract).then_inc(hid_lo_done, 1)
                    if ada:
                        ada_pair(i + ada[0], ada[1], i + ada[2])

            def cols(l, chunk0, dst):
                b = bada[:, l, chunk0:chunk0 + NC].unsqueeze(2).to_broadcast([P, NC, 2])
                link(dve.tensor_tensor(dst[:], ada_c[l][:, chunk0:chunk0 + NC], b, ALU.add))

            def gain(l, which):
                return gcol[:, l, which].unsqueeze(2).to_broadcast([P, NC, 2])

            nrs, nhi, nlo, nm, nx = [0], [0], [0], [0], [0]

            def pre_norm(l, sh, sc, g, T):
                cols(l, sh, col_sh)
                cols(l, sc, col_sc)
                link(dve.scalar_tensor_tensor(col_gs[:], col_sc[:], 1.0, gain(l, g), ALU.add, ALU.mult))
                nrs[0] += 1
                dve.wait_ge(rstd_ready, nrs[0])
                st = STREAMS[:2 if T == TOK else 1]
                for c in range(NC + 1):
                    if c >= 2:
                        dve.wait_ge(hlo_ready, nlo[0])
                    if c < NC:
                        for lo, hi, v in st:
                            dve.scalar_tensor_tensor(tmp[:, c % 2, lo:hi], x[:, c, lo:hi], col_gs[:, c, v:v + 1],
                                                     rstd[:, lo:hi], ALU.mult, ALU.mult).then_inc(scaled, 1)
                    if c:
                        for lo, hi, v in st:
                            nhi[0] += 1
                            nlo[0] += 1
                            dve.wait_ge(hhi_ready, nhi[0])
                            dve.scalar_tensor_tensor(h_lo[:, c - 1, lo:hi], tmp[:, (c - 1) % 2, lo:hi],
                                                     col_sh[:, c - 1, v:v + 1], h_hi[:, c - 1, lo:hi].bitcast(F32),
                                                     ALU.add, ALU.subtract).then_inc(hlo_ready, 1)
                dve.wait_ge(hlo_ready, nlo[0])

            def post_norm(l, gt, g, T):
                cols(l, gt, col_gg)
                link(dve.tensor_tensor(col_gg[:], col_gg[:], gain(l, g), ALU.mult))
                nrs[0] += 1
                dve.wait_ge(rstd_ready, nrs[0])
                st = STREAMS[:2 if T == TOK else 1]
                for c in range(NC + 1):
                    if c < NC:
                        for lo, hi, v in st:
                            dve.scalar_tensor_tensor(f_t[:, c, lo:hi], f_t[:, c, lo:hi], col_gg[:, c, v:v + 1],
                                                     rstd[:, lo:hi], ALU.mult, ALU.mult).then_inc(pn_m, 1)
                    if c:
                        dve.wait_ge(pn_m, nm[0] + c * len(st))
                        dve.tensor_tensor(x[:, c - 1, 0:T], x[:, c - 1, 0:T], f_t[:, c - 1, 0:T], ALU.add)\
                           .then_inc(x_upd, 1)
                nm[0] += NC * len(st)
                nx[0] += NC
                dve.wait_ge(x_upd, nx[0])

            def attention(kind, l):
                tiles = attention_plan(kind, l)
                u0, t0 = unit0[kind, l], tile0[kind, l]
                U = 4 * len(tiles)
                L = 384 if kind == "swa" else 256
                f0 = 0 if kind == "na" else 4

                def band_bias(cb):
                    if cb >= 2:
                        dve.wait_ge(at_n, u0 + 4 * (cb - 1))
                    dve.wait_ge(na_ld[cb % 2], 16 * ROWS * (2 * l + cb // 2 + 1))
                    for h in range(4):
                        v = na_b[:, 4 * (cb % 2) + h].rearrange("p (r c) -> p r c", c=BAND)
                        m = na_m[:, cb].unsqueeze(1).to_broadcast([P, ROWS, BAND])
                        r = na_r[:, cb % 2].rearrange("p (r h c) -> p r h c", r=ROWS, h=4)[:, :, h]
                        ins = dve.scalar_tensor_tensor(v, r, 1.0 / SCALE, m, ALU.mult, ALU.add)
                    ins.then_inc(na_bias, 1)
                    dve.wait_ge(na_bias, 4 * l + cb + 1)

                def score_max(s):
                    t, h = s // 4, s % 4
                    lat, i = tiles[t]
                    n = L * lat + 256
                    dve.wait_ge(at_s, u0 + s + 1)
                    if u0 + s >= 4:
                        dve.wait_ge(at_p, u0 + s - 3)
                    if u0 + s >= 2:
                        dve.wait_ge(at_n, u0 + s - 1)
                    dst, src = s_sb[:, s % 4, KEYS - n:KEYS], ps[s % 2][:, 768 - n:768]
                    if kind == "swa":
                        bias = sw_m[:, (0, 1, 1, 2)[i], :] if lat else sw_m[:, 0, 384:640]
                    elif lat:
                        first = 4 * (i % 2) + h
                        bias = na_b[:, first:9:8 - first, :]
                        dst, src = (a.rearrange("p (k c) -> p k c", k=2) for a in (dst, src))
                    else:
                        bias = na_b[:, 8, :]
                    link(dve.tensor_tensor_reduce(dst, src, bias, 1.0, -3e38, ALU.add, ALU.max,
                                                  mx[:, s % 2:s % 2 + 1]))
                    if kind == "na":
                        dve.tensor_scalar(nb[:, h:h + 1], mx[:, s % 2:s % 2 + 1], -SCALE, None, ALU.mult)\
                           .then_inc(at_n, 1)
                    else:
                        dve.tensor_scalar(nb[:, h:h + 1], mx[:, s % 2:s % 2 + 1], sink8[:, l, h:h + 1],
                                          -SCALE, ALU.max, ALU.mult).then_inc(at_n, 1)

                def normalise(v):
                    n = L * tiles[v // 4][0] + 256
                    dve.wait_ge(at_p, u0 + v + 1)
                    if u0 + v:
                        dve.wait_ge(at_q, u0 + v)
                    link(dve.reciprocal(rinv[:], sums[:, v % 4:v % 4 + 1]))
                    p = p_sb[:, v % 3, KEYS - n:KEYS]
                    dve.tensor_scalar(p, p, rinv[:], None, ALU.mult).then_inc(at_q, 1)

                def out_copy(t):
                    lat, i = tiles[t]
                    dve.wait_ge(at_pv, u0 + 4 * t + 4)
                    src, dst = ps_out[(t0 + t) % 2][:, 0:2 * P], f_t[:, f0:f0 + 2, :]
                    if kind == "na" and lat:
                        dst = dst[:, :, 0:LAT].rearrange("p b (r c) -> p b r c", c=GRID_W)
                        dst = backwards(dst[:, :, :, 16 * i:16 * i + 16])
                        src = src.rearrange("p (b r c) -> p b r c", r=ROWS, c=16)
                    else:
                        o = P * i if lat else LAT + P * i
                        dst = dst[:, :, o:o + P]
                        src = src.rearrange("p (b t) -> p b t", b=2)
                    dve.tensor_copy(dst, src).then_inc(at_o, 1)

                if kind == "na":
                    dve.wait_ge(mix_done, MIXERS * l + 1)
                    dve.memset(na_b[:, 8], 0.0)
                    dve.wait_ge(nv_t, 5 * l + 1)
                    dve.tensor_copy(na_vc[:].rearrange("p j d -> p (j d)"), ps_v).then_inc(nv_c, 1)
                    dve.wait_ge(at_ld, 64 * l + 16)
                else:
                    dve.wait_ge(at_pre, l + 1)
                    dve.tensor_copy(sw_v[:].rearrange("p j d -> p (j d)"), ps[2][:, 0:TOK]).then_inc(at_pre_c, 1)
                    dve.wait_ge(at_ld, 64 * l + 64)
                    link(dve.tensor_copy(s_sb[:, :, KEYS:KEYS + 1], sink8[:, l].unsqueeze(2)))
                    for n, blk in enumerate((KS, QS, QS + 1)):
                        dve.wait_ge(rope_p, 3 * l + n + 1)
                        if 3 * l + n:
                            dve.wait_ge(rope_d, 3 * l + n)
                        dve.tensor_tensor(sw_t[:, 0], ps[n % 2][:, 0:LAT], sw_cs[:, 1], ALU.mult)
                        link(dve.tensor_tensor(sw_t[:, 1], u_t[:, blk, 0:LAT], sw_cs[:, 0], ALU.mult))
                        dve.tensor_tensor(u_t[:, blk, 0:LAT], sw_t[:, 0], sw_t[:, 1], ALU.add).then_inc(rope_d, 1)
                for s in range(U + 3):
                    if kind == "na" and s % 4 == 0 and s // 4 < 4:
                        dve.wait_ge(nv_t, 5 * l + s // 4 + 2)
                        dve.tensor_copy(na_v[:, s // 4 % 2].rearrange("p j d -> p (j d)"), ps_v).then_inc(nv_c, 1)
                        band_bias(s // 4)
                    if s < U:
                        score_max(s)
                    if 1 <= s <= U:
                        normalise(s - 1)
                    if s >= 3 and (s - 3) % 4 == 3:
                        out_copy((s - 3) // 4)
                dve.wait_ge(at_o, t0 + len(tiles))
                dve.sem_inc(mix_done, 1)

            def halves(ap, m, right):
                if ap.shape[-1] == P:
                    return ap.rearrange("p (n two m) -> p n two m", two=2, m=m)[:, :, right]
                return ap.rearrange("p (c n two m) -> p c n two m", n=P // (2 * m), two=2, m=m)[:, :, :, right]

            def hgrn(l):
                T = width[l]
                nch = T // P
                dve.wait_ge(mix_done, MIXERS * l + 3)
                dve.wait_ge(hg_ld, 16 * (l + 1))
                link(dve.tensor_copy(hmask[:], hmask_f[:]))
                for p in range(2):
                    n = 2 * l + p
                    dve.wait_ge(hg_gate, n + 1)
                    for d in range(2):
                        f = u_t[:, (FF, FB)[d] + p, :]
                        if l:
                            dve.tensor_scalar(hk[:, d], hk[:, d], lb1[:, d, p:p + 1], None, ALU.mult)
                            link(dve.tensor_scalar(f, f, lb1[:, d, p:p + 1], lb[:, d, p:p + 1], ALU.mult, ALU.add))
                        dve.tensor_tensor(hq[:, d, 0:T], u_t[:, QD + p, 0:T], f[:, 0:T], ALU.mult)\
                           .then_inc(hg_init, 1)
                    dve.tensor_tensor(ho[:, 0:T], hk[:, 0, 0:T], hk[:, 1, 0:T], ALU.add).then_inc(hg_init, 1)
                    dve.wait_ge(hg_v, n + 1)
                    dve.tensor_copy(hv[:].rearrange("p c d -> p (c d)"), ps[2][:, 0:TOK]).then_inc(hg_vc, 1)
                    na = 30 * n
                    for h in range(2):
                        dve.wait_ge(hg_a, na + h + 1)
                        dve.tensor_tensor(hatt[:, h, 0:T].rearrange("p (c t) -> p c t", t=P),
                                          ps[h][:, 0:T].rearrange("p (c t) -> p c t", t=P),
                                          ident.unsqueeze(1).to_broadcast([P, nch, P]), ALU.mult).then_inc(hg_m, 1)
                    tot = [u_t[:, FF + p, :], u_t[:, FB + p, :]]
                    off = 0
                    for i in range(LEVELS):
                        m = 1 << i
                        nbk = TOK // (2 * m)
                        for d in range(2):
                            for h in range(2):
                                k = na + 2 + 2 * (2 * i + d) + h
                                dve.wait_ge(hg_a, k + 1)
                                dve.wait_ge(hg_m, k)
                                dve.copy_predicated(halves(hatt[:, h, 0:T], m, 1 - d),
                                                    halves(hmask[:, LEVELS * d + i], m, 1 - d).unsqueeze(1)
                                                    .to_broadcast([P, nch, P // (2 * m), m]),
                                                    halves(ps[h][:, 0:T], m, 1 - d))\
                                   .then_inc(hg_m, 1)
                            a = tot[d].rearrange("p (n two) -> p n two", two=2)
                            kv = hk[:, d].rearrange("p (n two m) -> p n two m", two=2, m=m)
                            qv = hq[:, d].rearrange("p (n two m) -> p n two m", two=2, m=m)
                            nq = T // (2 * m)
                            qs, ks = (1, 0) if d == 0 else (0, 1)
                            dve.tensor_tensor(qv[:, 0:nq, qs], qv[:, 0:nq, qs],
                                              a[:, 0:nq, 1 - qs].unsqueeze(2).to_broadcast([P, nq, m]), ALU.mult)
                            dve.tensor_tensor(kv[:, :, ks], kv[:, :, ks],
                                              a[:, :, 1 - ks].unsqueeze(2).to_broadcast([P, nbk, m]), ALU.mult)
                            nxt = ha[:, d, off:off + nbk]
                            dve.tensor_tensor(nxt, a[:, :, 0], a[:, :, 1], ALU.mult).then_inc(hg_u, 1)
                            dve.wait_ge(hg_u, 14 * n + 2 * i + d + 1)
                            tot[d] = nxt
                        off += nbk
                    for d in range(2):
                        dve.wait_ge(hg_ds, 2 * n + d + 1)
                        for j, c in enumerate(ORDER[d][:5]):
                            ds = ps[2][:, P * j:P * j + P]
                            if j == 0:
                                link(dve.tensor_copy(hst[:, d, 1], ds))
                            else:
                                link(dve.scalar_tensor_tensor(hst[:, d, j + 1], hst[:, d, j], tot[d][:, c:c + 1], ds,
                                                              ALU.mult, ALU.add))
                        dve.tensor_tensor(hst[:, d, 1:6], hst[:, d, 1:6],
                                          blockones.unsqueeze(1).to_broadcast([P, 5, P]), ALU.mult)\
                           .then_inc(hg_st, 1)
                    dve.wait_ge(hg_rs, n + 1)
                    link(dve.scalar_tensor_tensor(ho[:, 0:T], ps[3][:, 0:T], hgain[:, l, p:p + 1], hkt[:, 1, 0:T],
                                                  ALU.mult, ALU.mult))
                    link(dve.tensor_tensor(f_t[:, 6 + p, 0:T], ho[:, 0:T], u_t[:, GD + p, 0:T], ALU.mult))
                    dve.sem_inc(hg_end, 1)
                dve.sem_inc(mix_done, 1)

            dve.memset(eps_c[:], EPS)
            for count in (hid_hi_done, hid_lo_done, ada_done, ada_copied):
                dve.sem_inc(count, 1)
            dve.wait_ge(s_in, 16 * 7)
            dve.tensor_scalar(sink8[:], sinks[:], 1.0 / SCALE, None, ALU.mult)
            link(dve.tensor_tensor(lb[:], lbc[:, :, 0], lbc[:, :, 1], ALU.max))
            for j in range(2):
                ins = dve.tensor_tensor(lbt[:, j], lbc[:, :, j], lb[:], ALU.subtract)
            ins.then_inc(consts_done, 1)
            dve.wait_ge(consts_done, 2)
            link(dve.tensor_tensor(lb1[:], lbt[:, 0], lbt[:, 1], ALU.add))
            link(dve.reciprocal(lb1[:], lb1[:]))
            link(dve.tensor_tensor(lb[:], lbt[:, 1], lb1[:], ALU.mult))
            link(dve.tensor_tensor(lb1[:], lbt[:, 0], lb1[:], ALU.mult))
            for u in range(2):
                dve.wait_ge(w_hi_done, u + 1)
                dve.tensor_tensor(w_lo[:, u].rearrange("p c n -> p (c n)"), raw[:, u],
                                  w_hi[:, u].rearrange("p c n -> p (c n)").bitcast(F32), ALU.subtract)\
                   .then_inc(w_lo_done, 1)
            dve.wait_ge(s_cb, 1)
            with dve.Fori(0, 9) as q:
                ada_pair(q, 0, q)

            for l in range(DEPTH):
                tp, T = TP[l], width[l]
                dve.wait_ge(ada_copied, 10 if l == 0 else 49)
                pre_norm(l, SH1, SC1, G_PRE_MIX, TOK)
                lo_phase(tp["proj"], N_PROJ // 2, ada=(9, 0, 9) if l == 0 else None)
                for u in range(2):
                    dve.wait_ge(bank_free[u], tp["wout"] + 1)
                for b in range(2):
                    dve.wait_ge(fn_t, 2 * l + b + 1)
                    dve.tensor_copy(fn_f[:, b, 0:T], ps[b][:, 0:T]).then_inc(fn_te, 1)
                for n in range(2):
                    dve.wait_ge(fn_o, 2 * l + n + 1)
                    ins = dve.tensor_copy(f_t[:, 2 + n, 0:T], ps[2 + n][:, 0:T])
                ins.then_inc(mix_done, 1)
                attention("na", l)
                attention("swa", l)
                hgrn(l)
                for c in range(NC):
                    nhi[0] += 1
                    nlo[0] += 1
                    dve.wait_ge(hhi_ready, nhi[0])
                    dve.tensor_tensor(h_lo[:, c, 0:T], f_t[:, c, 0:T], h_hi[:, c, 0:T].bitcast(F32),
                                      ALU.subtract).then_inc(hlo_ready, 1)
                lo_phase(tp["wout"], N_OUT // 2, ada=(20, 0, 20) if l == 0 else None)
                if l == 0:
                    dve.wait_ge(ada_copied, 25)
                post_norm(l, GT1, G_POST_MIX, T)
                pre_norm(l, SH2, SC2, G_PRE_FFN, T)
                for p, kc in enumerate(FFN_CHUNKS):
                    a = (24 + 12 * p, 1, 12 * p) if l == 0 and p < 2 else None
                    ffn_in(tp["in", p], l * 22 + sum(FFN_CHUNKS[:p]), kc, T, a)
                    a = (32 + 12 * p, 1, 12 * p + 8) if l == 0 and p < 2 else None
                    lo_phase(tp["out", p], N_OUT // 2, ada=a, add=p > 0, T=T,
                             last=l == DEPTH - 1 and p == len(FFN_CHUNKS) - 1)
                post_norm(l, GT2, G_POST_FFN, T)


ORDER = ((4, 5, 0, 1, 2, 3), (5, 4, 3, 2, 1, 0))


def _tile(w):
    t = np.zeros((P, NC, P), w.dtype)
    t[:, :w.shape[0] // P] = w.reshape(-1, P, P).transpose(1, 0, 2)
    return t.reshape(P, NC * P)


def _weight_stream(w_in, w_out, w_ffn_in, w_ffn_out):
    tiles = []
    swa = np.r_[0:64, 128:192, 64:128, 192:256] + 8 * P
    cols = [range(P * b, P * b + P) for b in (2, 3, 4, 5, 10, 11, 14, 15, 16, 17, 18, 19, 0, 1, 6, 7)]
    cols += [swa[:P], swa[P:]] + [range(P * b, P * b + P) for b in (12, 13, 20, 21)]
    for l in range(DEPTH):
        tiles += [_tile(w_in[l][:, np.asarray(c)]) for c in cols]
        tiles += [_tile(w_out[l][:, P * o:P * o + P]) for o in range(NC)]
        j = 0
        for kc in FFN_CHUNKS:
            for c in range(j, j + kc):
                tiles += [_tile(w_ffn_in[l][:, h * DFF + P * c:h * DFF + P * c + P]) for h in range(2)]
            tiles += [_tile(w_ffn_out[l][P * j:P * (j + kc), P * o:P * o + P]) for o in range(NC)]
            j += kc
    return np.stack(tiles)


def _tables():
    f = np.float32
    tok, ch = np.arange(LAT), np.arange(HD)

    def dft(n):
        a = 2 * np.pi * (np.outer(np.arange(n), np.arange(n)) % n) / n
        t = np.stack([np.cos(a), -np.sin(a)], 1) / np.sqrt(n * HD)
        return t.reshape(n // P, P, 2, n).transpose(1, 0, 2, 3).astype(f)

    a = 2 * np.pi * (np.outer(ch, ch) % HD) / HD
    dftd = np.concatenate([np.kron(np.eye(2), np.cos(a)), np.kron(np.eye(2), np.sin(a))], 1).astype(f)
    d = np.arange(P)
    rot = np.zeros((P, P), f)
    first = d % 32 < 16
    rot[d[first] + 16, d[first]] = -1
    rot[d[~first] - 16, d[~first]] = 1
    freq = 10000.0 ** (-(d % 16) / 16)
    pos = np.where((d % HD < 32)[:, None], tok // GRID_W, tok % GRID_W)
    rope = np.stack([np.cos(pos * freq[:, None]), np.sin(pos * freq[:, None])], 1).astype(f)
    swa = np.zeros((P, 3, 640), f)
    for kind in range(3):
        rel = np.arange(384) - P * kind - d[:, None]
        swa[:, kind, :384] = np.where(np.abs(rel) <= 128, 0, NEG)
    na = np.zeros((P, 4, BAND), f)
    for cb in range(4):
        q = 16 * cb + 15 - d % 16
        first_col = np.clip(q - 8, 0, GRID_W - 16)[:, None]
        key = BAND0[cb] + np.arange(BAND)
        na[:, cb] = np.where((key >= first_col) & (key < first_col + 16), 0, NEG)
    lv = np.zeros((P, 2 * LEVELS, P), f)
    for i in range(LEVELS):
        m = 1 << i
        same = d[:, None] // (2 * m) == d // (2 * m)
        right = d // m % 2 == 1
        lv[:, i] = same & ~right[:, None] & right
        lv[:, LEVELS + i] = same & right[:, None] & ~right
    squares = np.stack([np.ones((P, P)), np.eye(P), np.kron(np.eye(2), np.ones((HD, HD)))]).astype(f)
    return {"dftL": dft(LAT), "dftC": dft(CTX), "dftD": dftd, "rotm": rot, "rope": rope, "swamask": swa,
            "namask": na, "lvmask": lv, "sqc": squares}


def kernel(x, c, ctx, c_ctx, w_ada, b_ada, g_pre_mix, g_post_mix, g_pre_ffn, g_post_ffn, w_in, w_out, na_rpb, w_fnet,
           swa_sink, hgrn_lb_logits, hgrn_norm_g, w_ffn_in, w_ffn_out):
    import concourse.bacc as bacc
    from concourse.bass_utils import run_bass_kernel_spmd

    a = {
        "xT": np.concatenate([np.asarray(x)[0].T, np.asarray(ctx)[0].T], 1),
        "cvec": np.stack([np.asarray(c)[0], np.asarray(c_ctx)]),
        "wstream": _weight_stream(*map(np.asarray, (w_in, w_out, w_ffn_in, w_ffn_out))),
        "adaT": np.asarray(w_ada).transpose(0, 2, 1).reshape(DEPTH * N_ADA, P, D),
        "badaT": np.asarray(b_ada).reshape(DEPTH, N_ADA, P).transpose(2, 0, 1),
        "gT": np.stack([np.asarray(g) for g in (g_pre_mix, g_post_mix, g_pre_ffn, g_post_ffn)], 1)
        .reshape(DEPTH, 4, NC, P).transpose(3, 0, 1, 2),
        "rpb": np.pad(np.asarray(na_rpb).transpose(0, 2, 1, 3), ((0, 0), (0, 0), (0, 0), (RPB_PAD, RPB_W - RPB_PAD - 31))),
        "wf": np.asarray(w_fnet).reshape(DEPTH, 2, P, 2 * P).transpose(0, 2, 1, 3),
        "sink": np.asarray(swa_sink),
        "lbT": np.asarray(hgrn_lb_logits).reshape(2, DEPTH, 2, P).transpose(3, 0, 1, 2),
        "hgT": np.asarray(hgrn_norm_g).reshape(DEPTH, 2, P).transpose(2, 0, 1),
        **_tables(),
    }
    arrays = {f"in_{k}": np.ascontiguousarray(v) for k, v in a.items()}
    nc = bacc.Bacc("TRN2", target_bir_lowering=False, num_devices=1)
    args = {k: nc.dram_tensor(f"in_{k}", arrays[f"in_{k}"].shape, mybir.dt.from_np(arrays[f"in_{k}"].dtype),
                              kind="ExternalInput").ap() for k in a}
    out = nc.dram_tensor("out_xT", (D, LAT), F32, kind="ExternalOutput").ap()
    hybrid_kernel(nc, **args, out=out)
    r = run_bass_kernel_spmd(nc, [arrays], core_ids=[0])
    return np.ascontiguousarray(r.results[0]["out_xT"].T)[None]
```

```python
from contextlib import ExitStack

import numpy as np

import concourse.bass as bass
from concourse import mybir
from concourse.alu_op_type import AluOpType as ALU

ACT = mybir.ActivationFunctionType
AX_X = mybir.AxisListType.X
F32 = mybir.dt.float32
F32R = mybir.dt.float32r
U8 = mybir.dt.uint8

P = 128
D = 1024
NC = D // P
LAT, CTX = 512, 256
TOK = LAT + CTX
DEPTH = 2
DFF = 2816
GRID_W, ROWS = 64, LAT // 64
HD = 64
EPS = 1e-6
NEG = -1e30
SCALE = HD ** -0.5

KA, VA, KS, VS, FF, FB, IV, QA, UB, QS, QD, GD = 0, 2, 4, 5, 6, 8, 10, 12, 14, 16, 18, 20
N_PROJ, N_PROJ_CTX = 22, 12
FFN_CHUNKS = (8, 8, 6)
N_OUT = NC

SH1, SC1, GT1, SH2, SC2, GT2 = (NC * i for i in range(6))
N_ADA = 6 * NC
ADA_FIRST = (SC1 + NC) // 2
G_PRE_MIX, G_POST_MIX, G_PRE_FFN, G_POST_FFN = range(4)

RPB_W = 64
RPB_PAD = 16
BAND = 32
BAND0 = (0, 8, 24, 32)

LEVELS = 7

KEYS = 640

STREAMS = ((0, LAT, 0), (LAT, TOK, 1))


def tile_counts(layer):
    g = layer * 49
    at = {"proj": g}
    g += N_PROJ // 2
    at["wout"] = g
    g += N_OUT // 2
    for p, kc in enumerate(FFN_CHUNKS):
        at["in", p] = g
        g += kc
        at["out", p] = g
        g += N_OUT // 2
    at["end"] = g
    return at


N_PAIRS = tile_counts(DEPTH - 1)["end"]


def backwards(ap):
    dims = [list(d) for d in ap.ap]
    step, n = dims[-1]
    return bass.AP(ap.tensor, ap.offset + step * (n - 1), dims[:-1] + [[-step, n]])


def attention_plan(kind, layer):
    return [(True, t) for t in range(4)] + ([(False, t) for t in range(2)] if layer < DEPTH - 1 else [])


def hybrid_kernel(nc, xT, cvec, wstream, adaT, badaT, gT, rpb, wf, sink, lbT, hgT, dftL, dftC, dftD, rotm,
                  rope, swamask, namask, lvmask, sqc, out):
    with ExitStack() as ctx:
        def sem(name):
            return ctx.enter_context(nc.semaphore(name))

        top = [(nc.sbuf_base + 63) // 64 * 64]
        ctx.enter_context(nc.sbuf_tensor("arena", [P, 212_600], U8))

        def region(nbytes):
            top[0] += nbytes
            return top[0] - nbytes

        def at(name, shape, dt, base, off=0):
            return nc.alloc_sbuf_tensor_at(name, shape, dt, offset=base + off)

        CH = TOK * 4
        r_x, r_h, r_big, r_f = region(NC * CH), region(2 * NC * CH), region(N_PROJ * CH), region(NC * CH)
        r_w, r_ada, r_cb = region(3 * 2 * D * 4), region(2 * D * 4), region(2 * D * 4)
        r_sm = region(5700)
        assert top[0] <= nc.sbuf_usable_end

        x = at("x", [P, NC, TOK], F32, r_x)
        h_hi = at("h_hi", [P, NC, TOK], F32R, r_h)
        h_lo = at("h_lo", [P, NC, TOK], F32R, r_h, NC * CH)
        u_t = at("u_t", [P, N_PROJ, TOK], F32, r_big)
        hid_hi = at("hid_hi", [P, 8, TOK], F32R, r_big)
        hid_lo = at("hid_lo", [P, 8, TOK], F32R, r_big, 8 * CH)
        sq = at("sq", [P, 2, TOK], F32, r_big, 16 * CH)
        tmp = at("tmp", [P, 2, TOK], F32, r_big, 18 * CH)
        lnms = at("lnms", [P, TOK], F32, r_big, 20 * CH)
        rstd = at("rstd", [P, TOK], F32, r_big, 21 * CH)
        f_t = at("f_t", [P, NC, TOK], F32, r_f)
        raw = at("raw", [P, 2, D], F32, r_w)
        w_hi = at("w_hi", [P, 2, NC, P], F32R, r_w, 2 * D * 4)
        w_lo = at("w_lo", [P, 2, NC, P], F32R, r_w, 4 * D * 4)
        ada_0 = [at("ada_0a", [P, 12, D], F32, r_big), at("ada_0b", [P, 4, D], F32, r_f)]
        ada_w = at("ada_w", [P, 2, D], F32, r_ada)
        c_b = at("c_b", [P, 2, D], F32, r_cb)
        small_top = [0]

        def small(name, shape, dt=F32):
            n = int(np.prod(shape[1:])) * (4 if dt == F32 else 1)
            small_top[0] += (n + 31) // 32 * 32
            assert small_top[0] <= 5700
            return at(name, shape, dt, r_sm, small_top[0] - (n + 31) // 32 * 32)

        consts = small("consts", [P, 3, P])
        ones, ident, blockones = consts[:, 0], consts[:, 1], consts[:, 2]
        ada_c = [small(f"ada_c{l}", [P, N_ADA, 2]) for l in range(DEPTH)]
        ada_t = small("ada_t", [P, 2, 2])
        bada = small("bada", [P, DEPTH, N_ADA])
        gcol = small("gcol", [P, DEPTH, 4, NC])
        col_sh = small("col_sh", [P, NC, 2])
        col_sc = small("col_sc", [P, NC, 2])
        col_gs = small("col_gs", [P, NC, 2])
        col_gg = small("col_gg", [P, NC, 2])
        eps_c = small("eps_c", [P, 1])
        sinks = small("sinks", [P, DEPTH, 4])
        sink8 = small("sink8", [P, DEPTH, 4])
        lbc = small("lbc", [P, 2, DEPTH, 2])
        lb = small("lb", [P, 2, 2])
        lb1 = small("lb1", [P, 2, 2])
        lbt = small("lbt", [P, 2, 2, 2])
        hgain = small("hgain", [P, DEPTH, 2])
        mx = small("mx", [P, 2])
        nb = small("nb", [P, 4])
        sums = small("sums", [P, 4])
        rinv = small("rinv", [P, 1])

        fn_l = at("fn_l", [P, 4, 2, LAT], F32, r_f)
        fn_c = at("fn_c", [P, 2, 2, CTX], F32, r_f, 16384)
        fn_d = at("fn_d", [P, 2 * P], F32, r_f, 20480)
        fn_w = at("fn_w", [P, 2, 2 * P], F32, r_f, 21504)
        fn_ab = at("fn_ab", [P, 6, 4 * P], F32, r_h)
        fn_f = at("fn_f", [P, 2, TOK], F32, r_h, 12288)

        s_sb = at("s_sb", [P, 4, 656], F32, r_h)
        p_sb = at("p_sb", [P, 3, 656], F32, r_h, 10496)
        pt_sb = at("pt_sb", [P, 2, 640], F32, r_h, 18368)
        na_b = at("na_b", [P, 9, 256], F32, r_h, 23488)
        na_v = at("na_v", [P, 2, 2, 256], F32, r_h, 32704)
        na_vc = at("na_vc", [P, 2, 256], F32, r_h, 36800)
        na_m = at("na_m", [P, 4, BAND], F32, r_h, 38848)
        na_r = at("na_r", [P, 2, 1024], F32, r_h, 39360)
        na_q = at("na_q", [P, 2, 2, 2, P], F32, r_f, 4 * CH)
        na_qc = at("na_qc", [P, 2, 2, CTX], F32, r_f, 4 * CH + 4096)
        na_vs = at("na_vs", [P, 2, 2, 256], F32, r_f, 6 * CH + 2048)
        qz = at("qz", [P, 2, 2, TOK], F32, r_big)
        sw_m = at("sw_m", [P, 3, 640], F32, r_h, 23488)
        sw_v = at("sw_v", [P, 6, P], F32, r_h, 31168)
        sw_cs = at("sw_cs", [P, 2, LAT], F32, r_big, 16 * CH - 4608)
        sw_r = at("sw_r", [P, P], F32, r_big, 16 * CH - 512)
        sw_t = at("sw_t", [P, 2, LAT], F32, r_h, 38848)

        hk = [at(f"hk{p}", [P, 2, TOK], F32, *a) for p, a in enumerate(((r_h, 6144), (r_big, QS * CH)))]
        hqz = [qz, at("qz1", [P, 2, 2, TOK], F32, r_big, QA * CH)]
        ha = at("ha", [P, 2, TOK], F32, r_h, 12288)
        hatt = at("hatt", [P, 2, TOK], F32, r_h, 18432)
        hv = at("hv", [P, 6, P], F32, r_h, 24576)
        hkt = at("hkt", [P, 2, TOK], F32, r_h, 27648)
        hst = at("hst", [P, 2, 6, P], F32, r_h, 33792)
        ho = at("ho", [P, TOK], F32, r_h, 39936)
        hmask = at("hmask", [P, 2 * LEVELS, P], U8, r_h, 43008)
        hmask_f = at("hmask_f", [P, 2 * LEVELS, P], F32, r_big, QA * CH)
        hms = at("hms", [P, TOK], F32, r_h, 44800)

        ps = [ctx.enter_context(nc.psum_tensor(f"ps{i}", [P, 1024], F32)) for i in range(4)]
        ps_out = [ps[3][:, 0:512], ps[3][:, 512:1024]]
        ps_v = ps[2][:, 512:1024]

        raw_ld = [sem(f"raw_loaded{u}") for u in range(2)]
        w_hi_done, w_lo_done = sem("w_hi_done"), sem("w_lo_done")
        blk_done = sem("block_product_done")
        bank_free = [sem(f"block_bank_free{u}") for u in range(2)]
        hid_hi_done, hid_lo_done = sem("hid_hi_done"), sem("hid_lo_done")
        ada_ld = [sem(f"ada_loaded{u}") for u in range(2)]
        ada_done, ada_copied = sem("ada_products_done"), sem("ada_copied")
        x_ld = [sem(f"x_loaded{k}") for k in range(2)]
        s_in, s_cin, s_cb = sem("inputs_loaded"), sem("c_loaded"), sem("c_activated")
        s_out = sem("output_stored")
        consts_done = sem("small_consts_done")
        dve_chain, act_chain, pool_chain = sem("dve_chain"), sem("act_chain"), sem("pool_chain")
        sq_sum = sem("squares_summed")
        ada_0_ld = [sem(f"ada_first_loaded{k}") for k in range(ADA_FIRST)]
        ada_0_done = sem("ada_first_done")
        sq_ready, sq_used = sem("squares_ready"), sem("squares_used")
        rstd_ready = sem("rstd_ready")
        scaled = sem("scaled_ready")
        hhi_ready, hlo_ready = sem("h_hi_ready"), sem("h_lo_ready")
        x_upd, pn_m = sem("x_updated"), sem("post_norm_scaled")
        mix_done = sem("mixer_done")
        fn_ld, fn_a, fn_abe = sem("fnet_loaded"), sem("fnet_channels"), sem("fnet_channels_copied")
        fn_t, fn_te, fn_o = sem("fnet_tokens"), sem("fnet_tokens_copied"), sem("fnet_out")
        at_ld, rope_ld = sem("swa_masks_loaded"), sem("rope_tables_loaded")
        na_ld = [sem(f"na_bias_loaded{u}") for u in range(2)]
        na_mask = sem("na_mask_loaded")
        na_bias, na_st = sem("na_bias_ready"), sem("na_block_staged")
        sw_st = sem("swa_queries_staged")
        at_pre, at_pre_c = sem("attention_v_transposed"), sem("attention_v_copied")
        rope_p, rope_d = sem("rope_rotated"), sem("rope_done")
        at_s, at_n, at_p = sem("scores"), sem("score_max"), sem("probs")
        at_t, at_tc, at_pv = sem("probs_transposed"), sem("probs_t_copied"), sem("pv_done")
        at_q, at_o = sem("probs_scaled"), sem("attention_out_copied")
        nv_t, nv_c = sem("na_v_transposed"), sem("na_v_copied")
        hg_ld, hg_gate, hg_init = sem("hgrn_masks_loaded"), sem("hgrn_gates"), sem("hgrn_init")
        hg_v, hg_vc = sem("hgrn_v_transposed"), sem("hgrn_v_copied")
        hg_a, hg_m, hg_u = sem("hgrn_att"), sem("hgrn_att_masked"), sem("hgrn_level_up")
        hg_mc = sem("hgrn_masks_converted")
        hg_f, hg_q = sem("hgrn_gates_bounded"), sem("hgrn_queries")
        hg_kt, hg_ktc = sem("hgrn_k_transposed"), sem("hgrn_k_copied")
        hg_ds, hg_st, hg_o = sem("hgrn_ds"), sem("hgrn_states"), sem("hgrn_out")
        hg_sq, hg_ms, hg_rs, hg_end = sem("hgrn_sq"), sem("hgrn_ms"), sem("hgrn_rstd"), sem("hgrn_pair_done")

        block = ctx.enter_context(nc.Block())
        TP = [tile_counts(l) for l in range(DEPTH)]
        full = [l < DEPTH - 1 for l in range(DEPTH)]
        width = [TOK if f else LAT for f in full]
        MIXERS = 4
        phases = [(kind, l) for l in range(DEPTH) for kind in ("na", "swa")]
        unit0, tile0 = {}, {}
        nu = nt = 0
        for ph in phases:
            unit0[ph], tile0[ph] = nu, nt
            tiles = attention_plan(*ph)
            nu, nt = nu + 4 * len(tiles), nt + len(tiles)

        def first_units(k):
            return ada_0[0][:, 2 * k:2 * k + 2] if k < 6 else ada_0[1][:, 2 * k - 12:2 * k - 10]

        @block.sync
        def _(sp):
            for v in range(2):
                sp.dma_start(c_b[:, v], bass.AP(cvec.tensor, v * D, [[0, P], [1, D]])).then_inc(s_cin, 16)
            for k in range(ADA_FIRST):
                if k == ADA_FIRST // 2 + 1:
                    sp.wait_ge(x_ld[0], 16)
                sp.dma_start(first_units(k), adaT[2 * k:2 * k + 2].rearrange("u p d -> p u d")).then_inc(ada_0_ld[k], 16)
                if k == ADA_FIRST // 2:
                    for u in range(2):
                        sp.dma_start(raw[:, u], wstream[u]).then_inc(raw_ld[u], 16)

            def stream(g0, g1):
                with sp.Fori(g0, g1) as g:
                    for u in range(2):
                        sp.wait_ge(w_lo_done, 2 * g + (u - 1))
                        sp.dma_start(raw[:, u], wstream[2 * g + u]).then_inc(raw_ld[u], 16)

            def mixer_tables(l):
                sp.wait_ge(blk_done, 2 * TP[l]["wout"])
                sp.dma_start(na_m[:], namask).then_inc(na_mask, 16)
                for cb in range(4):
                    if cb == 2:
                        sp.wait_ge(mix_done, MIXERS * l + 1)
                        sp.dma_start(sw_r[:], rotm).then_inc(rope_ld, 16)
                        sp.dma_start(sw_cs[:], rope).then_inc(rope_ld, 16)
                    if cb >= 2:
                        sp.wait_ge(na_bias, 4 * l + cb - 1)
                    for rq in range(ROWS):
                        off = (l * 15 + 7 - rq) * 4 * RPB_W + BAND0[cb] - 16 * cb + RPB_PAD
                        src = bass.AP(rpb.tensor, off, [[1, 16], [RPB_W, 4 * ROWS], [1, BAND]])
                        dst = na_r[16 * rq:16 * rq + 16, cb % 2].rearrange("p (n c) -> p n c", c=BAND)
                        sp.dma_start(dst, src).then_inc(na_ld[cb % 2], 16)
                sp.wait_ge(mix_done, MIXERS * l + 2)
                sp.dma_start(sw_m[:], swamask).then_inc(at_ld, 16)
                sp.dma_start(hmask_f[:], lvmask).then_inc(hg_ld, 16)

            first = 1
            for l in range(DEPTH):
                stream(first, TP[l]["wout"] + 2)
                mixer_tables(l)
                first = TP[l]["wout"] + 2
            stream(first, N_PAIRS)
            outT = out.rearrange("(c p) t -> p c t", p=P)
            for c in range(0, NC, 2):
                sp.wait_ge(x_upd, 2 * DEPTH * NC - NC + c + 2)
                sp.dma_start(outT[:, c:c + 2], x[:, c:c + 2, 0:LAT]).then_inc(s_out, 16)
            sp.wait_ge(s_out, 16 * NC // 2)

        @block.gpsimd
        def _(pool):
            def ada_loads(p0, n):
                with pool.Fori(p0, p0 + n) as q:
                    for u in range(2):
                        pool.wait_ge(ada_done, 4 * q + (2 * u - 1))
                        pool.dma_start(ada_w[:, u], adaT[2 * q + (2 * ADA_FIRST + u)]).then_inc(ada_ld[u], 16)

            chain = [0]

            def link(ins):
                chain[0] += 1
                ins.then_inc(pool_chain, 1)
                pool.wait_ge(pool_chain, chain[0])

            def squares(g0, b0, n, T):
                for b in range(b0, min(b0 + n, N_OUT - 1)):
                    pool.wait_ge(bank_free[b % 2], g0 + b // 2 + 2)
                    f = f_t[:, b, 0:T]
                    link(pool.tensor_tensor(sq[:, 1 if b == 0 else 0, 0:T], f, f, ALU.mult))
                    if b:
                        link(pool.tensor_tensor(sq[:, 1, 0:T], sq[:, 1, 0:T], sq[:, 0, 0:T], ALU.add))
                    if b == N_OUT - 2:
                        pool.sem_inc(sq_sum, 1)

            def hgrn_queries(l):
                T = width[l]
                pool.wait_ge(hg_mc, l + 1)
                pool.memset(hqz[1][64:128, :, 0], 0.0)
                pool.memset(hqz[1][0:64, :, 1], 0.0)
                for p in range(2):
                    n = 2 * l + p
                    qz = hqz[p]
                    pool.wait_ge(hg_gate, n + 1)
                    tot = [u_t[:, FF + p, :], u_t[:, FB + p, :]]
                    for d in range(2):
                        if l:
                            pool.wait_ge(hg_f, 2 * p + d + 1)
                        for h in range(2):
                            a = slice(64 * h, 64 * h + 64)
                            ins = pool.tensor_tensor(qz[a, d, h, 0:T], u_t[a, QD + p, 0:T], tot[d][a, 0:T], ALU.mult)
                        ins.then_inc(hg_q, 1)
                    off = 0
                    for i in range(LEVELS):
                        m = 1 << i
                        nq = T // (2 * m)
                        for d in range(2):
                            j = 2 * i + d
                            pool.wait_ge(hg_a, 16 * n + 2 + j + 1)
                            if i:
                                pool.wait_ge(hg_u, 14 * n + j - 1)
                            pool.wait_ge(hg_q, 16 * n + j + 1)
                            for h in range(2):
                                r = slice(64 * h, 64 * h + 64)
                                a = tot[d][r].rearrange("p (n two) -> p n two", two=2)[:, 0:nq, d]
                                q = qz[r, d, h, 0:T].rearrange("p (n two m) -> p n two m", two=2, m=m)[:, :, 1 - d]
                                ins = pool.tensor_tensor(q, q, a.unsqueeze(2).to_broadcast([64, nq, m]), ALU.mult)
                            ins.then_inc(hg_q, 1)
                            tot[d] = ha[:, d, off:off + TOK // (2 * m)]
                        off += TOK // (2 * m)

            pool.dma_start(consts[:], sqc.rearrange("k p n -> p k n")).then_inc(s_in, 16)
            pool.wait_ge(ada_0_ld[0], 16)
            for k in range(2):
                half = xT.rearrange("(k c p) t -> k p c t", k=2, p=P)[k]
                pool.dma_start(x[:, NC // 2 * k:NC // 2 * (k + 1)], half).then_inc(x_ld[k], 16)
            pool.dma_start(bada[:], badaT).then_inc(s_in, 16)
            pool.dma_start(gcol[:], gT).then_inc(s_in, 16)
            pool.dma_start(sinks[:], bass.AP(sink.tensor, 0, [[0, P], [4, DEPTH], [1, 4]])).then_inc(s_in, 16)
            pool.dma_start(lbc[:], lbT).then_inc(s_in, 16)
            pool.dma_start(hgain[:], hgT).then_inc(s_in, 16)
            for u in range(2):
                pool.dma_start(ada_w[:, u], adaT[2 * ADA_FIRST + u]).then_inc(ada_ld[u], 16)
            for l in range(DEPTH):
                if l:
                    pool.wait_ge(x_upd, 2 * l * NC)
                else:
                    pool.wait_ge(ada_0_done, 4 * ADA_FIRST)
                pool.dma_start(fn_d[:], dftD).then_inc(fn_ld, 16)
                pool.dma_start(fn_l[:], dftL).then_inc(fn_ld, 16)
                pool.dma_start(fn_c[:], dftC).then_inc(fn_ld, 16)
                pool.dma_start(fn_w[:], wf[l]).then_inc(fn_ld, 16)
                if l == 0:
                    ada_loads(1, 11)
                pool.wait_ge(mix_done, MIXERS * l + 1)
                for z in (na_q[64:128, :, :, 0], na_q[0:64, :, :, 1], na_qc[64:128, :, 0], na_qc[0:64, :, 1]):
                    ins = pool.memset(z, 0.0)
                ins.then_inc(na_st, 1)
                for cb in range(4):
                    if cb >= 2:
                        pool.wait_ge(at_s, unit0["na", l] + 4 * (cb - 1))
                    pool.wait_ge(na_st, 5 * l + cb + 1)
                    for p in range(2):
                        v = u_t[:, VA + p, 0:LAT].rearrange("p (r c) -> p r c", c=GRID_W)
                        ins = pool.tensor_copy(na_vs[:, cb % 2, p].rearrange("p (r c) -> p r c", c=BAND),
                                               v[:, :, BAND0[cb]:BAND0[cb] + BAND])
                    link(ins)
                    for p in range(2):
                        q = u_t[:, QA + p, 0:LAT].rearrange("p (r c) -> p r c", c=GRID_W)
                        for h in range(2):
                            a = slice(64 * h, 64 * h + 64)
                            ins = pool.tensor_copy(na_q[a, cb % 2, p, h].rearrange("p (r c) -> p r c", c=16),
                                                   backwards(q[a, :, 16 * cb:16 * cb + 16]))
                    if full[l] and cb == 3:
                        for h in range(2):
                            a = slice(64 * h, 64 * h + 64)
                            ins = pool.tensor_copy(na_qc[a, :, h], u_t[a, QA:QA + 2, LAT:TOK])
                    ins.then_inc(na_st, 1)
                pool.wait_ge(mix_done, MIXERS * l + 2)
                pool.memset(qz[64:128, :, 0], 0.0)
                ins = pool.memset(qz[0:64, :, 1], 0.0)
                if full[l]:
                    for h in range(2):
                        a = slice(64 * h, 64 * h + 64)
                        ins = pool.tensor_copy(qz[a, :, h, LAT:TOK], u_t[a, QS:QS + 2, LAT:TOK])
                ins.then_inc(sw_st, 1)
                pool.wait_ge(mix_done, MIXERS * l + 3)
                hgrn_queries(l)
                tp, T = TP[l], width[l]
                if l == 0:
                    for i in range(N_OUT // 2):
                        ada_loads(12 + i, 1)
                        squares(tp["wout"], 2 * i, 2, T)
                    ada_loads(16, 24)
                else:
                    squares(tp["wout"], 0, N_OUT, T)
                squares(tp["out", len(FFN_CHUNKS) - 1], 0, N_OUT, T)

        @block.scalar
        def _(act):
            chain = [0]

            def link(ins):
                chain[0] += 1
                ins.then_inc(act_chain, 1)
                act.wait_ge(act_chain, chain[0])

            def split_hi(g, u):
                act.wait_ge(raw_ld[u], 16 * g + 32)
                act.wait_ge(blk_done, 2 * g + (u + 1))
                act.activation(w_hi[:, u].rearrange("p c n -> p (c n)"), raw[:, u], ACT.Copy).then_inc(w_hi_done, 1)

            def copy_phase(g0, n, dst, b0, T):
                with act.Fori(0, n) as i:
                    for u in range(2):
                        act.wait_ge(blk_done, 2 * i + (2 * g0 + u + 1))
                        act.activation(dst[:, 2 * i + (b0 + u), 0:T], ps[u][:, 0:T], ACT.Copy)\
                           .then_inc(bank_free[u], 1)
                        split_hi(i + g0, u)

            def splits_only(g0, n, last):
                if n - last > 0:
                    with act.Fori(0, n - last) as i:
                        for u in range(2):
                            split_hi(i + g0, u)

            def ffn_in(g0, n, T):
                with act.Fori(0, n) as i:
                    act.wait_ge(blk_done, 2 * i + (2 * g0 + 1))
                    act.wait_ge(bank_free[1], i + (g0 + 1))
                    act.activation(tmp[:, 0, 0:T], ps[0][:, 0:T], ACT.Silu).then_inc(bank_free[0], 1)
                    split_hi(i + g0, 0)
                    split_hi(i + g0, 1)
                    act.wait_ge(bank_free[1], i + (g0 + 2))
                    act.activation(hid_hi[:, i, 0:T], tmp[:, 1, 0:T], ACT.Copy).then_inc(hid_hi_done, 1)

            nsq, nn = [0], [0]

            def mean_square(src, T, ready):
                for c in range(NC):
                    ready(c)
                    if nsq[0] >= 2:
                        act.wait_ge(sq_used, nsq[0] - 1)
                    act.activation(sq[:, c % 2, 0:T], src[:, c, 0:T], ACT.Square).then_inc(sq_ready, 1)
                    nsq[0] += 1
                inverse_root(T)

            def inverse_root(T):
                act.wait_ge(sq_used, nsq[0])
                link(act.activation(lnms[:, 0:T], ps[2][:, 0:T], ACT.Ln, bias=eps_c[:, 0:1], scale=1.0 / D))
                act.activation(rstd[:, 0:T], lnms[:, 0:T], ACT.Exp, scale=-0.5).then_inc(rstd_ready, 1)

            def late_mean_square(T):
                act.activation(lnms[:, 0:T], f_t[:, NC - 1, 0:T], ACT.Square).then_inc(sq_ready, 1)
                nsq[0] += 1
                inverse_root(T)

            def pre_norm(T, ready):
                mean_square(x, T, ready)
                for c in range(NC):
                    for lo, hi, v in STREAMS[:2 if T == TOK else 1]:
                        act.wait_ge(scaled, nn[0] + 1)
                        nn[0] += 1
                        act.activation(h_hi[:, c, lo:hi], tmp[:, c % 2, lo:hi], ACT.Identity,
                                       bias=col_sh[:, c, v:v + 1]).then_inc(hhi_ready, 1)

            def attention(kind, l):
                tiles = attention_plan(kind, l)
                u0 = unit0[kind, l]
                U = 4 * len(tiles)
                if kind == "swa":
                    act.wait_ge(mix_done, MIXERS * l + 2)
                else:
                    act.wait_ge(mix_done, MIXERS * l + 1)
                for s in range(U + 2):
                    if s >= 2:
                        v = s - 2
                        n = (384 if kind == "swa" else 256) * tiles[v // 4][0] + 256
                        act.wait_ge(at_t, u0 + v + 1)
                        if u0 + v >= 2:
                            act.wait_ge(at_pv, u0 + v - 1)
                        act.activation(pt_sb[:, v % 2, 0:n], ps[2][:, 0:n], ACT.Copy).then_inc(at_tc, 1)
                    if s < U:
                        n = (384 if kind == "swa" else 256) * tiles[s // 4][0] + 256
                        last = KEYS + (kind == "swa")
                        act.wait_ge(at_n, u0 + s + 1)
                        if u0 + s >= 3:
                            act.wait_ge(at_t, u0 + s - 2)
                        if u0 + s >= 4:
                            act.wait_ge(at_q, u0 + s - 3)
                        act.activation(p_sb[:, s % 3, KEYS - n:last], s_sb[:, s % 4, KEYS - n:last], ACT.Exp,
                                       bias=nb[:, s % 4:s % 4 + 1], scale=SCALE,
                                       accum_out=sums[:, s % 4:s % 4 + 1]).then_inc(at_p, 1)

            for u in range(2):
                act.sem_inc(bank_free[u], 1)
            act.wait_ge(s_cin, 32)
            act.activation(c_b[:].rearrange("p v d -> p (v d)"), c_b[:].rearrange("p v d -> p (v d)"),
                           ACT.Silu).then_inc(s_cb, 1)
            for u in range(2):
                act.wait_ge(raw_ld[u], 16)
                act.activation(w_hi[:, u].rearrange("p c n -> p (c n)"), raw[:, u], ACT.Copy).then_inc(w_hi_done, 1)

            for l in range(DEPTH):
                tp, T = TP[l], width[l]
                if l == 0:
                    act.wait_ge(s_in, 16 * 6)
                    act.wait_ge(consts_done, 1)
                    pre_norm(TOK, lambda c: act.wait_ge(x_ld[2 * c // NC], 16))
                    act.wait_ge(consts_done, 2)
                    act.activation(lbt[:], lbt[:], ACT.Exp).then_inc(consts_done, 1)
                    copy_phase(tp["proj"], N_PROJ // 2, u_t, 0, TOK)
                else:
                    pre_norm(TOK, lambda c: act.wait_ge(x_upd, 2 * l * NC - NC + c + 1))
                    copy_phase(tp["proj"], N_PROJ_CTX // 2, u_t, 0, TOK)
                    copy_phase(tp["proj"] + N_PROJ_CTX // 2, (N_PROJ - N_PROJ_CTX) // 2, u_t, N_PROJ_CTX, LAT)
                for j in range(T // P):
                    act.wait_ge(fn_a, sum(width[:l]) // P + j + 1)
                    act.activation(fn_ab[:, j], ps[j % 2][:, 0:512], ACT.Copy).then_inc(fn_abe, 1)
                for blk in (QD, QD + 1, GD, GD + 1):
                    act.activation(u_t[:, blk, 0:T], u_t[:, blk, 0:T], ACT.Silu)
                attention("na", l)
                attention("swa", l)
                act.wait_ge(mix_done, MIXERS * l + 3)
                for p in range(2):
                    for d in range(2):
                        fz = u_t[:, (FF, FB)[d] + p, :]
                        link(act.activation(hk[p][:, d], fz, ACT.Sigmoid, scale=-1.0))
                        ins = act.activation(fz, fz, ACT.Sigmoid)
                    ins.then_inc(hg_gate, 1)
                for p in range(2):
                    n = 2 * l + p
                    if p:
                        act.wait_ge(hg_end, n)
                    for d in range(2):
                        act.wait_ge(hg_kt, 2 * n + d + 1)
                        act.activation(hkt[:, d], ps[d][:, 0:TOK], ACT.Copy).then_inc(hg_ktc, 1)
                    act.wait_ge(hg_o, n + 1)
                    act.activation(hkt[:, 0, 0:T], ps[3][:, 0:T], ACT.Square).then_inc(hg_sq, 1)
                    act.wait_ge(hg_ms, n + 1)
                    link(act.activation(hms[:, 0:T], ps[2][:, 0:T], ACT.Ln, bias=eps_c[:, 0:1], scale=1.0 / HD))
                    act.activation(hkt[:, 1, 0:T], hms[:, 0:T], ACT.Exp, scale=-0.5).then_inc(hg_rs, 1)
                act.wait_ge(mix_done, MIXERS * l + 4)
                for c in range(NC):
                    act.activation(h_hi[:, c, 0:T], f_t[:, c, 0:T], ACT.Copy).then_inc(hhi_ready, 1)
                copy_phase(tp["wout"], N_OUT // 2, f_t, 0, T)
                act.wait_ge(bank_free[0], tp["wout"] + N_OUT // 2 + 1)
                act.wait_ge(bank_free[1], tp["wout"] + N_OUT // 2 + 1)
                late_mean_square(T)
                pre_norm(T, lambda c: act.wait_ge(x_upd, 2 * l * NC + c + 1))
                for p, kc in enumerate(FFN_CHUNKS):
                    ffn_in(tp["in", p], kc, T)
                    if p == 0:
                        copy_phase(tp["out", p], N_OUT // 2, f_t, 0, T)
                    else:
                        last = l == DEPTH - 1 and p == len(FFN_CHUNKS) - 1
                        splits_only(tp["out", p], N_OUT // 2, last)
                act.wait_ge(bank_free[0], tp["end"] + 1)
                act.wait_ge(bank_free[1], tp["end"] + 1)
                late_mean_square(T)

        @block.tensor
        def _(pe):
            def passes(u, k, rhs_hi, rhs_lo, kc, T):
                for w, r, first, last in ((w_hi, rhs_hi, k == 0, False), (w_hi, rhs_lo, False, False),
                                          (w_lo, rhs_hi, False, k == kc - 1)):
                    for lo, hi, _ in STREAMS[:2 if T == TOK else 1]:
                        mm = pe.matmul(ps[u][:, lo:hi], w[:, u, k], r[:, k, lo:hi], start=first, stop=last)
                return mm

            def product_phase(g0, n, rhs_hi, rhs_lo, kc, T, ready=None):
                if ready:
                    for u in range(2):
                        pe.wait_ge(w_lo_done, 2 * g0 + u + 1)
                        pe.wait_ge(bank_free[u], g0 + 1)
                    for k in range(kc):
                        ready(k)
                        for u in range(2):
                            mm = passes(u, k, rhs_hi, rhs_lo, kc, T)
                            if k == kc - 1:
                                mm.then_inc(blk_done, 1)
                with pe.Fori(1 if ready else 0, n) as i:
                    for u in range(2):
                        pe.wait_ge(w_lo_done, 2 * i + (2 * g0 + u + 1))
                        pe.wait_ge(bank_free[u], i + (g0 + 1))
                        for k in range(kc):
                            mm = passes(u, k, rhs_hi, rhs_lo, kc, T)
                        mm.then_inc(blk_done, 1)

            nsq = [0]

            def mean_square(T):
                for c in range(NC):
                    pe.wait_ge(sq_ready, nsq[0] + 1)
                    for lo, hi, _ in STREAMS[:2 if T == TOK else 1]:
                        mm = pe.matmul(ps[2][:, lo:hi], ones, sq[:, c % 2, lo:hi], start=c == 0, stop=c == NC - 1)
                    mm.then_inc(sq_used, 1)
                    nsq[0] += 1

            late = [0]

            def late_mean_square(T):
                late[0] += 1
                for j, (ready, count, src) in enumerate(((sq_sum, late[0], sq[:, 1]), (sq_ready, nsq[0] + 1, lnms))):
                    pe.wait_ge(ready, count)
                    for lo, hi, _ in STREAMS[:2 if T == TOK else 1]:
                        mm = pe.matmul(ps[2][:, lo:hi], ones, src[:, lo:hi], start=j == 0, stop=j == 1)
                mm.then_inc(sq_used, 1)
                nsq[0] += 1

            def fourier(l):
                T = width[l]
                pe.wait_ge(fn_ld, 64 * (l + 1))
                done = sum(width[:l]) // P
                for j in range(T // P):
                    if j >= 2:
                        pe.wait_ge(fn_abe, done + j - 1)
                    for b in range(2):
                        mm = pe.matmul(ps[j % 2][:, 256 * b:256 * b + 256], u_t[:, UB + b, P * j:P * j + P],
                                       fn_d[:], start=True, stop=True)
                    mm.then_inc(fn_a, 1)
                pe.wait_ge(fn_abe, done + T // P)
                for b in range(2):
                    for lo, hi, m, tab in ((0, LAT, 4, fn_l), (LAT, TOK, 2, fn_c))[:2 if T == TOK else 1]:
                        for j in range(m):
                            for part in range(2):
                                mm = pe.matmul(ps[b][:, lo:hi],
                                               fn_ab[:, lo // P + j, 256 * b + P * part:256 * b + P * part + P],
                                               tab[:, j, part], start=j + part == 0, stop=j == m - 1 and part == 1)
                    mm.then_inc(fn_t, 1)
                pe.wait_ge(fn_te, 2 * (l + 1))
                for n in range(2):
                    for lo, hi, _ in STREAMS[:2 if T == TOK else 1]:
                        for b in range(2):
                            mm = pe.matmul(ps[2 + n][:, lo:hi], fn_w[:, b, P * n:P * n + P], fn_f[:, b, lo:hi],
                                           start=b == 0, stop=b == 1)
                    mm.then_inc(fn_o, 1)

            def attention(kind, l):
                tiles = attention_plan(kind, l)
                u0, t0 = unit0[kind, l], tile0[kind, l]
                U = 4 * len(tiles)
                L = 384 if kind == "swa" else 256

                def queries(t, h):
                    lat, i = tiles[t]
                    if kind == "na":
                        return na_q[:, i % 2, h // 2, h % 2] if lat else na_qc[:, h // 2, h % 2, P * i:P * i + P]
                    o = P * i if lat else LAT + P * i
                    return qz[:, h % 2, h // 2, o:o + P]

                def scores(s):
                    t, h = s // 4, s % 4
                    lat, i = tiles[t]
                    bank = ps[s % 2]
                    if u0 + s >= 2:
                        pe.wait_ge(at_n, u0 + s - 1)
                    kb = KA + h // 2 if kind == "na" else KS
                    if lat:
                        if kind == "na":
                            keys = u_t[:, kb, 0:LAT].rearrange("p (r c) -> p r c", c=GRID_W)
                            keys = keys[:, :, BAND0[i]:BAND0[i] + BAND]
                            dst = bank[:, 256:512].rearrange("p (r c) -> p r c", c=BAND)
                        else:
                            first = P * min(max(i - 1, 0), 1)
                            keys = u_t[:, kb, first:first + L]
                            dst = bank[:, 512 - L:512]
                        pe.matmul(dst, queries(t, h), keys, start=True, stop=True)
                    pe.matmul(bank[:, 512:768], queries(t, h), u_t[:, kb, LAT:TOK],
                              start=True, stop=True).then_inc(at_s, 1)

                def transposes(v):
                    n = L * tiles[v // 4][0] + 256
                    pe.wait_ge(at_q, u0 + v + 1)
                    if u0 + v >= 1:
                        pe.wait_ge(at_tc, u0 + v)
                    for j in range(n // P):
                        o = KEYS - n + P * j
                        mm = pe.transpose(ps[2][:, P * j:P * j + P], p_sb[:, v % 3, o:o + P], ident)
                    mm.then_inc(at_t, 1)

                def pv(v):
                    t, h = v // 4, v % 4
                    lat, i = tiles[t]
                    n = L * lat + 256
                    pe.wait_ge(at_tc, u0 + v + 1)
                    if h == 0 and t0 + t >= 2:
                        pe.wait_ge(at_o, t0 + t - 1)
                    if kind == "na" and h == 0:
                        pe.wait_ge(nv_c, 5 * l + (i + 2 if lat else 1))
                    a = 64 * (h % 2)
                    dst = ps_out[(t0 + t) % 2][a:a + 64, P * (h // 2):P * (h // 2) + P]
                    for j in range(n // P):
                        local = j < L // P and lat
                        if kind == "na":
                            val = (na_v[:, i % 2, j] if local else na_vc[:, j - L // P * lat])[:, HD * h:HD * h + HD]
                        else:
                            row = min(max(i - 1, 0), 1) + j if local else 4 + j - L // P * lat
                            val = sw_v[:, row, HD * (h // 2):HD * (h // 2) + HD]
                        mm = pe.matmul(dst, val, pt_sb[:, v % 2, P * j:P * j + P], start=j == 0,
                                       stop=j == n // P - 1, skip_group_check=True)
                    mm.then_inc(at_pv, 1)

                def band_v(i):
                    pe.wait_ge(na_st, 5 * l + i + 2)
                    pe.wait_ge(nv_c, 5 * l + i + 1)
                    for j in range(2):
                        for p in range(2):
                            mm = pe.transpose(ps_v[:, 256 * j + P * p:256 * j + P * p + P],
                                              na_vs[:, i % 2, p, P * j:P * j + P], ident)
                    mm.then_inc(nv_t, 1)

                pe.wait_ge(mix_done, MIXERS * l + (1 if kind == "na" else 2))
                if kind == "na":
                    for j in range(2):
                        for p in range(2):
                            mm = pe.transpose(ps_v[:, 256 * j + P * p:256 * j + P * p + P],
                                              u_t[:, VA + p, LAT + P * j:LAT + P * j + P], ident)
                    mm.then_inc(nv_t, 1)
                else:
                    for j in range(6):
                        mm = pe.transpose(ps[2][:, P * j:P * j + P], u_t[:, VS, P * j:P * j + P], ident)
                    mm.then_inc(at_pre, 1)
                    pe.wait_ge(rope_ld, 32 * (l + 1))
                    for n, blk in enumerate((KS, QS, QS + 1)):
                        if n >= 2:
                            pe.wait_ge(rope_d, 3 * l + n - 1)
                        pe.matmul(ps[n % 2][:, 0:LAT], sw_r[:], u_t[:, blk, 0:LAT], start=True, stop=True)\
                          .then_inc(rope_p, 1)
                    pe.wait_ge(rope_d, 3 * l + 3)
                    pe.wait_ge(sw_st, l + 1)
                    pe.wait_ge(at_pre_c, l + 1)
                for s in range(U + 3):
                    if kind == "na" and s % 4 == 0 and s // 4 < 4:
                        band_v(s // 4)
                    if s < U:
                        scores(s)
                    if 2 <= s < U + 2:
                        transposes(s - 2)
                    if s >= 3:
                        pv(s - 3)

            def level_products(slot, qz, hk, d, m, T):
                for c in range(T // P):
                    q = qz[:, d, :, P * c:P * c + P].rearrange("p h (n two m) -> p h n two m", two=2, m=m)
                    mm = pe.matmul(slot[:, P * c:P * c + P].rearrange("p (h n m) -> p h n m", h=2, m=m),
                                   hk[:, d, P * c:P * c + P], q[:, :, :, 1 - d], start=True, stop=True)
                return mm

            def hgrn(l):
                T = width[l]

                def values(p):
                    for c in range(6):
                        mm = pe.transpose(ps[2][:, P * c:P * c + P], u_t[:, IV + p, P * c:P * c + P], ident)
                    mm.then_inc(hg_v, 1)

                pe.wait_ge(mix_done, MIXERS * l + 3)
                values(0)
                for p in range(2):
                    n = 2 * l + p
                    m0 = 30 * n
                    pe.wait_ge(hg_init, n + 1)
                    if p:
                        pe.wait_ge(hg_ktc, 2 * n)
                    for h in range(2):
                        for c in range(T // P):
                            mm = pe.matmul(ps[h][:, P * c:P * c + P], ho[64 * h:64 * h + 64, P * c:P * c + P],
                                           u_t[64 * h:64 * h + 64, QD + p, P * c:P * c + P], start=True, stop=True)
                        mm.then_inc(hg_a, 1)
                    if p:
                        pe.wait_ge(hg_rs, n)
                        values(1)
                    for j in range(2 * LEVELS):
                        i, d = j // 2, j % 2
                        pe.wait_ge(hg_q, 16 * n + j + 1)
                        if i:
                            pe.wait_ge(hg_u, 14 * n + j - 1)
                        if j == 2:
                            pe.wait_ge(hg_vc, n + 1)
                        else:
                            pe.wait_ge(hg_m, m0 + (j + 1 if j < 2 else 2 * j - 2))
                        level_products(ps[j % 3], hqz[p], hk[p], d, 1 << i, T).then_inc(hg_a, 1)
                    for d in range(2):
                        pe.wait_ge(hg_u, 14 * n + 12 + d + 1)
                        pe.wait_ge(hg_m, m0 + 30)
                        for c in range(6):
                            mm = pe.transpose(ps[d][:, P * c:P * c + P], hk[p][:, d, P * c:P * c + P], ident)
                        mm.then_inc(hg_kt, 1)
                    pe.wait_ge(hg_vc, n + 1)
                    for d in range(2):
                        pe.wait_ge(hg_ktc, 2 * n + d + 1)
                        if d:
                            pe.wait_ge(hg_st, 2 * n + 1)
                        for j, c in enumerate(ORDER[d][:5]):
                            mm = pe.matmul(ps[2][:, P * j:P * j + P], hkt[:, d, P * c:P * c + P], hv[:, c],
                                           start=True, stop=True)
                        mm.then_inc(hg_ds, 1)
                    pe.wait_ge(hg_st, 2 * n + 2)
                    pe.wait_ge(hg_q, 16 * n + 16)
                    if p:
                        pe.wait_ge(hg_end, n)
                    for c in range(T // P):
                        o = ps[3][:, P * c:P * c + P]
                        terms = [d for d in range(2) if ORDER[d].index(c) > 0]
                        for h in range(2):
                            pe.matmul(o[64 * h:64 * h + 64], hv[:, c, 64 * h:64 * h + 64],
                                      hatt[:, h, P * c:P * c + P], start=True, stop=False, skip_group_check=True)
                        for d in terms:
                            for h in range(2):
                                mm = pe.matmul(o[64 * h:64 * h + 64],
                                               hst[:, d, ORDER[d].index(c), 64 * h:64 * h + 64],
                                               hqz[p][:, d, h, P * c:P * c + P], start=False, stop=d == terms[-1],
                                               skip_group_check=True)
                    mm.then_inc(hg_o, 1)
                    pe.wait_ge(hg_sq, n + 1)
                    for lo, hi, _ in STREAMS[:2 if T == TOK else 1]:
                        mm = pe.matmul(ps[2][:, lo:hi], blockones, hkt[:, 0, lo:hi], start=True, stop=True)
                    mm.then_inc(hg_ms, 1)

            hh = [0]

            def chunks_split(parts):
                base = hh[0]
                hh[0] += NC * parts
                return lambda k: pe.wait_ge(hlo_ready, base + (k + 1) * parts)

            for l in range(DEPTH):
                tp, T = TP[l], width[l]
                if l == 0:
                    pe.wait_ge(s_in, 16 * 6)
                mean_square(TOK)
                ready = chunks_split(2)
                if full[l]:
                    product_phase(tp["proj"], N_PROJ // 2, h_hi, h_lo, NC, TOK, ready)
                else:
                    product_phase(tp["proj"], N_PROJ_CTX // 2, h_hi, h_lo, NC, TOK, ready)
                    product_phase(tp["proj"] + N_PROJ_CTX // 2, (N_PROJ - N_PROJ_CTX) // 2, h_hi, h_lo, NC, LAT)
                for u in range(2):
                    pe.wait_ge(bank_free[u], tp["wout"] + 1)
                fourier(l)
                attention("na", l)
                attention("swa", l)
                hgrn(l)
                product_phase(tp["wout"], N_OUT // 2, h_hi, h_lo, NC, T, chunks_split(1))
                late_mean_square(T)
                mean_square(T)
                ready = chunks_split(2 if full[l] else 1)
                for p, kc in enumerate(FFN_CHUNKS):
                    done = l * 22 + sum(FFN_CHUNKS[:p])
                    product_phase(tp["in", p], kc, h_hi, h_lo, NC, T, None if p else ready)
                    product_phase(tp["out", p], N_OUT // 2, hid_hi, hid_lo, kc, T,
                                  lambda k: pe.wait_ge(hid_lo_done, done + k + 2))
                late_mean_square(T)

        @block.vector
        def _(dve):
            chain = [0]

            def link(ins):
                chain[0] += 1
                ins.then_inc(dve_chain, 1)
                dve.wait_ge(dve_chain, chain[0])

            def split_lo(g, u):
                dve.wait_ge(w_hi_done, 2 * g + (u + 3))
                dve.tensor_tensor(w_lo[:, u].rearrange("p c n -> p (c n)"), raw[:, u],
                                  w_hi[:, u].rearrange("p c n -> p (c n)").bitcast(F32), ALU.subtract)\
                   .then_inc(w_lo_done, 1)

            def ada_pair(q, l, ql):
                dve.wait_ge(ada_copied, q + 1)
                for u in range(2):
                    dve.wait_ge(ada_ld[u], 16 * q + 16)
                    for v in range(2):
                        dve.wait_ge(ada_done, 4 * q + (2 * u + v + 1))
                        dve.tensor_tensor_reduce(ps[3][:], ada_w[:, u], c_b[:, v], 1.0, 0.0, ALU.mult, ALU.add,
                                                 ada_t[:, u, v:v + 1]).then_inc(ada_done, 1)
                dve.wait_ge(ada_done, 4 * q + 5)
                dst = ada_c[l][:].rearrange("p n v -> p (n v)")[:, bass.ds(4 * ql, 4)]
                dve.tensor_copy(dst, ada_t[:].rearrange("p u v -> p (u v)")).then_inc(ada_copied, 1)

            def lo_phase(g0, n, ada=None, add=False, T=TOK, last=False):
                def body(i, split):
                    for u in range(2):
                        if add:
                            dve.wait_ge(blk_done, 2 * i + (2 * g0 + u + 1))
                            dst = f_t[:, 2 * i + u, 0:T]
                            dve.tensor_tensor(dst, dst, ps[u][:, 0:T], ALU.add).then_inc(bank_free[u], 1)
                        if split:
                            split_lo(i + g0, u)
                    if ada:
                        ada_pair(i + ada[0], ada[1], i + ada[2])
                with dve.Fori(0, n - last) as i:
                    body(i, True)
                if last:
                    body(n - 1, False)

            def ffn_in(g0, q0, n, T, ada=None):
                with dve.Fori(0, n) as i:
                    split_lo(i + g0, 0)
                    dve.wait_ge(blk_done, 2 * i + (2 * g0 + 2))
                    dve.wait_ge(bank_free[0], i + (g0 + 2))
                    dve.wait_ge(hid_lo_done, i + (q0 + 1))
                    dve.wait_ge(hid_hi_done, i + (q0 + 1))
                    dve.tensor_tensor(tmp[:, 1, 0:T], tmp[:, 0, 0:T], ps[1][:, 0:T], ALU.mult)\
                       .then_inc(bank_free[1], 1)
                    split_lo(i + g0, 1)
                    dve.wait_ge(hid_hi_done, i + (q0 + 2))
                    dve.tensor_tensor(hid_lo[:, i, 0:T], tmp[:, 1, 0:T], hid_hi[:, i, 0:T].bitcast(F32),
                                      ALU.subtract).then_inc(hid_lo_done, 1)
                    if ada:
                        ada_pair(i + ada[0], ada[1], i + ada[2])

            def cols(l, chunk0, dst):
                b = bada[:, l, chunk0:chunk0 + NC].unsqueeze(2).to_broadcast([P, NC, 2])
                link(dve.tensor_tensor(dst[:], ada_c[l][:, chunk0:chunk0 + NC], b, ALU.add))

            def gain(l, which):
                return gcol[:, l, which].unsqueeze(2).to_broadcast([P, NC, 2])

            nrs, nhi, nlo, nm, nx = [0], [0], [0], [0], [0]

            def pre_norm(l, sh, sc, g, T):
                cols(l, sh, col_sh)
                cols(l, sc, col_sc)
                link(dve.scalar_tensor_tensor(col_gs[:], col_sc[:], 1.0, gain(l, g), ALU.add, ALU.mult))
                nrs[0] += 1
                dve.wait_ge(rstd_ready, nrs[0])
                st = STREAMS[:2 if T == TOK else 1]
                for c in range(NC + 1):
                    if c >= 2:
                        dve.wait_ge(hlo_ready, nlo[0])
                    if c < NC:
                        for lo, hi, v in st:
                            dve.scalar_tensor_tensor(tmp[:, c % 2, lo:hi], x[:, c, lo:hi], col_gs[:, c, v:v + 1],
                                                     rstd[:, lo:hi], ALU.mult, ALU.mult).then_inc(scaled, 1)
                    if c:
                        for lo, hi, v in st:
                            nhi[0] += 1
                            nlo[0] += 1
                            dve.wait_ge(hhi_ready, nhi[0])
                            dve.scalar_tensor_tensor(h_lo[:, c - 1, lo:hi], tmp[:, (c - 1) % 2, lo:hi],
                                                     col_sh[:, c - 1, v:v + 1], h_hi[:, c - 1, lo:hi].bitcast(F32),
                                                     ALU.add, ALU.subtract).then_inc(hlo_ready, 1)
                dve.wait_ge(hlo_ready, nlo[0])

            def post_norm(l, gt, g, T):
                cols(l, gt, col_gg)
                link(dve.tensor_tensor(col_gg[:], col_gg[:], gain(l, g), ALU.mult))
                nrs[0] += 1
                dve.wait_ge(rstd_ready, nrs[0])
                st = STREAMS[:2 if T == TOK else 1]
                for c in range(NC + 1):
                    if c < NC:
                        for lo, hi, v in st:
                            dve.scalar_tensor_tensor(f_t[:, c, lo:hi], f_t[:, c, lo:hi], col_gg[:, c, v:v + 1],
                                                     rstd[:, lo:hi], ALU.mult, ALU.mult).then_inc(pn_m, 1)
                    if c:
                        dve.wait_ge(pn_m, nm[0] + c * len(st))
                        dve.tensor_tensor(x[:, c - 1, 0:T], x[:, c - 1, 0:T], f_t[:, c - 1, 0:T], ALU.add)\
                           .then_inc(x_upd, 1)
                nm[0] += NC * len(st)
                nx[0] += NC
                dve.wait_ge(x_upd, nx[0])

            def attention(kind, l):
                tiles = attention_plan(kind, l)
                u0, t0 = unit0[kind, l], tile0[kind, l]
                U = 4 * len(tiles)
                L = 384 if kind == "swa" else 256
                f0 = 0 if kind == "na" else 4

                def band_bias(cb):
                    if cb >= 2:
                        dve.wait_ge(at_n, u0 + 4 * (cb - 1))
                    dve.wait_ge(na_ld[cb % 2], 16 * ROWS * (2 * l + cb // 2 + 1))
                    for h in range(4):
                        v = na_b[:, 4 * (cb % 2) + h].rearrange("p (r c) -> p r c", c=BAND)
                        m = na_m[:, cb].unsqueeze(1).to_broadcast([P, ROWS, BAND])
                        r = na_r[:, cb % 2].rearrange("p (r h c) -> p r h c", r=ROWS, h=4)[:, :, h]
                        ins = dve.scalar_tensor_tensor(v, r, 1.0 / SCALE, m, ALU.mult, ALU.add)
                    ins.then_inc(na_bias, 1)
                    dve.wait_ge(na_bias, 4 * l + cb + 1)

                def score_max(s):
                    t, h = s // 4, s % 4
                    lat, i = tiles[t]
                    n = L * lat + 256
                    dve.wait_ge(at_s, u0 + s + 1)
                    if u0 + s >= 4:
                        dve.wait_ge(at_p, u0 + s - 3)
                    if u0 + s >= 2:
                        dve.wait_ge(at_n, u0 + s - 1)
                    dst, src = s_sb[:, s % 4, KEYS - n:KEYS], ps[s % 2][:, 768 - n:768]
                    if kind == "swa":
                        bias = sw_m[:, (0, 1, 1, 2)[i], :] if lat else sw_m[:, 0, 384:640]
                    elif lat:
                        first = 4 * (i % 2) + h
                        bias = na_b[:, first:9:8 - first, :]
                        dst, src = (a.rearrange("p (k c) -> p k c", k=2) for a in (dst, src))
                    else:
                        bias = na_b[:, 8, :]
                    link(dve.tensor_tensor_reduce(dst, src, bias, 1.0, -3e38, ALU.add, ALU.max,
                                                  mx[:, s % 2:s % 2 + 1]))
                    if kind == "na":
                        dve.tensor_scalar(nb[:, h:h + 1], mx[:, s % 2:s % 2 + 1], -SCALE, None, ALU.mult)\
                           .then_inc(at_n, 1)
                    else:
                        dve.tensor_scalar(nb[:, h:h + 1], mx[:, s % 2:s % 2 + 1], sink8[:, l, h:h + 1],
                                          -SCALE, ALU.max, ALU.mult).then_inc(at_n, 1)

                def normalise(v):
                    n = L * tiles[v // 4][0] + 256
                    dve.wait_ge(at_p, u0 + v + 1)
                    if u0 + v:
                        dve.wait_ge(at_q, u0 + v)
                    link(dve.reciprocal(rinv[:], sums[:, v % 4:v % 4 + 1]))
                    p = p_sb[:, v % 3, KEYS - n:KEYS]
                    dve.tensor_scalar(p, p, rinv[:], None, ALU.mult).then_inc(at_q, 1)

                def out_copy(t):
                    lat, i = tiles[t]
                    dve.wait_ge(at_pv, u0 + 4 * t + 4)
                    src, dst = ps_out[(t0 + t) % 2][:, 0:2 * P], f_t[:, f0:f0 + 2, :]
                    if kind == "na" and lat:
                        dst = dst[:, :, 0:LAT].rearrange("p b (r c) -> p b r c", c=GRID_W)
                        dst = backwards(dst[:, :, :, 16 * i:16 * i + 16])
                        src = src.rearrange("p (b r c) -> p b r c", r=ROWS, c=16)
                    else:
                        o = P * i if lat else LAT + P * i
                        dst = dst[:, :, o:o + P]
                        src = src.rearrange("p (b t) -> p b t", b=2)
                    dve.tensor_copy(dst, src).then_inc(at_o, 1)

                if kind == "na":
                    dve.wait_ge(mix_done, MIXERS * l + 1)
                    dve.memset(na_b[:, 8], 0.0)
                    dve.wait_ge(nv_t, 5 * l + 1)
                    dve.tensor_copy(na_vc[:].rearrange("p j d -> p (j d)"), ps_v).then_inc(nv_c, 1)
                    dve.wait_ge(na_mask, 16 * (l + 1))
                else:
                    dve.wait_ge(at_pre, l + 1)
                    dve.tensor_copy(sw_v[:].rearrange("p j d -> p (j d)"), ps[2][:, 0:TOK]).then_inc(at_pre_c, 1)
                    dve.wait_ge(rope_ld, 32 * (l + 1))
                    link(dve.tensor_copy(s_sb[:, :, KEYS:KEYS + 1], sink8[:, l].unsqueeze(2)))
                    for n, blk in enumerate((KS, QS, QS + 1)):
                        dve.wait_ge(rope_p, 3 * l + n + 1)
                        if 3 * l + n:
                            dve.wait_ge(rope_d, 3 * l + n)
                        dve.tensor_tensor(sw_t[:, 0], ps[n % 2][:, 0:LAT], sw_cs[:, 1], ALU.mult)
                        link(dve.tensor_tensor(sw_t[:, 1], u_t[:, blk, 0:LAT], sw_cs[:, 0], ALU.mult))
                        if n == 0:
                            ins = dve.tensor_tensor(u_t[:, blk, 0:LAT], sw_t[:, 0], sw_t[:, 1], ALU.add)
                        else:
                            for h in range(2):
                                a = slice(64 * h, 64 * h + 64)
                                ins = dve.tensor_tensor(qz[a, n - 1, h, 0:LAT], sw_t[a, 0], sw_t[a, 1], ALU.add)
                        ins.then_inc(rope_d, 1)
                    dve.wait_ge(at_ld, 16 * (l + 1))
                for s in range(U + 3):
                    if kind == "na" and s % 4 == 0 and s // 4 < 4:
                        dve.wait_ge(nv_t, 5 * l + s // 4 + 2)
                        dve.tensor_copy(na_v[:, s // 4 % 2].rearrange("p j d -> p (j d)"), ps_v).then_inc(nv_c, 1)
                        band_bias(s // 4)
                    if s < U:
                        score_max(s)
                    if 1 <= s <= U:
                        normalise(s - 1)
                    if s >= 3 and (s - 3) % 4 == 3:
                        out_copy((s - 3) // 4)
                dve.wait_ge(at_o, t0 + len(tiles))
                dve.sem_inc(mix_done, 1)

            def halves(ap, m, right):
                if ap.shape[-1] == P:
                    return ap.rearrange("p (n two m) -> p n two m", two=2, m=m)[:, :, right]
                return ap.rearrange("p (c n two m) -> p c n two m", n=P // (2 * m), two=2, m=m)[:, :, :, right]

            def key_sum(l, p):
                T = width[l]
                dve.tensor_tensor(ho[:, 0:T], hk[p][:, 0, 0:T], hk[p][:, 1, 0:T], ALU.add).then_inc(hg_init, 1)

            def hgrn(l):
                T = width[l]
                nch = T // P
                dve.wait_ge(mix_done, MIXERS * l + 3)
                dve.wait_ge(hg_ld, 16 * (l + 1))
                dve.tensor_copy(hmask[:], hmask_f[:]).then_inc(hg_mc, 1)
                for p in range(2):
                    dve.wait_ge(hg_gate, 2 * l + p + 1)
                    for d in range(2 if l else 0):
                        f = u_t[:, (FF, FB)[d] + p, :]
                        dve.tensor_scalar(hk[p][:, d], hk[p][:, d], lb1[:, d, p:p + 1], None, ALU.mult)
                        link(dve.tensor_scalar(f, f, lb1[:, d, p:p + 1], lb[:, d, p:p + 1], ALU.mult, ALU.add))
                        dve.sem_inc(hg_f, 1)
                    if p == 0:
                        key_sum(l, 0)
                dve.wait_ge(hg_mc, l + 1)
                for p in range(2):
                    n = 2 * l + p
                    a0, m0 = 16 * n, 30 * n
                    for h in range(2):
                        dve.wait_ge(hg_a, a0 + h + 1)
                        dve.tensor_tensor(hatt[:, h, 0:T].rearrange("p (c t) -> p c t", t=P),
                                          ps[h][:, 0:T].rearrange("p (c t) -> p c t", t=P),
                                          ident.unsqueeze(1).to_broadcast([P, nch, P]), ALU.mult).then_inc(hg_m, 1)
                    dve.wait_ge(hg_v, n + 1)
                    dve.tensor_copy(hv[:].rearrange("p c d -> p (c d)"), ps[2][:, 0:TOK]).then_inc(hg_vc, 1)
                    tot = [u_t[:, FF + p, :], u_t[:, FB + p, :]]
                    off = 0
                    for i in range(LEVELS):
                        m = 1 << i
                        nbk = TOK // (2 * m)
                        for d in range(2):
                            j = 2 * i + d
                            ks = d
                            dve.wait_ge(hg_a, a0 + 2 + j + 1)
                            a = tot[d].rearrange("p (n two) -> p n two", two=2)
                            kv = hk[p][:, d].rearrange("p (n two m) -> p n two m", two=2, m=m)
                            dve.tensor_tensor(kv[:, :, ks], kv[:, :, ks],
                                              a[:, :, 1 - ks].unsqueeze(2).to_broadcast([P, nbk, m]), ALU.mult)
                            nxt = ha[:, d, off:off + nbk]
                            dve.tensor_tensor(nxt, a[:, :, 0], a[:, :, 1], ALU.mult).then_inc(hg_u, 1)
                            for h in range(2):
                                dve.wait_ge(hg_m, m0 + 2 * j + h + 1)
                                dve.copy_predicated(halves(hatt[:, h, 0:T], m, 1 - d),
                                                    halves(hmask[:, LEVELS * d + i], m, 1 - d).unsqueeze(1)
                                                    .to_broadcast([P, nch, P // (2 * m), m]),
                                                    ps[j % 3][:, 0:T].rearrange("p (c h n m) -> p c h n m", h=2,
                                                                                n=P // (2 * m), m=m)[:, :, h])\
                                   .then_inc(hg_m, 1)
                            dve.wait_ge(hg_u, 14 * n + j + 1)
                            tot[d] = nxt
                        off += nbk
                    for d in range(2):
                        dve.wait_ge(hg_ds, 2 * n + d + 1)
                        for j, c in enumerate(ORDER[d][:5]):
                            ds = ps[2][:, P * j:P * j + P]
                            if j == 0:
                                link(dve.tensor_copy(hst[:, d, 1], ds))
                            else:
                                link(dve.scalar_tensor_tensor(hst[:, d, j + 1], hst[:, d, j], tot[d][:, c:c + 1], ds,
                                                              ALU.mult, ALU.add))
                        dve.sem_inc(hg_st, 1)
                    if p == 0:
                        key_sum(l, 1)
                    dve.wait_ge(hg_rs, n + 1)
                    link(dve.scalar_tensor_tensor(hatt[:, 0, 0:T], ps[3][:, 0:T], hgain[:, l, p:p + 1], hkt[:, 1, 0:T],
                                                  ALU.mult, ALU.mult))
                    link(dve.tensor_tensor(f_t[:, 6 + p, 0:T], hatt[:, 0, 0:T], u_t[:, GD + p, 0:T], ALU.mult))
                    dve.sem_inc(hg_end, 1)
                dve.sem_inc(mix_done, 1)

            def gate_bounds():
                dve.tensor_scalar(sink8[:], sinks[:], 1.0 / SCALE, None, ALU.mult)
                link(dve.tensor_tensor(lb[:], lbc[:, :, 0], lbc[:, :, 1], ALU.max))
                for j in range(2):
                    ins = dve.tensor_tensor(lbt[:, j], lbc[:, :, j], lb[:], ALU.subtract)
                ins.then_inc(consts_done, 1)
                dve.wait_ge(consts_done, 3)
                link(dve.tensor_tensor(lb1[:], lbt[:, 0], lbt[:, 1], ALU.add))
                link(dve.reciprocal(lb1[:], lb1[:]))
                link(dve.tensor_tensor(lb[:], lbt[:, 1], lb1[:], ALU.mult))
                link(dve.tensor_tensor(lb1[:], lbt[:, 0], lb1[:], ALU.mult))

            dve.memset(eps_c[:], EPS).then_inc(consts_done, 1)
            for count in (hid_hi_done, hid_lo_done, ada_done, ada_copied):
                dve.sem_inc(count, 1)
            dve.wait_ge(s_cb, 1)
            for k in range(2 * ADA_FIRST):
                if k % 2 == 0:
                    dve.wait_ge(ada_0_ld[k // 2], 16)
                for v in range(2):
                    if 2 * k + v:
                        dve.wait_ge(ada_0_done, 2 * k + v)
                    dve.tensor_tensor_reduce(ps[3][:], first_units(k // 2)[:, k % 2], c_b[:, v], 1.0, 0.0, ALU.mult,
                                             ALU.add, ada_c[0][:, k, v:v + 1]).then_inc(ada_0_done, 1)
            for u in range(2):
                dve.wait_ge(w_hi_done, u + 1)
                dve.tensor_tensor(w_lo[:, u].rearrange("p c n -> p (c n)"), raw[:, u],
                                  w_hi[:, u].rearrange("p c n -> p (c n)").bitcast(F32), ALU.subtract)\
                   .then_inc(w_lo_done, 1)
            dve.wait_ge(s_in, 16 * 6)
            for k in range(2):
                dve.wait_ge(x_ld[k], 16)
            dve.wait_ge(ada_0_done, 4 * ADA_FIRST)

            for l in range(DEPTH):
                tp, T = TP[l], width[l]
                if l:
                    dve.wait_ge(ada_copied, 41)
                pre_norm(l, SH1, SC1, G_PRE_MIX, TOK)
                if l == 0:
                    ada_pair(0, 0, 8)
                    gate_bounds()
                lo_phase(tp["proj"], N_PROJ // 2, ada=(1, 0, 9) if l == 0 else None)
                for u in range(2):
                    dve.wait_ge(bank_free[u], tp["wout"] + 1)
                for b in range(2):
                    dve.wait_ge(fn_t, 2 * l + b + 1)
                    dve.tensor_copy(fn_f[:, b, 0:T], ps[b][:, 0:T]).then_inc(fn_te, 1)
                for n in range(2):
                    dve.wait_ge(fn_o, 2 * l + n + 1)
                    ins = dve.tensor_copy(f_t[:, 2 + n, 0:T], ps[2 + n][:, 0:T])
                ins.then_inc(mix_done, 1)
                attention("na", l)
                attention("swa", l)
                hgrn(l)
                for c in range(NC):
                    nhi[0] += 1
                    nlo[0] += 1
                    dve.wait_ge(hhi_ready, nhi[0])
                    dve.tensor_tensor(h_lo[:, c, 0:T], f_t[:, c, 0:T], h_hi[:, c, 0:T].bitcast(F32),
                                      ALU.subtract).then_inc(hlo_ready, 1)
                lo_phase(tp["wout"], N_OUT // 2, ada=(12, 0, 20) if l == 0 else None)
                if l == 0:
                    dve.wait_ge(ada_copied, 17)
                post_norm(l, GT1, G_POST_MIX, T)
                pre_norm(l, SH2, SC2, G_PRE_FFN, T)
                for p, kc in enumerate(FFN_CHUNKS):
                    a = (16 + 12 * p, 1, 12 * p) if l == 0 and p < 2 else None
                    ffn_in(tp["in", p], l * 22 + sum(FFN_CHUNKS[:p]), kc, T, a)
                    a = (24 + 12 * p, 1, 12 * p + 8) if l == 0 and p < 2 else None
                    lo_phase(tp["out", p], N_OUT // 2, ada=a, add=p > 0, T=T,
                             last=l == DEPTH - 1 and p == len(FFN_CHUNKS) - 1)
                post_norm(l, GT2, G_POST_FFN, T)


ORDER = ((4, 5, 0, 1, 2, 3), (5, 4, 3, 2, 1, 0))


def _tile(w):
    t = np.zeros((P, NC, P), w.dtype)
    t[:, :w.shape[0] // P] = w.reshape(-1, P, P).transpose(1, 0, 2)
    return t.reshape(P, NC * P)


def _weight_stream(w_in, w_out, w_ffn_in, w_ffn_out):
    tiles = []
    swa = np.r_[0:64, 128:192, 64:128, 192:256] + 8 * P
    cols = [range(P * b, P * b + P) for b in (2, 3, 4, 5, 10, 11, 14, 15, 16, 17, 18, 19, 0, 1, 6, 7)]
    cols += [swa[:P], swa[P:]] + [range(P * b, P * b + P) for b in (12, 13, 20, 21)]
    for l in range(DEPTH):
        tiles += [_tile(w_in[l][:, np.asarray(c)]) for c in cols]
        tiles += [_tile(w_out[l][:, P * o:P * o + P]) for o in range(NC)]
        j = 0
        for kc in FFN_CHUNKS:
            for c in range(j, j + kc):
                tiles += [_tile(w_ffn_in[l][:, h * DFF + P * c:h * DFF + P * c + P]) for h in range(2)]
            tiles += [_tile(w_ffn_out[l][P * j:P * (j + kc), P * o:P * o + P]) for o in range(NC)]
            j += kc
    return np.stack(tiles)


def _tables():
    f = np.float32
    tok, ch = np.arange(LAT), np.arange(HD)

    def dft(n):
        a = 2 * np.pi * (np.outer(np.arange(n), np.arange(n)) % n) / n
        t = np.stack([np.cos(a), -np.sin(a)], 1) / np.sqrt(n * HD)
        return t.reshape(n // P, P, 2, n).transpose(1, 0, 2, 3).astype(f)

    a = 2 * np.pi * (np.outer(ch, ch) % HD) / HD
    dftd = np.concatenate([np.kron(np.eye(2), np.cos(a)), np.kron(np.eye(2), np.sin(a))], 1).astype(f)
    d = np.arange(P)
    rot = np.zeros((P, P), f)
    first = d % 32 < 16
    rot[d[first] + 16, d[first]] = -1
    rot[d[~first] - 16, d[~first]] = 1
    freq = 10000.0 ** (-(d % 16) / 16)
    pos = np.where((d % HD < 32)[:, None], tok // GRID_W, tok % GRID_W)
    rope = np.stack([np.cos(pos * freq[:, None]), np.sin(pos * freq[:, None])], 1).astype(f)
    swa = np.zeros((P, 3, 640), f)
    for kind in range(3):
        rel = np.arange(384) - P * kind - d[:, None]
        swa[:, kind, :384] = np.where(np.abs(rel) <= 128, 0, NEG)
    na = np.zeros((P, 4, BAND), f)
    for cb in range(4):
        q = 16 * cb + 15 - d % 16
        first_col = np.clip(q - 8, 0, GRID_W - 16)[:, None]
        key = BAND0[cb] + np.arange(BAND)
        na[:, cb] = np.where((key >= first_col) & (key < first_col + 16), 0, NEG)
    lv = np.zeros((P, 2 * LEVELS, P), f)
    for i in range(LEVELS):
        m = 1 << i
        same = d[:, None] // (2 * m) == d // (2 * m)
        right = d // m % 2 == 1
        lv[:, i] = same & ~right[:, None] & right
        lv[:, LEVELS + i] = same & right[:, None] & ~right
    squares = np.stack([np.ones((P, P)), np.eye(P), np.kron(np.eye(2), np.ones((HD, HD)))]).astype(f)
    return {"dftL": dft(LAT), "dftC": dft(CTX), "dftD": dftd, "rotm": rot, "rope": rope, "swamask": swa,
            "namask": na, "lvmask": lv, "sqc": squares}


def kernel(x, c, ctx, c_ctx, w_ada, b_ada, g_pre_mix, g_post_mix, g_pre_ffn, g_post_ffn, w_in, w_out, na_rpb, w_fnet,
           swa_sink, hgrn_lb_logits, hgrn_norm_g, w_ffn_in, w_ffn_out):
    import concourse.bacc as bacc
    from concourse.bass_utils import run_bass_kernel_spmd

    a = {
        "xT": np.concatenate([np.asarray(x)[0].T, np.asarray(ctx)[0].T], 1),
        "cvec": np.stack([np.asarray(c)[0], np.asarray(c_ctx)]),
        "wstream": _weight_stream(*map(np.asarray, (w_in, w_out, w_ffn_in, w_ffn_out))),
        "adaT": np.asarray(w_ada).transpose(0, 2, 1).reshape(DEPTH * N_ADA, P, D),
        "badaT": np.asarray(b_ada).reshape(DEPTH, N_ADA, P).transpose(2, 0, 1),
        "gT": np.stack([np.asarray(g) for g in (g_pre_mix, g_post_mix, g_pre_ffn, g_post_ffn)], 1)
        .reshape(DEPTH, 4, NC, P).transpose(3, 0, 1, 2),
        "rpb": np.pad(np.asarray(na_rpb).transpose(0, 2, 1, 3), ((0, 0), (0, 0), (0, 0), (RPB_PAD, RPB_W - RPB_PAD - 31))),
        "wf": np.asarray(w_fnet).reshape(DEPTH, 2, P, 2 * P).transpose(0, 2, 1, 3),
        "sink": np.asarray(swa_sink),
        "lbT": np.asarray(hgrn_lb_logits).reshape(2, DEPTH, 2, P).transpose(3, 0, 1, 2),
        "hgT": np.asarray(hgrn_norm_g).reshape(DEPTH, 2, P).transpose(2, 0, 1),
        **_tables(),
    }
    arrays = {f"in_{k}": np.ascontiguousarray(v) for k, v in a.items()}
    nc = bacc.Bacc("TRN2", target_bir_lowering=False, num_devices=1)
    args = {k: nc.dram_tensor(f"in_{k}", arrays[f"in_{k}"].shape, mybir.dt.from_np(arrays[f"in_{k}"].dtype),
                              kind="ExternalInput").ap() for k in a}
    out = nc.dram_tensor("out_xT", (D, LAT), F32, kind="ExternalOutput").ap()
    hybrid_kernel(nc, **args, out=out)
    r = run_bass_kernel_spmd(nc, [arrays], core_ids=[0])
    return np.ascontiguousarray(r.results[0]["out_xT"].T)[None]
```
